# Optimizing a Trainium2 kernel written in Bass

```python
import math
import jax, jax.numpy as jnp
from jax import lax
import numpy as np

D_MODEL = 1024
BATCH = 1
SEQ = 512
DEPTH = 2

M_HEADS = 4
M_DH = D_MODEL // M_HEADS
M_W = M_HEADS * M_DH
M_CHUNK = 128
CONV_W = 4
POOL_WINDOWS = (2, 4, 8, 16)
POOL_GROUPS = 4
POOL_W = D_MODEL
POOL_G = POOL_W // POOL_GROUPS
A_HEADS = 8
A_DK = 64
A_DV = 2 * A_DK
A_QK_W = A_HEADS * 2 * A_DK
A_V_W = A_HEADS * A_DV
Q_BLOCK = 128
ROPE_THETA = 10000.0
N_BRANCH = 3
FF = -(-8 * D_MODEL // (3 * 256)) * 256
NORM_EPS = 1e-6
NEG_BIG = -1e30

SPLIT_SIZES = (M_W, M_W, M_W, M_W, M_HEADS, M_HEADS, POOL_W, A_QK_W, A_QK_W, A_V_W, N_BRANCH * D_MODEL)
N_IN = sum(SPLIT_SIZES)

kernel_name = "hybrid_mlstm_pool_diffattn_block"

def rmsnorm(x, g):
    xf = x.astype(jnp.float32)
    y = xf * lax.rsqrt(jnp.mean(xf * xf, axis=-1, keepdims=True) + NORM_EPS)
    return (y * g.astype(jnp.float32)).astype(x.dtype)

def rope(x):
    S, d = x.shape[-2], x.shape[-1]
    half = d // 2
    inv = ROPE_THETA ** (-jnp.arange(half, dtype=jnp.float32) / half)
    ang = jnp.arange(S, dtype=jnp.float32)[:, None] * inv[None, :]
    cos, sin = jnp.cos(ang), jnp.sin(ang)
    xf = x.astype(jnp.float32)
    x1, x2 = xf[..., :half], xf[..., half:]
    return jnp.concatenate([x1 * cos - x2 * sin, x2 * cos + x1 * sin], axis=-1).astype(x.dtype)

def causal_conv(u, w):
    C = u.shape[-1]
    return lax.conv_general_dilated(u, w[:, None, :].astype(u.dtype), window_strides=(1,),
                                    padding=((CONV_W - 1, 0),),
                                    dimension_numbers=('NWC', 'WIO', 'NWC'),
                                    feature_group_count=C)

def mlstm_chunkwise(q, k, v, i_pre, f_pre):
    B, H, S, Dh = q.shape
    L = M_CHUNK
    NC = S // L
    q = q.reshape(B, H, NC, L, Dh) * (Dh ** -0.5)
    k = k.reshape(B, H, NC, L, Dh)
    v = v.reshape(B, H, NC, L, Dh)
    li = i_pre.reshape(B, H, NC, L)
    lf = jax.nn.log_sigmoid(f_pre).reshape(B, H, NC, L)
    b = jnp.cumsum(lf, axis=-1)
    g = b[..., -1]
    w_state = g[..., None] - b + li
    m_loc = jnp.max(w_state, axis=-1)
    e_state = jnp.exp(w_state - m_loc[..., None])
    C_loc = jnp.einsum('bhcsk,bhcsv->bhckv', k * e_state[..., None], v)
    n_loc = jnp.einsum('bhcs,bhcsk->bhck', e_state, k)

    def step(carry, inp):
        C, n, m = carry
        g_c, m_c, C_c, n_c = inp
        m_new = jnp.maximum(g_c + m, m_c)
        a = jnp.exp(g_c + m - m_new)
        bb = jnp.exp(m_c - m_new)
        C_new = a[..., None, None] * C + bb[..., None, None] * C_c
        n_new = a[..., None] * n + bb[..., None] * n_c
        return (C_new, n_new, m_new), (C, n, m)

    init = (jnp.zeros((B, H, Dh, Dh), jnp.float32), jnp.zeros((B, H, Dh), jnp.float32),
            jnp.full((B, H), NEG_BIG, jnp.float32))
    xs = (jnp.moveaxis(g, 2, 0), jnp.moveaxis(m_loc, 2, 0), jnp.moveaxis(C_loc, 2, 0), jnp.moveaxis(n_loc, 2, 0))
    _, (C_prev, n_prev, m_prev) = lax.scan(step, init, xs)
    C_prev = jnp.moveaxis(C_prev, 0, 2)
    n_prev = jnp.moveaxis(n_prev, 0, 2)
    m_prev = jnp.moveaxis(m_prev, 0, 2)

    causal = jnp.tril(jnp.ones((L, L), dtype=bool))
    Dm = jnp.where(causal, b[..., :, None] - b[..., None, :] + li[..., None, :], -jnp.inf)
    m_inter = b + m_prev[..., None]
    m_t = jnp.maximum(m_inter, jnp.max(Dm, axis=-1))
    P = jnp.exp(Dm - m_t[..., None])
    Sqk = jnp.einsum('bhcjd,bhcsd->bhcjs', q, k) * P
    inter = jnp.exp(m_inter - m_t)
    num = jnp.einsum('bhcjs,bhcsv->bhcjv', Sqk, v) + inter[..., None] * jnp.einsum('bhcjk,bhckv->bhcjv', q, C_prev)
    den = jnp.sum(Sqk, axis=-1) + inter * jnp.einsum('bhcjk,bhck->bhcj', q, n_prev)
    h = num / jnp.maximum(jnp.abs(den), jnp.exp(-m_t))[..., None]
    return h.reshape(B, H, S, Dh)

def pool_mixer(u, w_pool, scale):
    B, S, _ = u.shape
    uf = u.astype(jnp.float32)
    cs = jnp.concatenate([jnp.zeros((B, 1, POOL_W), jnp.float32), jnp.cumsum(uf, axis=1)], axis=1)
    pos1 = jnp.arange(1, S + 1)
    means = []
    for gi, w in enumerate(POOL_WINDOWS):
        c = cs[..., gi * POOL_G:(gi + 1) * POOL_G]
        lo = jnp.concatenate([jnp.zeros((B, w - 1, POOL_G), jnp.float32), c[:, :S - w + 1]], axis=1)
        cnt = jnp.minimum(pos1, w).astype(jnp.float32)
        means.append((c[:, 1:] - lo) / cnt[None, :, None])
    pooled = jnp.concatenate(means, axis=-1) - uf
    y = jnp.einsum('bsgi,gio->bsgo', pooled.reshape(B, S, POOL_GROUPS, POOL_G),
                   w_pool.astype(jnp.float32)).reshape(B, S, POOL_W)
    return (y * scale.astype(jnp.float32)).astype(u.dtype)

def diff_attention(q, k, v, lam):
    B, H, _, S, dk = q.shape
    nb = S // Q_BLOCK
    qb = jnp.moveaxis(q.reshape(B, H, 2, nb, Q_BLOCK, dk), 3, 0)
    kpos = jnp.arange(S)
    scale = dk ** -0.5

    def block(args):
        q_blk, blk = args
        s = jnp.einsum('bhcqd,bhckd->bhcqk', q_blk, k).astype(jnp.float32) * scale
        qpos = blk * Q_BLOCK + jnp.arange(Q_BLOCK)
        s = jnp.where(kpos[None, :] <= qpos[:, None], s, -jnp.inf)
        p = jax.nn.softmax(s, axis=-1)
        a = p[:, :, 0] - lam * p[:, :, 1]
        return jnp.einsum('bhqk,bhkd->bhqd', a, v.astype(jnp.float32))

    out = lax.map(block, (qb, jnp.arange(nb)))
    return jnp.moveaxis(out, 0, 2).reshape(B, H, S, v.shape[-1]).astype(v.dtype)

def hybrid_mixer(x, layer_idx, g_mix, w_in, b_if, conv_qk, w_m_out, w_pool, pool_scale,
                 g_qk, lam_p, g_diff_head, w_diff_out, w_out):
    B, S, _ = x.shape
    h = rmsnorm(x, g_mix)
    proj = h @ w_in
    mq, mk, mv, mo, mi, mf, pu, aq, ak, av, gate_pre = jnp.split(
        proj, np.cumsum(SPLIT_SIZES)[:-1].tolist(), axis=-1)

    qk = jax.nn.silu(causal_conv(jnp.concatenate([mq, mk], axis=-1), conv_qk))
    mq, mk = jnp.split(qk, 2, axis=-1)

    def heads(t):
        return t.reshape(B, S, M_HEADS, M_DH).transpose(0, 2, 1, 3).astype(jnp.float32)

    i_pre = (mi + b_if[:M_HEADS]).astype(jnp.float32).transpose(0, 2, 1)
    f_pre = (mf + b_if[M_HEADS:]).astype(jnp.float32).transpose(0, 2, 1)
    hm = mlstm_chunkwise(heads(mq), heads(mk), heads(mv), i_pre, f_pre)
    hm = hm.transpose(0, 2, 1, 3).reshape(B, S, M_W).astype(x.dtype)
    y_m = (jax.nn.sigmoid(mo) * hm) @ w_m_out

    y_p = pool_mixer(pu, w_pool, pool_scale)

    q = aq.reshape(B, S, A_HEADS, 2, A_DK).transpose(0, 2, 3, 1, 4)
    k = ak.reshape(B, S, A_HEADS, 2, A_DK).transpose(0, 2, 3, 1, 4)
    q = rope(rmsnorm(q, g_qk[0]))
    k = rope(rmsnorm(k, g_qk[1]))
    v = av.reshape(B, S, A_HEADS, A_DV).transpose(0, 2, 1, 3)
    lam_init = 0.8 - 0.6 * math.exp(-0.3 * layer_idx)
    lp = lam_p.astype(jnp.float32)
    lam = jnp.exp(jnp.sum(lp[0] * lp[1])) - jnp.exp(jnp.sum(lp[2] * lp[3])) + lam_init
    o = diff_attention(q, k, v, lam)
    o = rmsnorm(o, g_diff_head) * (1.0 - lam_init)
    y_a = o.transpose(0, 2, 1, 3).reshape(B, S, A_V_W) @ w_diff_out

    g_m, g_p, g_a = jnp.split(jax.nn.sigmoid(gate_pre), N_BRANCH, axis=-1)
    merged = g_m * y_m + g_p * y_p + g_a * y_a
    return merged @ w_out

def swiglu_ffn(x, g_ffn, w_gate_up, w_down):
    h = rmsnorm(x, g_ffn)
    gate, up = jnp.split(h @ w_gate_up, 2, axis=-1)
    return (jax.nn.silu(gate) * up) @ w_down

def setup_inputs(seed: int = 0) -> dict:
    key = jax.random.key(seed)
    ks = jax.random.split(key, 18)
    f32 = jnp.float32

    def nrm(k, shape, scale):
        return jax.random.normal(k, shape, f32) * scale

    x = nrm(ks[0], (BATCH, SEQ, D_MODEL), 1.0)
    g_mix = 1.0 + nrm(ks[1], (DEPTH, D_MODEL), 0.02)
    w_in = nrm(ks[2], (DEPTH, D_MODEL, N_IN), D_MODEL ** -0.5)
    b_i = nrm(ks[3], (DEPTH, M_HEADS), 0.1)
    b_f = jnp.linspace(3.0, 6.0, M_HEADS, dtype=f32)[None, :] + nrm(ks[4], (DEPTH, M_HEADS), 0.1)
    b_if = jnp.concatenate([b_i, b_f], axis=-1)
    conv_qk = nrm(ks[5], (DEPTH, CONV_W, 2 * M_W), CONV_W ** -0.5)
    w_m_out = nrm(ks[6], (DEPTH, M_W, D_MODEL), M_W ** -0.5)
    w_pool = nrm(ks[7], (DEPTH, POOL_GROUPS, POOL_G, POOL_G), POOL_G ** -0.5)
    pool_scale = 1.0 + nrm(ks[8], (DEPTH, POOL_W), 0.02)
    g_qk = 1.0 + nrm(ks[9], (DEPTH, 2, A_DK), 0.02)
    lam_p = nrm(ks[10], (DEPTH, 4, A_DK), 0.1)
    g_diff_head = 1.0 + nrm(ks[11], (DEPTH, A_DV), 0.02)
    w_diff_out = nrm(ks[12], (DEPTH, A_V_W, D_MODEL), A_V_W ** -0.5)
    w_out = nrm(ks[13], (DEPTH, D_MODEL, D_MODEL), D_MODEL ** -0.5)
    g_ffn = 1.0 + nrm(ks[14], (DEPTH, D_MODEL), 0.02)
    w_gate_up = nrm(ks[15], (DEPTH, D_MODEL, 2 * FF), D_MODEL ** -0.5)
    w_down = nrm(ks[16], (DEPTH, FF, D_MODEL), FF ** -0.5)
    return {"x": x, "g_mix": g_mix, "w_in": w_in, "b_if": b_if, "conv_qk": conv_qk,
            "w_m_out": w_m_out, "w_pool": w_pool, "pool_scale": pool_scale, "g_qk": g_qk,
            "lam_p": lam_p, "g_diff_head": g_diff_head, "w_diff_out": w_diff_out, "w_out": w_out,
            "g_ffn": g_ffn, "w_gate_up": w_gate_up, "w_down": w_down}

def reference(x, g_mix, w_in, b_if, conv_qk, w_m_out, w_pool, pool_scale, g_qk, lam_p,
              g_diff_head, w_diff_out, w_out, g_ffn, w_gate_up, w_down):
    for l in range(DEPTH):
        x = x + hybrid_mixer(x, l, g_mix[l], w_in[l], b_if[l], conv_qk[l], w_m_out[l], w_pool[l],
                             pool_scale[l], g_qk[l], lam_p[l], g_diff_head[l], w_diff_out[l], w_out[l])
        x = x + swiglu_ffn(x, g_ffn[l], w_gate_up[l], w_down[l])
    return x


_drawn_inputs = setup_inputs


def setup_inputs(seed=0):
    import zlib

    import numpy as np

    out = dict(_drawn_inputs(seed))
    spreads = {}
    factors = {'pool_scale': 4.774, 'g_qk': 3.693, 'g_diff_head': 5.014, 'g_ffn': 3.064}
    for name, (base, spread) in spreads.items():
        noise = np.random.default_rng([zlib.crc32(name.encode()), seed]).standard_normal(out[name].shape)
        drawn = base * np.exp(spread * noise) if base else spread * noise
        out[name] = __import__('jax').numpy.asarray(drawn.astype(out[name].dtype))
    for name, factor in factors.items():
        out[name] = (out[name] * factor).astype(out[name].dtype)
    return out
```

```python
import concourse.bass as bass
from concourse import mybir
from concourse.alu_op_type import AluOpType as ALU

F32 = mybir.dt.float32
F32R = mybir.dt.float32r
ACT = mybir.ActivationFunctionType
AX = mybir.AxisListType

P = 128
D = 1024
S = 512
DEPTH = 2
KT = D // P
NB = S // P
FF = 2816
FT = FF // P
UC = 256
MH, MDH = 4, 256
AH, DK = 8, 64
EPS = 1e-6
NEG_BIG = -1e30

C_MQ, C_MK, C_MV, C_IF, C_PU = 0, D, 2 * D, 4 * D, 4 * D + 2 * MH
C_AQ = C_PU + D
C_GM = C_AQ + 3 * D
C_GP, C_GA = C_GM + D, C_GM + 2 * D

SECTIONS = [("aq", 4, 4), ("ak", 4, 4), ("av", 4, 4), ("vo", 8, 8), ("pu", 4, 4), ("mq", 4, 4), ("mk", 4, 4),
            ("pool", 4, 4), ("ga", 4, 4), ("wd", 4, 4), ("gp", 4, 4), ("gm", 4, 4), ("wm", 4, 4), ("wo", 4, 4),
            ("gu", 2 * FF // UC, 2 * FF // UC), ("dn", 12, 4)]
UBASE, VBASE = {}, {}
UPL = VPL = 0
for _n, _u, _v in SECTIONS:
    UBASE[_n], VBASE[_n] = UPL, VPL
    UPL, VPL = UPL + _u, VPL + _v
DOWN_K = ((0, 8), (8, 8), (16, 6))

R_GMIX, R_GFFN, R_PSC, R_CONV, R_GDH = 0, KT, 2 * KT, 3 * KT, 3 * KT + 64
NROWS = R_GDH + 1

K_ID, K_MASK, K_BIG, K_ONE, K_HOT, K_CNT, K_LAM, K_COS = 0, 128, 256, 384, 512, 516, 532, 536
K_ALL = K_COS + NB * 2 * (DK // 2)


def pair_off(jc):
    return jc * (jc + 1) // 2


def row_off(sc):
    return sum(NB - c for c in range(sc)) * P


def build_trunk(nc, x, g_mix, w_in, b_if, conv_qk, w_m_out, w_pool, pool_scale, g_qk, lam_p, g_diff_head,
                w_diff_out, w_out, g_ffn, w_gate_up, w_down, consts, out):
    base = (nc.sbuf_base + 31) // 32 * 32
    KB = 1024

    def at(name, offset, shape, dt=F32):
        return nc.alloc_sbuf_tensor_at(name, shape, dt, offset=base + offset)

    h_hi = at("h_hi", 0, [P, KT, S], F32R)
    h_lo = at("h_lo", 16 * KB, [P, KT, S], F32R)
    raw = [at(f"raw{s}", (32 + 8 * s) * KB, [P, KT, UC]) for s in range(2)]
    w_hi = [at(f"w_hi{s}", (48 + 8 * s) * KB, [P, KT, UC], F32R) for s in range(2)]
    w_lo = [at(f"w_lo{s}", (64 + 8 * s) * KB, [P, KT, UC], F32R) for s in range(2)]
    Z1, Z2, Z3, Z4, ZT = 80 * KB, 112 * KB, 144 * KB, 160 * KB, 176 * KB
    qkn = at("qkn", Z1, [P, AH, 2, NB, P])
    o_sp = at("o_sp", Z1, [P, AH, 2, S], F32R)
    merged_hi = at("merged_hi", Z1, [P, KT, S], F32R)
    merged_lo = at("merged_lo", Z1 + 16 * KB, [P, KT, S], F32R)
    xnat = at("xnat", Z1, [P, NB, D])
    vo = at("vo", Z2, [P, NB, 2 * D])
    mqk = at("mqk", Z2, [P, MH, 4, S])
    hm_sp = at("hm_sp", Z2, [P, MH, 4, S], F32R)
    sq = at("sq", Z2, [P, KT, S])
    av = at("av", Z3, [P, NB, D])
    gate = at("gate", Z3, [P, KT, S])
    mg = at("mg", Z4, [P, KT, S])
    act_hi = at("act_hi", Z1, [P, FT, S], F32R)
    act_lo = at("act_lo", Z1 + 44 * KB, [P, FT, S], F32R)
    xt = at("xt", ZT, [P, KT, S])
    glu = at("glu", ZT + 16 * KB, [P, 2, S])
    ntmp = at("ntmp", ZT + 16 * KB, [P, 2, S])
    diag = at("diag", ZT + 20 * KB, [P, NB, P])
    tg = at("tg", ZT + 16 * KB, [P, 2, S])
    gate_t = at("gate_t", Z4 + 8 * KB, [P, 2, S])
    e0 = at("e0", ZT, [P, 2, S])
    e1 = at("e1", ZT + 4 * KB, [P, 2, S])
    qk_t = at("qk_t", ZT + 8 * KB, [P, 2, S])
    probs = at("probs", ZT + 12 * KB, [P, 10 * P])
    probs_t = at("probs_t", ZT + 17 * KB, [P, 10 * P])
    osq = at("osq", ZT + 17 * KB, [P, NB, P])
    mc = at("mc", Z1, [P, 4, S])
    mvh = at("mvh", Z1 + 8 * KB, [P, NB, MDH])
    moh = at("moh", Z1 + 12 * KB, [P, NB, MDH])
    decay = at("decay", Z1 + 16 * KB, [P, 10 * P])
    hn = at("hn", Z1 + 21 * KB, [P, NB, MDH])
    mth = at("mth", Z1 + 25 * KB, [P, S])
    mdiag = at("mdiag", Z1 + 27 * KB, [P, NB, P])
    selh = at("selh", Z1 + 29 * KB, [P, P])
    pl = [at(f"pl{s}", ZT + (0 + 4 * s) * KB, [P, 2, S], F32R) for s in range(2)]
    ph = [at(f"ph{s}", ZT + (8 + 4 * s) * KB, [P, 2, S], F32R) for s in range(2)]
    pa = at("pa", Z3, [P, 2, S])
    pb = at("pb", Z3 + 4 * KB, [P, 2, S])
    ytmp = at("ytmp", ZT + 16 * KB, [P, 2, S])
    row_i = at("row_i", Z3 + 8 * KB, [P, S])
    row_b = at("row_b", Z3 + 10 * KB, [P, S])
    row_t = at("row_t", Z3 + 12 * KB, [P, S])
    row_u = at("row_u", Z3 + 14 * KB, [P, S])
    row_a = at("row_a", ZT + 16 * KB, [P, 10 * P])
    off = ZT + 22 * KB
    table = {}
    for name, cols in (("kc", K_ALL), ("rope", 2 * 2 * NB * DK), ("pcol", NROWS), ("prow", P),
                       ("ac", 40), ("emt", 4 * MH), ("ifn", NB * 8), ("wif", KT * 8), ("lamt", 8),
                       ("bif", 2), ("st", 48), ("st_s", 48), ("mx2", 24), ("mp", 8)):
        table[name] = at(name, off, [P, cols])
        if name == "rope":
            rope_at = off
        off += (4 * cols + 31) // 32 * 32
    wif_hi = at("wif_hi", off, [P, KT, 8], F32R)
    wif_lo = at("wif_lo", off + 32 * KT, [P, KT, 8], F32R)
    off += 64 * KT
    assert base + off <= nc.sbuf_usable_end, (base + off, nc.sbuf_usable_end)
    kc, pcol, prow, ac, emt, ifn, lamt, bif, st, st_s, mx2, mp = (
        table[n] for n in ("kc", "pcol", "prow", "ac", "emt", "ifn", "lamt", "bif", "st", "st_s", "mx2", "mp"))
    row_m = at("row_m", rope_at, [P, S])
    rope = table["rope"][:].rearrange("p (f a b d) -> p f a b d", f=2, a=2, b=NB)
    wif = table["wif"][:].rearrange("p (k c) -> p k c", k=KT)
    gqk = at("gqk", Z4 + 12 * KB, [P, 2, DK])
    lams = at("lams", Z4 + 13 * KB, [P, 4, DK])
    lamp = at("lamp", Z4 + 14 * KB, [P, 2, DK])
    ident = kc[:, K_ID:K_ID + P]
    causal = kc[:, K_MASK:K_MASK + P]
    big = kc[:, K_BIG:K_BIG + P]
    ones = kc[:, K_ONE:K_ONE + P]

    bank = [nc.alloc_psum_tensor(f"dense{t}", [P, S], F32) for t in range(2)]
    B = [nc.alloc_psum_tensor(f"side{t}", [P, S], F32) for t in range(6)]

    xt_dram = nc.dram_tensor("xt_spill", [P, KT * S], F32, kind="Internal").ap()
    vo_dram = nc.dram_tensor("vo_spill", [S, 2 * D], F32, kind="Internal").ap()

    sem_names = """raw_ready0 raw_ready1 hi_ready split_done units_done tile0_done
        bank_free0 bank_free1 const_loaded x_loaded xt_in_t xt_tile sq_done ms_done ms_sb rstd_done diag_done
        rb_done ntmp_done hhi_done hlo_done prow_loaded prow_t pcol_done small_loaded rope_done lam_sum lam_exp lam_done
        if_loaded if_hi if_split if_done ifn_done spilled xt_back aev q_sq q_ss q_rstd q_roped q_t q_tsb s_done s_max s_exp
        s_comb a_t a_tsb o_done o_sq o_ss o_rstd o_norm o_t o_hi o_lo row_t1 row_log row_ready row_t2 row_cols emt_cols
        vo_spilled m_sel m_mb m_diag m_decay m_conv m_th m_c m_s m_sp m_num m_vo m_tanh m_hn m_ht m_hi m_lo
        p_sum p_pool p_hi p_lo tg_done gate_done merged_val merged_hi_done merged_lo_done glu_t glu_v act_hi_done act_lo_done
        waits_over fin_t fin_sb stored vo_done""".split()
    sem = {n: nc.alloc_semaphore(n) for n in sem_names}
    raw_ready = [sem["raw_ready0"], sem["raw_ready1"]]
    START_AT_1 = ("o_norm", "s_exp", "a_t", "o_lo", "m_decay", "m_num", "m_lo", "act_lo_done")
    bank_free = [sem["bank_free0"], sem["bank_free1"]]

    def unit(l, name, j):
        return l * UPL + (UBASE[name] + j)

    def tile(l, name, j):
        return l * VPL + (VBASE[name] + j)

    def wait_alone(eng, s, value):
        eng.wait_ge(s, value)
        eng.sem_inc(sem["waits_over"], 1)

    def tile_wait(eng, l, name, j, t):
        if t == 1:
            eng.wait_ge(sem["units_done"], unit(l, name, j) + 3)
        else:
            eng.wait_ge(sem["tile0_done"], tile(l, name, j // 3 if name == "dn" else j) + 1)

    def read_out(l, name, j):
        return l * (2 * VBASE["pool"]) + 2 * (VBASE[name] + j)

    with nc.Block() as block:

        @block.sync
        def _(sp):
            sp.dma_start(kc[:, :], consts).then_inc(sem["const_loaded"], 16)
            sp.dma_start(xnat[:, :, :], x[0].rearrange("(b p) d -> p b d", p=P)).then_inc(sem["x_loaded"], 16)

            def load(l, name, j, s, src, kn=KT):
                need = sp.snap(unit(l, name, j) + 1)
                sp.wait_ge(sem["split_done"], need)
                sp.dma_start(raw[s][:, 0:kn, :], src).then_inc(raw_ready[s], 16)

            def columns(w, l, col, rows=D):
                return w[bass.ds(l, 1), :, bass.ds(col, UC)].rearrange("o (k p) n -> p (o k) n", p=P)

            def section(l, name, w, col, n):
                with sp.Fori(0, n // 2) as i:
                    for s in range(2):
                        load(l, name, 2 * i + s, s, columns(w, l, i * (2 * UC) + (col + s * UC)))

            with sp.Fori(0, DEPTH) as l:
                section(l, "aq", w_in, C_AQ, 12)
                section(l, "vo", w_in, C_MV, 8)
                section(l, "pu", w_in, C_PU, 4)
                section(l, "mq", w_in, C_MQ, 8)
                with sp.Fori(0, 2) as i:
                    for s in range(2):
                        g = w_pool[bass.ds(l, 1), bass.ds(2 * i + s, 1)].rearrange("o g (k p) n -> p (o g k) n", p=P)
                        load(l, "pool", 2 * i + s, s, g, 2)
                section(l, "ga", w_in, C_GA, 4)
                section(l, "wd", w_diff_out, 0, 4)
                section(l, "gp", w_in, C_GP, 4)
                section(l, "gm", w_in, C_GM, 4)
                section(l, "wm", w_m_out, 0, 4)
                section(l, "wo", w_out, 0, 4)
                with sp.Fori(0, FF // UC) as i:
                    for s in range(2):
                        load(l, "gu", 2 * i + s, s, columns(w_gate_up, l, i * UC + s * FF))
                with sp.Fori(0, 2) as i:
                    for j in range(6):
                        k0, kn = DOWN_K[j % 3]
                        src = w_down[bass.ds(l, 1), k0 * P:(k0 + kn) * P, bass.ds(i * (2 * UC) + (j // 3) * UC, UC)]
                        load(l, "dn", 6 * i + j, j % 2, src.rearrange("o (k p) n -> p (o k) n", p=P), kn)
            for b in range(NB):
                sp.wait_ge(sem["fin_sb"], 2 * b + 2)
                sp.dma_start(out[0, b * P:(b + 1) * P, :], xnat[:, b, :]).then_inc(sem["stored"], 16)
            sp.wait_ge(sem["stored"], 16 * NB)

        @block.gpsimd
        def _(pool):
            def inv_sqrt(dst, src, n):
                return pool.tensor_tensor(dst, src, mp[:, 0:1].to_broadcast([P, n]), ALU.pow)

            pool.memset(mp[:, 0:1], -0.5)
            pool.drain()

            def attention(l, h):
                hd = l * AH + h + 1
                wait_alone(pool, sem["q_ss"], hd)
                inv_sqrt(st[:, 16:32], st[:, 0:16], 16).then_inc(sem["q_rstd"], 1)

            def attention_out(l, h):
                wait_alone(pool, sem["o_ss"], l * AH + h + 1)
                inv_sqrt(st[:, 36:40], st[:, 32:36], 4).then_inc(sem["o_rstd"], 1)

            def norm(l, which):
                wait_alone(pool, sem["ms_sb"], 2 * l + which + 1)
                inv_sqrt(st[:, 44:48], st[:, 40:44], 4).then_inc(sem["rstd_done"], 1)

            with pool.Fori(0, DEPTH) as l:
                one = bass.ds(l, 1)
                with nc.allow_non_contiguous_dma(reason="eight numbers"):
                    pool.dma_start(bif[0:MH, 0:2], b_if[one].rearrange("o (t h) -> h (o t)", t=2)).then_inc(sem["small_loaded"], 16)
                pool.dma_start(prow[R_GMIX:R_GMIX + KT, :], g_mix[one].rearrange("o (t p) -> (o t) p", p=P)).then_inc(sem["prow_loaded"], 16)
                pool.dma_start(prow[R_GFFN:R_GFFN + KT, :], g_ffn[one].rearrange("o (t p) -> (o t) p", p=P)).then_inc(sem["prow_loaded"], 16)
                pool.dma_start(prow[R_PSC:R_PSC + KT, :], pool_scale[one].rearrange("o (t p) -> (o t) p", p=P)).then_inc(sem["prow_loaded"], 16)
                pool.dma_start(prow[R_CONV:R_CONV + 64, :], conv_qk[one].rearrange("o w (t p) -> (o w t) p", p=P)).then_inc(sem["prow_loaded"], 16)
                pool.dma_start(prow[R_GDH:R_GDH + 1, :], g_diff_head[one]).then_inc(sem["prow_loaded"], 16)
                pool.dma_start(gqk[:, :, :], g_qk[one].rearrange("o a d -> o (a d)").to_broadcast([P, 2 * DK]).rearrange("p (a d) -> p a d", a=2)).then_inc(sem["small_loaded"], 16)
                pool.dma_start(lams[:, :, :], lam_p[one].rearrange("o a d -> o (a d)").to_broadcast([P, 4 * DK]).rearrange("p (a d) -> p a d", a=4)).then_inc(sem["small_loaded"], 16)
                with nc.allow_non_contiguous_dma(reason="eight columns of w_in"):
                    pool.dma_start(wif, w_in[one, :, C_IF:C_IF + 2 * MH].rearrange("o (k p) n -> p (o k) n", p=P)).then_inc(sem["if_loaded"], 16)
                norm(l, 0)
                wait_alone(pool, sem["ntmp_done"], l * 16 + 8)
                pool.dma_start(xt_dram, xt[:, :, :].rearrange("p k s -> p (k s)")).then_inc(sem["spilled"], 16)
                attention(l, 0)
                with pool.Fori(1, 4) as i:
                    attention(l, i)
                    attention_out(l, i - 1)
                wait_alone(pool, sem["aev"], read_out(l, "vo", 8))
                pool.dma_start(vo_dram.rearrange("(b p) c -> p b c", p=P), vo[:, :, :]).then_inc(sem["vo_spilled"], 16)
                with pool.Fori(4, AH) as i:
                    attention(l, i)
                    attention_out(l, i - 1)
                attention_out(l, AH - 1)
                wait_alone(pool, sem["o_done"], l * AH + AH)
                wait_alone(pool, sem["aev"], read_out(l, "mq", 0))
                for g in range(4):
                    src = mg[:, 2 * g:2 * g + 2, :]
                    if g >= 1:
                        wait_alone(pool, sem["p_pool"], l * 4 + g)
                    for n in range(g + 1):
                        dst = (pa, pb)[n % 2]
                        w = 1 << n
                        pool.tensor_copy(dst[:, :, 0:w], src[:, :, 0:w])
                        last = pool.tensor_tensor(dst[:, :, w:S], src[:, :, w:S], src[:, :, 0:S - w], ALU.add)
                        if n < g:
                            pool.drain()
                        src = dst
                    last.then_inc(sem["p_sum"], 1)
                wait_alone(pool, sem["vo_spilled"], 16 * (l + 1))

                def vo_head(h):
                    with nc.allow_non_contiguous_dma(reason="a head's columns"):
                        pool.dma_start(mvh[:, :, :], vo_dram[:, bass.ds(h * MDH, MDH)].rearrange("(b p) c -> p b c", p=P)).then_inc(sem["m_vo"], 16)
                        pool.dma_start(moh[:, :, :], vo_dram[:, bass.ds(h * MDH + D, MDH)].rearrange("(b p) c -> p b c", p=P)).then_inc(sem["m_vo"], 16)

                wait_alone(pool, sem["units_done"], unit(l, "wd", 4) + 2)
                vo_head(0)
                wait_alone(pool, sem["spilled"], 16 * (l + 1))
                pool.dma_start(xt[:, :, :].rearrange("p k s -> p (k s)"), xt_dram).then_inc(sem["xt_back"], 16)
                with pool.Fori(1, MH) as h:
                    wait_alone(pool, sem["m_hn"], l * MH + h)
                    vo_head(h)
                norm(l, 1)

        @block.scalar
        def _(act):
            def copy(dst, src, scale=1.0):
                return nc.scalar.activation(dst, src, ACT.Identity, scale=scale)

            def split_hi(l, name, j, s, kn=KT):
                u = unit(l, name, j)
                act.wait_ge(sem["units_done"], u + 1)
                act.wait_ge(raw_ready[s], (u - s) * 8 + 16)
                copy(w_hi[s][:, 0:kn, :], raw[s][:, 0:kn, :]).then_inc(sem["hi_ready"], 1)

            def dense(l, name, i, evac, hooks=(None,) * 5, kn=KT, last_kn=KT, last=False):
                hooks = dict(enumerate(hooks))
                split_hi(l, name, 2 * i + 1, 1, kn)
                for s in range(2):
                    if s == 1 and not last:
                        split_hi(l, name, 2 * i + 2, 0, last_kn)
                    for t in range(2):
                        if hooks.get(2 * s + t):
                            hooks[2 * s + t]()
                        if evac:
                            tile_wait(act, l, name, 2 * i + s, t)
                            evac(s, t)
                if hooks.get(4):
                    hooks[4]()

            def norm(l, which):
                for k in range(KT):
                    act.wait_ge(sem["xt_tile"], l * 16 + (8 * which + (k + 1 if which else KT)))
                    nc.scalar.activation(sq[:, k, :], xt[:, k, :], ACT.Square).then_inc(sem["sq_done"], 1)
                for k in range(KT):
                    n = l * 16 + (8 * which + k)
                    act.wait_ge(sem["ntmp_done"], n + 1)
                    copy(h_hi[:, k, :], ntmp[:, k % 2, :]).then_inc(sem["hhi_done"], 1)

            def attn_square(l, h):
                act.wait_ge(sem["s_comb"], (l * AH + h) * 4)
                nc.scalar.activation(e0[:, :, :], qkn[:, bass.ds(h, 1)].rearrange("p o a b d -> p (o a) (b d)"),
                                     ACT.Square).then_inc(sem["q_sq"], 1)

            def attn_square_first(l):
                act.wait_ge(sem["aev"], read_out(l, "av", 4))
                act.wait_ge(sem["spilled"], 16 * (l + 1))
                nc.scalar.activation(e0[:, :, :], qkn[:, 0].rearrange("p a b d -> p a (b d)"),
                                     ACT.Square).then_inc(sem["q_sq"], 1)

            def attn_qk(l, h):
                act.wait_ge(sem["q_t"], l * AH + h + 1)
                for c in range(2):
                    copy(qk_t[:, c, :], B[4 + c][:, :]).then_inc(sem["q_tsb"], 1)

            smax, ssum = st_s[:, 0:8], st_s[:, 8:16]

            def attn_exp(l, h, qbs):
                for qb in qbs:
                    n = (qb + 1) * P
                    act.wait_ge(sem["s_max"], (l * AH + h) * 4 + qb + 1)
                    e = (e0, e1)[qb % 2]
                    if qb >= 2:
                        act.wait_ge(sem["s_comb"], (l * AH + h) * 4 + qb - 1)
                    for c in range(2):
                        o = 2 * qb + c
                        ins = nc.scalar.activation(e[:, c, 0:n], B[2 * (qb % 2) + c][:, 0:n], ACT.Exp,
                                                   bias=smax[:, o:o + 1], scale=DK ** -0.5, accum_out=ssum[:, o:o + 1])
                        ins.then_inc(sem["s_exp"], 1)

            def attn_probs(l, h, qbs):
                for qb in qbs:
                    act.wait_ge(sem["a_t"], (l * AH + h) * 4 + qb + 1 + 1)
                    n = (qb + 1) * P
                    o = pair_off(qb) * P
                    copy(probs_t[:, o:o + n], B[4 + qb % 2][:, 0:n]).then_inc(sem["a_tsb"], 1)

            def attn_osq(l, h):
                act.wait_ge(sem["o_done"], l * AH + h + 1)
                nc.scalar.activation(osq[:, :, :], B[4][:, :].rearrange("p (b d) -> p b d", b=NB),
                                     ACT.Square).then_inc(sem["o_sq"], 1)

            def attn_ohi(l, h):
                act.wait_ge(sem["o_t"], l * AH + h + 1)
                nc.scalar.activation(o_sp[:, bass.ds(h, 1), 0, :].rearrange("p o s -> p (o s)"), B[5][:, :], ACT.Identity,
                                     scale=lamt[:, 4:5]).then_inc(sem["o_hi"], 1)

            def evac_qk(l, i, qk):
                def evac(s, t):
                    dst = qkn[:, bass.ds(i * 4 + 2 * s, 2), qk, 2 * t:2 * t + 2, :].rearrange("p h b d -> p b h d")
                    copy(dst, bank[t][:, :].rearrange("p (b h d) -> p b h d", b=2, h=2)).then_inc(bank_free[t], 1)
                    act.drain().then_inc(sem["aev"], 1)
                return evac

            def evac_nat(i, dst):
                def evac(s, t):
                    copy(dst[:, 2 * t:2 * t + 2, bass.ds(i * (2 * UC) + s * UC, UC)],
                         bank[t][:, :].rearrange("p (b c) -> p b c", b=2)).then_inc(bank_free[t], 1)
                    act.drain().then_inc(sem["aev"], 1)
                return evac

            def evac_pu(i):
                def evac(s, t):
                    copy(mg[:, bass.ds(i * 4 + (2 * s + t), 1), :].rearrange("p o s -> p (o s)"), bank[t][:, :]).then_inc(bank_free[t], 1)
                    act.drain().then_inc(sem["aev"], 1)
                return evac

            def evac_mqk(i, j):
                def evac(s, t):
                    copy(mqk[:, bass.ds(i * 2 + s, 1), j + t, :].rearrange("p o s -> p (o s)"), bank[t][:, :]).then_inc(bank_free[t], 1)
                    act.drain().then_inc(sem["aev"], 1)
                return evac

            def attention_step(l, name, i, h, evac, tail=True):
                def before0():
                    if tail:
                        attn_square(l, h)
                        attn_probs(l, h - 1, (0, 1, 2, 3))
                    else:
                        attn_square_first(l)

                def before1():
                    if tail:
                        attn_osq(l, h - 1)

                def before2():
                    attn_qk(l, h)

                def before3():
                    attn_exp(l, h, (0, 1))

                def after():
                    if tail:
                        attn_ohi(l, h - 1)
                    attn_exp(l, h, (2, 3))

                dense(l, name, i, evac, (before0, before1, before2, before3, after))

            with act.Fori(0, DEPTH) as l:
                split_hi(l, "aq", 0, 0)
                norm(l, 0)
                act.wait_ge(sem["lam_sum"], l + 1)
                nc.scalar.activation(lamt[:, 2:4], lamt[:, 0:2], ACT.Exp).then_inc(sem["lam_exp"], 1)
                act.wait_ge(sem["if_loaded"], 16 * (l + 1))
                copy(wif_hi[:, :, :], wif).then_inc(sem["if_hi"], 1)
                for name, qk in (("aq", 0), ("ak", 1)):
                    with act.Fori(0, 2) as i:
                        dense(l, name, i, evac_qk(l, i, qk))
                with act.Fori(0, 2) as i:
                    dense(l, "av", i, evac_nat(i, av))
                attention_step(l, "vo", 0, 0, evac_nat(0, vo), tail=False)
                with act.Fori(1, 4) as i:
                    attention_step(l, "vo", i, i, evac_nat(i, vo))
                with act.Fori(0, 2) as i:
                    attention_step(l, "pu", i, i + 4, evac_pu(i))
                act.wait_ge(sem["vo_spilled"], 16 * (l + 1))
                with act.Fori(0, 2) as i:
                    attention_step(l, "mq", i, i + 6, evac_mqk(i, 0))

                def tail0():
                    attn_probs(l, AH - 1, (0, 1, 2, 3))

                def tail1():
                    attn_osq(l, AH - 1)

                def tail3():
                    attn_ohi(l, AH - 1)

                def rows_log():
                    act.wait_ge(sem["row_t1"], l + 1)
                    nc.scalar.activation(row_i[0:MH, :], B[0][0:MH, :], ACT.Identity, bias=bif[0:MH, 0:1])
                    nc.scalar.activation(row_b[0:MH, :], B[1][0:MH, :], ACT.Identity, bias=bif[0:MH, 1:2])
                    nc.scalar.activation(row_t[0:MH, :], B[1][0:MH, :], ACT.Abs, bias=bif[0:MH, 1:2])
                    act.drain()
                    nc.scalar.activation(row_u[0:MH, :], row_t[0:MH, :], ACT.Exp, scale=-1.0)
                    act.drain()
                    nc.scalar.activation(row_t[0:MH, :], row_u[0:MH, :], ACT.Ln, bias=1.0).then_inc(sem["row_log"], 1)

                def rows_emt():
                    act.wait_ge(sem["row_t2"], l + 1)
                    nc.scalar.activation(emt[:, :], B[0][:, 0:4 * MH], ACT.Exp, scale=-1.0).then_inc(sem["emt_cols"], 1)

                dense(l, "mk", 0, evac_mqk(0, 2), (tail0, tail1, None, tail3, rows_log))
                dense(l, "mk", 1, evac_mqk(1, 2), (None, None, None, rows_emt, None), last_kn=2)

                def pool_hi(g):
                    act.wait_ge(sem["p_pool"], l * 4 + g + 1)
                    if g >= 2:
                        act.wait_ge(sem["units_done"], unit(l, "pool", g - 1) + 2)
                    copy(ph[g % 2][:, :, :], mg[:, 2 * g:2 * g + 2, :]).then_inc(sem["p_hi"], 1)

                def evac_pool(i):
                    def evac(s, t):
                        n = 2 * (2 * i + s) + t
                        nc.scalar.activation(mg[:, n, :], bank[t][:, :], ACT.Identity,
                                             scale=pcol[:, R_PSC + n:R_PSC + n + 1]).then_inc(bank_free[t], 1)
                    return evac

                pool_hi(0)
                dense(l, "pool", 0, evac_pool(0), (lambda: pool_hi(1), None, lambda: pool_hi(2), None, lambda: pool_hi(3)), kn=2, last_kn=2)
                dense(l, "pool", 1, evac_pool(1), kn=2)

                def evac_gate(i):
                    def evac(s, t):
                        nc.scalar.activation(gate[:, bass.ds(i * 4 + (2 * s + t), 1), :].rearrange("p o s -> p (o s)"),
                                             bank[t][:, :], ACT.Tanh, scale=0.5).then_inc(bank_free[t], 1)
                        act.drain().then_inc(sem["gate_done"], 1)
                    return evac

                with act.Fori(0, 2) as i:
                    dense(l, "ga", i, evac_gate(i))
                with act.Fori(0, 2) as i:
                    dense(l, "wd", i, None)

                def m_front_decay(h):
                    hd = l * MH + h + 1
                    act.wait_ge(sem["m_diag"], hd)
                    act.wait_ge(sem["m_num"], l * MH + h + 1)
                    for jc in range(NB):
                        for sc in range(jc + 1):
                            src = mdiag[:, jc, :] if sc == jc else B[3][:, jc * P:(jc + 1) * P]
                            o = row_off(sc) + (jc - sc) * P
                            ins = nc.scalar.activation(decay[:, o:o + P], src, ACT.Exp, scale=-1.0,
                                                       bias=ac[:, bass.ds(h + 4 * (pair_off(jc) + sc), 1)])
                    ins.then_inc(sem["m_decay"], 1)

                def m_front_tanh(h):
                    for k in range(4):
                        act.wait_ge(sem["m_conv"], (l * MH + h) * 4 + k + 1)
                        if k:
                            act.wait_ge(sem["m_c"], (l * MH + h) * 4 + k)
                        nc.scalar.activation(mth[:, :], mc[:, k, :], ACT.Tanh, scale=0.5).then_inc(sem["m_th"], 1)

                def m_tail_tanh(h):
                    act.wait_ge(sem["m_vo"], (l * MH + h + 1) * 32)
                    nc.scalar.activation(moh[:, :, :], moh[:, :, :], ACT.Tanh, scale=0.5).then_inc(sem["m_tanh"], 1)

                def m_tail_hi(h):
                    act.wait_ge(sem["m_ht"], l * MH + h + 1)
                    for v in range(2):
                        copy(hm_sp[:, bass.ds(h, 1), v, :].rearrange("p o s -> p (o s)"), B[4 + v][:, :], 0.5).then_inc(sem["m_hi"], 1)

                def evac_tg(i, name):
                    def evac(s, t):
                        n = 4 * i + 2 * s + t
                        if n >= 2:
                            act.wait_ge(sem["merged_val"], l * (2 * KT) + (n - 1))
                        nc.scalar.activation(tg[:, t, :], bank[t][:, :], ACT.Tanh, scale=0.5).then_inc(bank_free[t], 1)
                        act.drain().then_inc(sem["tg_done"], 1)
                    return evac

                def mlstm_step(name, i, h, evac, tail=True):
                    def before0():
                        if tail:
                            m_tail_tanh(h - 1)

                    def before1():
                        m_front_decay(h)

                    def after():
                        if tail:
                            m_tail_hi(h - 1)

                    dense(l, name, i, evac, (before0, before1, lambda: m_front_tanh(h), None, after))

                mlstm_step("gp", 0, 0, evac_tg(0, "gp"), tail=False)
                mlstm_step("gp", 1, 1, evac_tg(1, "gp"))
                act.wait_ge(sem["merged_val"], l * (2 * KT) + KT)
                with act.Fori(0, 2) as i:
                    mlstm_step("gm", i, i + 2, evac_gate(i))

                def before0():
                    m_tail_tanh(MH - 1)

                def before1():
                    m_tail_hi(MH - 1)
                before0()
                before1()

                def merge_hi(n):
                    act.wait_ge(sem["merged_val"], l * (2 * KT) + KT + n + 1)
                    copy(merged_hi[:, bass.ds(n, 1), :].rearrange("p o s -> p (o s)"), mg[:, bass.ds(n, 1), :].rearrange("p o s -> p (o s)"), 0.5).then_inc(sem["merged_hi_done"], 1)

                with act.Fori(0, 2) as i:
                    dense(l, "wm", i, None, (None, lambda: merge_hi(i * 4), lambda: merge_hi(i * 4 + 1), lambda: merge_hi(i * 4 + 2), lambda: merge_hi(i * 4 + 3)))
                with act.Fori(0, 2) as i:
                    dense(l, "wo", i, None)
                norm(l, 1)

                def evac_gu(i):
                    def evac(s, t):
                        n = l * (2 * FF // UC) + 2 * i + t
                        if s == 0:
                            nc.scalar.activation(gate_t[:, t, :], bank[t][:, :], ACT.Tanh, scale=0.5).then_inc(sem["glu_t"], 1)
                        else:
                            act.wait_ge(sem["glu_v"], n + 1)
                            copy(act_hi[:, bass.ds(i * 2 + t, 1), :].rearrange("p o s -> p (o s)"), glu[:, t, :]).then_inc(sem["act_hi_done"], 1)
                    return evac

                with act.Fori(0, FF // UC) as i:
                    dense(l, "gu", i, evac_gu(i))
                for i in range(6):
                    dense(l, "dn", i, None, kn=DOWN_K[(2 * i + 1) % 3][1], last_kn=DOWN_K[(2 * i + 2) % 3][1], last=i == 5)

        @block.vector
        def _(dve):
            V = nc.vector

            def flat(a):
                return a.rearrange("p o s -> p (o s)")

            def split_lo(l, name, j, s, kn=KT):
                dve.wait_ge(sem["hi_ready"], unit(l, name, j) + 1)
                ins = V.tensor_tensor(w_lo[s][:, 0:kn, :], raw[s][:, 0:kn, :], w_hi[s][:, 0:kn, :].bitcast(F32), ALU.subtract)
                ins.then_inc(sem["split_done"], 1)

            def dense(l, name, i, evac, hooks=(None,) * 5, kn=KT, last_kn=KT, last=False):
                hooks = dict(enumerate(hooks))
                split_lo(l, name, 2 * i + 1, 1, kn)
                for s in range(2):
                    if s == 1 and not last:
                        split_lo(l, name, 2 * i + 2, 0, last_kn)
                    for t in range(2):
                        if hooks.get(2 * s + t):
                            hooks[2 * s + t]()
                        if evac:
                            evac(s, t)
                if hooks.get(4):
                    hooks[4]()

            dve.wait_ge(sem["const_loaded"], 16)
            V.memset(mx2[:, 20:21], 0.0).then_inc(sem["units_done"], 2)
            V.memset(mx2[:, 21:22], 0.0).then_inc(sem["split_done"], 2)
            V.memset(mx2[:, 22:23], 0.0).then_inc(bank_free[0], 1)
            V.memset(mx2[:, 23:24], 0.0).then_inc(bank_free[1], 1)
            for n, name in enumerate(START_AT_1):
                V.memset(st[:, n:n + 1], 0.0).then_inc(sem[name], 1)
            for k in range(KT):
                dve.wait_ge(sem["xt_in_t"], k + 1)
                V.tensor_copy(xt[:, k, :], B[k % 2][:, :]).then_inc(sem["xt_tile"], 1)

            def norm(l, which, gcol):
                dve.wait_ge(sem["ms_done"], 2 * l + which + 1)
                V.tensor_scalar(st[:, 40:44], B[0][:, 0:NB], 1.0 / D, EPS, ALU.mult, ALU.add).then_inc(sem["ms_sb"], 1)
                dve.wait_ge(sem["rstd_done"], 2 * l + which + 1)
                V.tensor_tensor(diag[:, :, :], ident.unsqueeze(1).to_broadcast([P, NB, P]),
                                st[:, 44:48].unsqueeze(2).to_broadcast([P, NB, P]), ALU.mult).then_inc(sem["diag_done"], 1)
                dve.wait_ge(sem["rb_done"], 2 * l + which + 1)
                for k in range(KT):
                    n = l * 16 + (8 * which + k)
                    if k >= 2:
                        dve.drain()
                    V.scalar_tensor_tensor(ntmp[:, k % 2, :], xt[:, k, :], pcol[:, gcol + k:gcol + k + 1], B[1][:, :],
                                           ALU.mult, ALU.mult).then_inc(sem["ntmp_done"], 1)
                    if k >= 1:
                        dve.wait_ge(sem["hhi_done"], n)
                        V.tensor_tensor(h_lo[:, k - 1, :], ntmp[:, (k - 1) % 2, :], h_hi[:, k - 1, :].bitcast(F32), ALU.subtract).then_inc(sem["hlo_done"], 1)
                n = l * 16 + 8 * which + KT
                dve.wait_ge(sem["hhi_done"], n)
                V.tensor_tensor(h_lo[:, KT - 1, :], ntmp[:, (KT - 1) % 2, :], h_hi[:, KT - 1, :].bitcast(F32), ALU.subtract).then_inc(sem["hlo_done"], 1)

            ssq, srstd = st[:, 0:16], st[:, 16:32]
            smax, ssum, rs, mx = st_s[:, 0:8], st_s[:, 8:16], st_s[:, 16:24], st_s[:, 24:32]

            def attn_rope(l, h):
                hd = l * AH + h + 1
                q = qkn[:, bass.ds(h, 1)].rearrange("p o a b d -> p (o a b d)") if not isinstance(h, int) else qkn[:, h].rearrange("p a b d -> p (a b d)")
                grp = q.rearrange("p (g d) -> p g d", d=DK)
                pos = lambda ap: ap.rearrange("p (ab c d) -> p ab c d", c=2, d=DK)
                tab = lambda f, lo, hi: rope[:, f, :, :, lo:hi].rearrange("p a b d -> p (a b) d").unsqueeze(2).to_broadcast([P, 2 * NB, 2, hi - lo])
                flat0, flat1 = e0[:, :, :].rearrange("p a s -> p (a s)"), e1[:, :, :].rearrange("p a s -> p (a s)")
                dve.wait_ge(sem["q_sq"], hd)
                V.tensor_reduce(mx2[:, 0:16], flat0.rearrange("p (g d) -> p g d", d=DK), AX.X, ALU.add)
                dve.drain()
                V.tensor_scalar(ssq, mx2[:, 0:16], 1.0 / DK, EPS, ALU.mult, ALU.add).then_inc(sem["q_ss"], 1)
                dve.wait_ge(sem["q_rstd"], hd)
                V.tensor_tensor(grp, grp, srstd.unsqueeze(2).to_broadcast([P, 16, DK]), ALU.mult)
                dve.drain()
                h2 = DK // 2
                V.tensor_tensor(pos(flat1), pos(q), tab(0, 0, DK), ALU.mult)
                V.tensor_tensor(pos(flat0)[:, :, :, 0:h2], pos(q)[:, :, :, h2:DK], tab(1, 0, h2), ALU.mult)
                V.tensor_tensor(pos(flat0)[:, :, :, h2:DK], pos(q)[:, :, :, 0:h2], tab(1, h2, DK), ALU.mult)
                dve.drain()
                V.tensor_tensor(flat1, flat1, flat0, ALU.add).then_inc(sem["q_roped"], 1)

            def attn_max(l, h, qb):
                n = (qb + 1) * P
                dve.wait_ge(sem["s_done"], (l * AH + h) * 4 + qb + 1)
                for c in range(2):
                    d = B[2 * (qb % 2) + c][:, qb * P:n]
                    V.tensor_tensor(d, d, causal, ALU.add)
                dve.drain()
                for c in range(2):
                    V.tensor_reduce(mx[:, 2 * qb + c:2 * qb + c + 1], B[2 * (qb % 2) + c][:, 0:n], AX.X, ALU.max)
                dve.drain()
                V.tensor_scalar(smax[:, 2 * qb:2 * qb + 2], mx[:, 2 * qb:2 * qb + 2], -DK ** -0.5, None, ALU.mult).then_inc(sem["s_max"], 1)

            def attn_combine(l, h, qb):
                n = (qb + 1) * P
                e = (e0, e1)[qb % 2]
                o = pair_off(qb) * P
                dve.wait_ge(sem["s_exp"], (l * AH + h) * 8 + 2 * qb + 2 + 1)
                if qb == 0:
                    dve.wait_ge(sem["a_t"], (l * AH + h) * 4 + 1)
                V.reciprocal(rs[:, 2 * qb:2 * qb + 2], ssum[:, 2 * qb:2 * qb + 2])
                dve.drain()
                V.tensor_scalar(e[:, 1, 0:n], e[:, 1, 0:n], rs[:, 2 * qb + 1:2 * qb + 2], lamt[:, 5:6], ALU.mult, ALU.mult)
                dve.drain()
                V.scalar_tensor_tensor(probs[:, o:o + n], e[:, 0, 0:n], rs[:, 2 * qb:2 * qb + 1], e[:, 1, 0:n],
                                       ALU.mult, ALU.add).then_inc(sem["s_comb"], 1)

            def attn_oss(l, h):
                dve.wait_ge(sem["o_sq"], l * AH + h + 1)
                V.tensor_reduce(mx2[:, 16:20], osq[:, :, :], AX.X, ALU.add)
                dve.drain()
                V.tensor_scalar(st[:, 32:36], mx2[:, 16:20], 1.0 / P, EPS, ALU.mult, ALU.add).then_inc(sem["o_ss"], 1)

            def attn_onorm(l, h):
                dve.wait_ge(sem["o_rstd"], l * AH + h + 1)
                V.tensor_tensor(osq[:, :, :], B[4][:, :].rearrange("p (b d) -> p b d", b=NB),
                                st[:, 36:40].unsqueeze(2).to_broadcast([P, NB, P]), ALU.mult).then_inc(sem["o_norm"], 1)

            def attn_olo(l, h):
                dve.wait_ge(sem["o_hi"], l * AH + h + 1)
                V.scalar_tensor_tensor(flat(o_sp[:, bass.ds(h, 1), 1, :]), B[5][:, :], lamt[:, 4:5],
                                       flat(o_sp[:, bass.ds(h, 1), 0, :]).bitcast(F32), ALU.mult, ALU.subtract).then_inc(sem["o_lo"], 1)

            def attention_step(l, name, i, h, tail=True):
                def before0():
                    attn_rope(l, h)

                def before1():
                    if tail:
                        attn_oss(l, h - 1)
                        attn_onorm(l, h - 1)

                def before3():
                    attn_max(l, h, 0)
                    attn_max(l, h, 1)
                    attn_combine(l, h, 0)
                    attn_combine(l, h, 1)

                def after():
                    attn_max(l, h, 2)
                    attn_max(l, h, 3)
                    if tail:
                        attn_olo(l, h - 1)
                    attn_combine(l, h, 2)
                    attn_combine(l, h, 3)

                dense(l, name, i, None, (before0, before1, None, before3, after))

            with dve.Fori(0, DEPTH) as l:
                dve.wait_ge(sem["prow_t"], l + 1)
                V.tensor_copy(pcol[:, :], B[2][:, 0:NROWS])
                dve.drain()
                split_lo(l, "aq", 0, 0)
                norm(l, 0, R_GMIX)
                V.tensor_scalar(lamt[:, 4:5], pcol[:, R_GDH:R_GDH + 1], kc[:, bass.ds(l * 2 + (K_LAM + 1), 1)], None, ALU.mult)
                dve.wait_ge(sem["small_loaded"], 48 * (l + 1))
                V.tensor_tensor(lamp[:, :, :], lams[:, 0:4:2, :], lams[:, 1:4:2, :], ALU.mult)
                dve.drain()
                V.tensor_reduce(lamt[:, 0:2], lamp[:, :, :], AX.X, ALU.add).then_inc(sem["lam_sum"], 1)
                cs = kc[:, K_COS:K_ALL].rearrange("p (b f d) -> p b f d", b=NB, f=2)
                h2 = DK // 2
                for a in range(2):
                    g = lambda lo: gqk[:, a, lo:lo + h2].unsqueeze(1).to_broadcast([P, NB, h2])
                    V.tensor_tensor(rope[:, 0, a, :, 0:h2], cs[:, :, 0, :], g(0), ALU.mult)
                    V.tensor_tensor(rope[:, 0, a, :, h2:DK], cs[:, :, 0, :], g(h2), ALU.mult)
                    V.scalar_tensor_tensor(rope[:, 1, a, :, 0:h2], cs[:, :, 1, :], -1.0, g(h2), ALU.mult, ALU.mult)
                    V.tensor_tensor(rope[:, 1, a, :, h2:DK], cs[:, :, 1, :], g(0), ALU.mult)
                dve.wait_ge(sem["if_hi"], l + 1)
                V.tensor_tensor(wif_lo[:, :, :], wif, wif_hi[:, :, :].bitcast(F32), ALU.subtract).then_inc(sem["if_split"], 1)
                dve.wait_ge(sem["lam_exp"], l + 1)
                V.tensor_tensor(lamt[:, 6:7], lamt[:, 3:4], lamt[:, 2:3], ALU.subtract)
                dve.drain()
                V.tensor_tensor(lamt[:, 5:6], lamt[:, 6:7], kc[:, bass.ds(l * 2 + K_LAM, 1)], ALU.subtract)
                dve.wait_ge(sem["if_done"], l + 1)
                V.tensor_copy(ifn[:, :], B[0][:, 0:NB * 8]).then_inc(sem["ifn_done"], 1)
                for name in ("aq", "ak", "av"):
                    with dve.Fori(0, 2) as i:
                        dense(l, name, i, None)
                attention_step(l, "vo", 0, 0, tail=False)
                with dve.Fori(1, 4) as i:
                    attention_step(l, "vo", i, i)
                with dve.Fori(0, 2) as i:
                    attention_step(l, "pu", i, i + 4)
                with dve.Fori(0, 2) as i:
                    attention_step(l, "mq", i, i + 6)

                def rows_scan():
                    dve.wait_ge(sem["row_log"], l + 1)
                    r = slice(0, MH)
                    V.scalar_tensor_tensor(row_u[r, :], row_b[r, :], 0.0, row_t[r, :], ALU.min, ALU.subtract)
                    dve.drain()
                    for c in range(NB):
                        k = slice(c * P, (c + 1) * P)
                        V.tensor_tensor_scan(row_b[r, k], ones[r, :], row_u[r, k], 0.0, ALU.mult, ALU.add)
                    dve.drain()
                    V.tensor_tensor(row_i[r, :], row_i[r, :], row_b[r, :], ALU.subtract)
                    V.memset(row_t[r, 0:P], 0.0)
                    dve.drain()
                    for c in range(NB):
                        k = slice(c * P, (c + 1) * P)
                        first = NEG_BIG if c == 0 else mp[r, c:c + 1]
                        V.tensor_tensor_scan(row_m[r, k], row_t[r, 0:P], row_i[r, k], first, ALU.add, ALU.max)
                        V.tensor_copy(row_a[r, (pair_off(c) + c) * P:pair_off(c + 1) * P], row_i[r, k])
                        dve.drain()
                        if c < NB - 1:
                            end = (c + 1) * P - 1
                            V.tensor_tensor(mp[r, c + 1:c + 2], row_m[r, end:end + 1], row_b[r, end:end + 1], ALU.add)
                            V.tensor_scalar(row_a[r, pair_off(c + 1) * P:(pair_off(c + 1) + c + 1) * P],
                                            row_a[r, pair_off(c) * P:pair_off(c + 1) * P], row_b[r, end:end + 1], None, ALU.add)
                            dve.drain()
                    V.tensor_tensor(row_u[r, :], row_b[r, :], row_m[r, :], ALU.add).then_inc(sem["row_ready"], 1)

                def rows_cols():
                    dve.wait_ge(sem["row_t2"], l + 1)
                    V.tensor_copy(ac[:, :], B[1][:, 0:40]).then_inc(sem["row_cols"], 1)

                dense(l, "mk", 0, None, (None, lambda: (attn_oss(l, AH - 1), attn_onorm(l, AH - 1)), None, None, lambda: attn_olo(l, AH - 1)))

                def pooled(g):
                    w = 2 << g
                    src = (pa, pb)[g % 2]
                    dve.wait_ge(sem["p_sum"], l * 4 + g + 1)
                    V.scalar_tensor_tensor(src[:, :, 0:w], src[:, :, 0:w], float(w),
                                           kc[:, K_CNT:K_CNT + w].unsqueeze(1).to_broadcast([P, 2, w]), ALU.mult, ALU.mult)
                    dve.drain()
                    V.scalar_tensor_tensor(mg[:, 2 * g:2 * g + 2, :], src[:, :, :], 1.0 / w, mg[:, 2 * g:2 * g + 2, :],
                                           ALU.mult, ALU.subtract).then_inc(sem["p_pool"], 1)

                def pool_lo(g):
                    dve.wait_ge(sem["p_hi"], l * 4 + g + 1)
                    if g >= 2:
                        dve.wait_ge(sem["units_done"], unit(l, "pool", g - 1) + 2)
                    V.tensor_tensor(pl[g % 2][:, :, :], mg[:, 2 * g:2 * g + 2, :], ph[g % 2][:, :, :].bitcast(F32), ALU.subtract).then_inc(sem["p_lo"], 1)

                dense(l, "mk", 1, None, (None, rows_scan, None, rows_cols, None), last_kn=2)
                pooled(0)
                pool_lo(0)
                dense(l, "pool", 0, None, (lambda: (pooled(1), pool_lo(1)), None, lambda: (pooled(2), pool_lo(2)), None,
                                           lambda: (pooled(3), pool_lo(3))), kn=2, last_kn=2)
                dense(l, "pool", 1, None, kn=2)
                with dve.Fori(0, 2) as i:
                    dense(l, "ga", i, None)

                def evac_wd(i):
                    def evac(s, t):
                        tile_wait(dve, l, "wd", 2 * i + s, t)
                        g = flat(gate[:, bass.ds(i * 4 + (2 * s + t), 1), :])
                        V.scalar_tensor_tensor(g, g, 1.0, bank[t][:, :], ALU.add, ALU.mult).then_inc(bank_free[t], 1)
                    return evac

                wait_alone(dve, sem["gate_done"], (2 * l + 1) * KT)
                with dve.Fori(0, 2) as i:
                    dense(l, "wd", i, evac_wd(i))

                def evac_gp(i):
                    def evac(s, t):
                        n = 4 * i + 2 * s + t
                        dve.wait_ge(sem["tg_done"], l * KT + n + 1)
                        V.scalar_tensor_tensor(mg[:, n, :], tg[:, t, :], 1.0, mg[:, n, :], ALU.add, ALU.mult)
                        dve.drain()
                        V.tensor_tensor(mg[:, n, :], mg[:, n, :], gate[:, n, :], ALU.add).then_inc(sem["merged_val"], 1)
                    return evac

                def m_select(h):
                    V.tensor_scalar(selh[0:MH, :], ones[0:MH, :], kc[0:MH, bass.ds(h + K_HOT, 1)], None, ALU.mult).then_inc(sem["m_sel"], 1)

                def m_mask(h):
                    dve.wait_ge(sem["m_mb"], l * MH + h + 1)
                    V.tensor_tensor(mdiag[:, :, :], B[3][:, :].rearrange("p (b j) -> p b j", b=NB),
                                    big.unsqueeze(1).to_broadcast([P, NB, P]), ALU.add).then_inc(sem["m_diag"], 1)

                def m_conv(h):
                    for k in range(4):
                        src = mqk[:, bass.ds(h, 1), k, :].rearrange("p o s -> p (o s)") if not isinstance(h, int) else mqk[:, h, k, :]
                        w = lambda tap: pcol[:, bass.ds(h * 2 + (R_CONV + tap * 16 + (k // 2) * 8 + k % 2), 1)]
                        V.tensor_scalar(mc[:, k, :], src, w(3), None, ALU.mult)
                        for r in range(1, 4):
                            dve.drain()
                            ins = V.scalar_tensor_tensor(mc[:, k, r:S], src[:, 0:S - r], w(3 - r), mc[:, k, r:S], ALU.mult, ALU.add)
                        ins.then_inc(sem["m_conv"], 1)

                def m_silu(h):
                    for k in range(4):
                        dve.wait_ge(sem["m_th"], (l * MH + h) * 4 + k + 1)
                        V.scalar_tensor_tensor(mc[:, k, :], mth[:, :], 1.0, mc[:, k, :], ALU.add, ALU.mult).then_inc(sem["m_c"], 1)

                def m_weigh(h):
                    hd = l * MH + h + 1
                    dve.wait_ge(sem["m_s"], hd)
                    dve.wait_ge(sem["m_decay"], hd + 1)
                    where = ((0, 0), (1, 0), (2, 0), (1, 3 * P))
                    for sc in range(NB):
                        n = (NB - sc) * P
                        b, o = where[sc]
                        d = decay[:, row_off(sc):row_off(sc) + n]
                        ins = V.scalar_tensor_tensor(d, B[b][:, o:o + n], MDH ** -0.5 / 4, d, ALU.mult, ALU.mult)
                    ins.then_inc(sem["m_sp"], 1)

                def m_norm(h):
                    hd = l * MH + h + 1
                    dve.wait_ge(sem["m_num"], hd + 1)
                    dve.wait_ge(sem["m_tanh"], hd)
                    den, neg, rec = st_s[:, 32:36], st_s[:, 36:40], st_s[:, 40:44]
                    V.tensor_copy(den, B[2][:, 0:NB])
                    for b in range(2):
                        V.scalar_tensor_tensor(hn[:, 2 * b:2 * b + 2, :].rearrange("p b c -> p (b c)"),
                                               moh[:, 2 * b:2 * b + 2, :].rearrange("p b c -> p (b c)"), 1.0,
                                               B[b][:, :], ALU.add, ALU.mult)
                    dve.drain()
                    V.scalar_tensor_tensor(neg, den, -1.0, den, ALU.mult, ALU.max)
                    dve.drain()
                    floor = emt[:, :].rearrange("p (b h) -> p b h", h=MH)[:, :, bass.ds(h, 1)].rearrange("p b o -> p (b o)")
                    V.tensor_tensor(den, neg, floor, ALU.max)
                    dve.drain()
                    V.reciprocal(rec, den)
                    dve.drain()
                    for b in range(NB):
                        ins = V.tensor_scalar(hn[:, b, :], hn[:, b, :], rec[:, b:b + 1], None, ALU.mult)
                    ins.then_inc(sem["m_hn"], 1)

                def m_lo(h):
                    hd = l * MH + h + 1
                    dve.wait_ge(sem["m_hi"], 2 * hd)
                    for v in range(2):
                        ins = V.scalar_tensor_tensor(flat(hm_sp[:, bass.ds(h, 1), 2 + v, :]), B[4 + v][:, :], 0.5,
                                                     flat(hm_sp[:, bass.ds(h, 1), v, :]).bitcast(F32), ALU.mult, ALU.subtract)
                    ins.then_inc(sem["m_lo"], 1)

                def mlstm_step(name, i, h, evac, tail=True):
                    def before0():
                        m_select(h)
                        m_mask(h)
                        m_conv(h)

                    def before1():
                        if tail:
                            m_norm(h - 1)

                    def before2():
                        m_silu(h)

                    def after():
                        m_weigh(h)
                        if tail:
                            m_lo(h - 1)

                    dense(l, name, i, evac, (before0, before1, before2, None, after))

                dve.wait_ge(sem["units_done"], unit(l, "wd", 4) + 2)
                dve.wait_ge(sem["aev"], read_out(l, "mk", 4))
                mlstm_step("gp", 0, 0, evac_gp(0), tail=False)
                mlstm_step("gp", 1, 1, evac_gp(1))
                with dve.Fori(0, 2) as i:
                    mlstm_step("gm", i, i + 2, None)
                m_norm(MH - 1)
                m_lo(MH - 1)

                def evac_wm(i):
                    def evac(s, t):
                        tile_wait(dve, l, "wm", 2 * i + s, t)
                        n = i * 4 + (2 * s + t)
                        V.scalar_tensor_tensor(ytmp[:, t, :], flat(gate[:, bass.ds(n, 1), :]), 1.0, bank[t][:, :], ALU.add, ALU.mult).then_inc(bank_free[t], 1)
                        dve.drain()
                        m = flat(mg[:, bass.ds(n, 1), :])
                        V.tensor_tensor(m, m, ytmp[:, t, :], ALU.add).then_inc(sem["merged_val"], 1)
                        dve.wait_ge(sem["merged_hi_done"], l * KT + n + 1)
                        V.scalar_tensor_tensor(flat(merged_lo[:, bass.ds(n, 1), :]), m, 0.5, flat(merged_hi[:, bass.ds(n, 1), :]).bitcast(F32),
                                               ALU.mult, ALU.subtract).then_inc(sem["merged_lo_done"], 1)
                    return evac

                wait_alone(dve, sem["gate_done"], (2 * l + 2) * KT)
                with dve.Fori(0, 2) as i:
                    dense(l, "wm", i, evac_wm(i))

                def evac_add(name, i):
                    def evac(s, t):
                        tile_wait(dve, l, name, 2 * i + s, t)
                        xk = flat(xt[:, bass.ds(i * 4 + (2 * s + t), 1), :])
                        V.tensor_tensor(xk, xk, bank[t][:, :], ALU.add).then_inc(bank_free[t], 1)
                        dve.drain().then_inc(sem["xt_tile"], 1)
                    return evac

                wait_alone(dve, sem["xt_back"], 16 * (l + 1))
                with dve.Fori(0, 2) as i:
                    dense(l, "wo", i, evac_add("wo", i))
                norm(l, 1, R_GFFN)

                def evac_gu(i):
                    def evac(s, t):
                        n = l * (2 * FF // UC) + 2 * i + t
                        tile_wait(dve, l, "gu", 2 * i + s, t)
                        if s == 0:
                            dve.wait_ge(sem["act_lo_done"], n - t + 1)
                            dve.wait_ge(sem["glu_t"], n + 1)
                            V.scalar_tensor_tensor(glu[:, t, :], gate_t[:, t, :], 1.0, bank[t][:, :], ALU.add, ALU.mult).then_inc(bank_free[t], 1)
                        else:
                            V.scalar_tensor_tensor(glu[:, t, :], glu[:, t, :], 0.5, bank[t][:, :], ALU.mult, ALU.mult).then_inc(bank_free[t], 1)
                            dve.drain().then_inc(sem["glu_v"], 1)
                            dve.wait_ge(sem["act_hi_done"], n + 1)
                            V.tensor_tensor(flat(act_lo[:, bass.ds(i * 2 + t, 1), :]), glu[:, t, :], flat(act_hi[:, bass.ds(i * 2 + t, 1), :]).bitcast(F32),
                                            ALU.subtract).then_inc(sem["act_lo_done"], 1)
                    return evac

                with dve.Fori(0, FF // UC) as i:
                    dense(l, "gu", i, evac_gu(i))

                for i in range(6):
                    def evac_dn(s, t):
                        j = 2 * i + s
                        if j % 3 == 2:
                            tile_wait(dve, l, "dn", j, t)
                            n = 2 * (j // 3) + t
                            V.tensor_tensor(xt[:, n, :], xt[:, n, :], bank[t][:, :], ALU.add).then_inc(bank_free[t], 1)
                            dve.drain().then_inc(sem["xt_tile"], 1)
                    dense(l, "dn", i, evac_dn, kn=DOWN_K[(2 * i + 1) % 3][1], last_kn=DOWN_K[(2 * i + 2) % 3][1], last=i == 5)

            for b in range(NB):
                for c in range(2):
                    n = 2 * b + c
                    dve.wait_ge(sem["fin_t"], n + 1)
                    V.tensor_copy(xnat[:, b, c * S:(c + 1) * S], B[n % 2][:, :]).then_inc(sem["fin_sb"], 1)

        @block.tensor
        def _(pe):
            mm, tr = nc.tensor.matmul, nc.tensor.transpose

            def dense(l, name, i, natural, a_hi, a_lo, kn=KT, hooks=None, tiles=(0, 1)):
                hooks = hooks or {}
                for s in range(2):
                    pe.wait_ge(sem["split_done"], unit(l, name, 2 * i + s) + 3)
                    for t in range(2):
                        pe.wait_ge(bank_free[t], tile(l, name, 2 * i + s) + 1)
                        for half in range(2):
                            if 4 * s + 2 * t + half in hooks:
                                hooks[4 * s + 2 * t + half]()
                            if natural:
                                b = 2 * t + half
                                tok = slice(b * P, (b + 1) * P)
                                dst = bank[t][:, half * UC:(half + 1) * UC]
                                for k in range(kn):
                                    mm(dst, a_hi[:, k, tok], w_hi[s][:, k, :], start=k == 0, stop=False)
                                    mm(dst, a_hi[:, k, tok], w_lo[s][:, k, :], start=False, stop=False)
                                    ins = mm(dst, a_lo[:, k, tok], w_hi[s][:, k, :], start=False, stop=k == kn - 1)
                            else:
                                col = slice(t * P, (t + 1) * P)
                                for k in range(half * kn // 2, (half + 1) * kn // 2):
                                    mm(bank[t][:, :], w_hi[s][:, k, col], a_hi(s, k), start=k == 0, stop=False)
                                    mm(bank[t][:, :], w_hi[s][:, k, col], a_lo(s, k), start=False, stop=False)
                                    ins = mm(bank[t][:, :], w_lo[s][:, k, col], a_hi(s, k), start=False, stop=k == kn - 1)
                        ins.then_inc((sem["tile0_done"], sem["units_done"])[t], 1)

            stream_hi, stream_lo = (lambda s, k: h_hi[:, k, :]), (lambda s, k: h_lo[:, k, :])

            def norm(l, which):
                pe.wait_ge(sem["sq_done"], l * 16 + (8 * which + 8))
                for b in range(NB):
                    for k in range(KT):
                        ins = mm(B[0][:, b:b + 1], sq[:, k, b * P:(b + 1) * P], ones[:, 0:1], start=k == 0, stop=k == KT - 1)
                ins.then_inc(sem["ms_done"], 1)
                pe.wait_ge(sem["diag_done"], 2 * l + which + 1)
                mm(B[1][:, :], ones, diag[:, :, :].rearrange("p b j -> p (b j)"), start=True, stop=True).then_inc(sem["rb_done"], 1)
                wait_alone(pe, sem["hlo_done"], l * 16 + (8 * which + 8))

            def attn_tqk(l, h):
                pe.wait_ge(sem["q_roped"], l * AH + h + 1)
                pe.wait_ge(sem["o_norm"], l * AH + h + 1)
                src = e1[:, :, :].rearrange("p a (b d) -> p a b d", b=NB)
                for a in range(2):
                    for b in range(NB):
                        ins = tr(B[4 + a][:, b * P:(b + 1) * P], src[:, a, b, :], ident)
                ins.then_inc(sem["q_t"], 1)

            def attn_scores(l, h, qb):
                if qb == 0:
                    pe.wait_ge(sem["q_tsb"], (l * AH + h + 1) * 2)
                    pe.wait_ge(sem["s_exp"], (l * AH + h) * 8 + 1)
                elif qb >= 2:
                    pe.wait_ge(sem["s_exp"], (l * AH + h) * 8 + 2 * (qb - 1) + 1)
                n = (qb + 1) * P
                for c in range(2):
                    r = slice(c * DK, (c + 1) * DK)
                    ins = mm(B[2 * (qb % 2) + c][:, 0:n], qk_t[r, 0, qb * P:n], qk_t[r, 1, 0:n], start=True, stop=True)
                ins.then_inc(sem["s_done"], 1)

            def attn_tprobs(l, h, qbs):
                for qb in qbs:
                    pe.wait_ge(sem["s_comb"], (l * AH + h) * 4 + qb + 1)
                    if qb == 1:
                        pe.wait_ge(sem["o_lo"], l * AH + h + 1)
                    if qb >= 2:
                        pe.wait_ge(sem["a_tsb"], (l * AH + h) * 4 + qb - 1)
                    for kb in range(qb + 1):
                        o = (pair_off(qb) + kb) * P
                        ins = tr(B[4 + qb % 2][:, kb * P:(kb + 1) * P], probs[:, o:o + P], ident)
                    ins.then_inc(sem["a_t"], 1)

            def attn_values(l, h):
                pe.wait_ge(sem["a_tsb"], (l * AH + h) * 4 + 4)
                pe.wait_ge(sem["aev"], read_out(l, "av", 4))
                for qb in range(NB):
                    for kb in range(qb + 1):
                        o = (pair_off(qb) + kb) * P
                        ins = mm(B[4][:, qb * P:(qb + 1) * P], probs_t[:, o:o + P],
                                 av[:, kb, bass.ds(h * P, P)], start=kb == 0, stop=kb == qb)
                ins.then_inc(sem["o_done"], 1)

            def attn_tout(l, h):
                pe.wait_ge(sem["o_norm"], l * AH + h + 1 + 1)
                for b in range(NB):
                    ins = tr(B[5][:, b * P:(b + 1) * P], osq[:, b, :], ident)
                ins.then_inc(sem["o_t"], 1)

            def attn_hooks(l, h, tail=True):
                hooks = {4: lambda: attn_tqk(l, h), 5: lambda: (attn_scores(l, h, 0), attn_scores(l, h, 1)),
                         7: lambda: (attn_scores(l, h, 2), attn_scores(l, h, 3))}
                if tail:
                    hooks[0] = lambda: attn_tprobs(l, h - 1, (0, 1))
                    hooks[1] = lambda: attn_tprobs(l, h - 1, (2, 3))
                    hooks[2] = lambda: attn_values(l, h - 1)
                    hooks[6] = lambda: (attn_tout(l, h - 1))
                return hooks

            pe.wait_ge(sem["const_loaded"], 16)
            pe.wait_ge(sem["x_loaded"], 16)
            for k in range(KT):
                if k >= 2:
                    pe.wait_ge(sem["xt_tile"], k - 1)
                for b in range(NB):
                    ins = tr(B[k % 2][:, b * P:(b + 1) * P], xnat[:, b, k * P:(k + 1) * P], ident)
                ins.then_inc(sem["xt_in_t"], 1)

            with pe.Fori(0, DEPTH) as l:
                pe.wait_ge(sem["prow_loaded"], 80 * (l + 1))
                tr(B[2][:, 0:NROWS], prow[0:NROWS, :], ident[0:NROWS, 0:NROWS]).then_inc(sem["prow_t"], 1)
                norm(l, 0)
                pe.wait_ge(sem["if_split"], l + 1)
                for b in range(NB):
                    tok = slice(b * P, (b + 1) * P)
                    dst = B[0][:, b * 8:(b + 1) * 8]
                    for k in range(KT):
                        mm(dst, h_hi[:, k, tok], wif_hi[:, k, :], start=k == 0, stop=False)
                        mm(dst, h_hi[:, k, tok], wif_lo[:, k, :], start=False, stop=False)
                        ins = mm(dst, h_lo[:, k, tok], wif_hi[:, k, :], start=False, stop=k == KT - 1)
                ins.then_inc(sem["if_done"], 1)
                for name in ("aq", "ak", "av"):
                    with pe.Fori(0, 2) as i:
                        dense(l, name, i, True, h_hi, h_lo)
                dense(l, "vo", 0, True, h_hi, h_lo, hooks=attn_hooks(l, 0, tail=False))
                with pe.Fori(1, 4) as i:
                    dense(l, "vo", i, True, h_hi, h_lo, hooks=attn_hooks(l, i))
                with pe.Fori(0, 2) as i:
                    dense(l, "pu", i, False, stream_hi, stream_lo, hooks=attn_hooks(l, i + 4))
                with pe.Fori(0, 2) as i:
                    dense(l, "mq", i, False, stream_hi, stream_lo, hooks=attn_hooks(l, i + 6))

                def rows_in():
                    wait_alone(pe, sem["ifn_done"], l + 1)
                    for a in range(2):
                        for b in range(NB):
                            ins = tr(B[a][0:MH, b * P:(b + 1) * P], ifn[:, b * 8 + a * MH:b * 8 + (a + 1) * MH], ident)
                    ins.then_inc(sem["row_t1"], 1)

                def rows_out():
                    wait_alone(pe, sem["row_ready"], l + 1)
                    for b in range(NB):
                        tr(B[0][:, b * MH:(b + 1) * MH], row_u[0:MH, b * P:(b + 1) * P], ident[0:MH, 0:MH])
                    for n in range(10):
                        ins = tr(B[1][:, n * MH:(n + 1) * MH], row_a[0:MH, n * P:(n + 1) * P], ident[0:MH, 0:MH])
                    ins.then_inc(sem["row_t2"], 1)

                last = AH - 1
                dense(l, "mk", 0, False, stream_hi, stream_lo, hooks={
                    0: lambda: attn_tprobs(l, last, (0, 1)), 1: lambda: attn_tprobs(l, last, (2, 3)),
                    2: lambda: attn_values(l, last), 4: lambda: attn_tout(l, last), 6: rows_in})
                dense(l, "mk", 1, False, stream_hi, stream_lo, hooks={6: rows_out})
                for i in range(2):
                    for_unit = {4 * s: (lambda s=s: pe.wait_ge(sem["p_lo"], l * 4 + (2 * i + s) + 1)) for s in range(2)}
                    dense(l, "pool", i, False, lambda s, k: ph[s][:, k, :], lambda s, k: pl[s][:, k, :], kn=2, hooks=for_unit)
                with pe.Fori(0, 2) as i:
                    dense(l, "ga", i, False, stream_hi, stream_lo)
                wait_alone(pe, sem["o_lo"], l * AH + AH + 1)
                with pe.Fori(0, 2) as i:
                    dense(l, "wd", i, False, lambda s, k: o_sp[:, k, 0, :], lambda s, k: o_sp[:, k, 1, :])

                def m_spread(h):
                    pe.wait_ge(sem["m_sel"], l * MH + h + 1)
                    pe.wait_ge(sem["m_decay"], l * MH + h + 1)
                    mm(B[3][:, :], selh[0:MH, :], row_m[0:MH, :], start=True, stop=True).then_inc(sem["m_mb"], 1)

                def m_scores(h):
                    pe.wait_ge(sem["m_c"], (l * MH + h + 1) * 4)
                    for sc in range(NB):
                        b, o = ((0, 0), (1, 0), (2, 0), (1, 3 * P))[sc]
                        n = (NB - sc) * P
                        for k in range(2):
                            ins = mm(B[b][:, o:o + n], mc[:, 2 + k, sc * P:(sc + 1) * P], mc[:, k, sc * P:S], start=k == 0, stop=k == 1)
                    ins.then_inc(sem["m_s"], 1)

                def m_values(h):
                    hd = l * MH + h + 1
                    pe.wait_ge(sem["m_sp"], hd)
                    pe.wait_ge(sem["m_vo"], hd * 32)
                    for jc in range(NB):
                        for sc in range(jc + 1):
                            o = row_off(sc) + (jc - sc) * P
                            w = decay[:, o:o + P]
                            mm(B[jc // 2][:, (jc % 2) * MDH:(jc % 2 + 1) * MDH], w, mvh[:, sc, :], start=sc == 0, stop=sc == jc)
                            ins = mm(B[2][:, jc:jc + 1], w, ones[:, 0:1], start=sc == 0, stop=sc == jc)
                    ins.then_inc(sem["m_num"], 1)

                def m_turn(h):
                    pe.wait_ge(sem["m_hn"], l * MH + h + 1)
                    pe.wait_ge(sem["m_lo"], l * MH + h + 1)
                    for v in range(2):
                        for b in range(NB):
                            ins = tr(B[4 + v][:, b * P:(b + 1) * P], hn[:, b, v * P:(v + 1) * P], ident)
                    ins.then_inc(sem["m_ht"], 1)

                def m_hooks(h, tail=True):
                    hooks = {0: lambda: m_spread(h), 6: lambda: m_scores(h)}
                    if tail:
                        hooks[1] = lambda: m_values(h - 1)
                        hooks[5] = lambda: m_turn(h - 1)
                    return hooks

                dense(l, "gp", 0, False, stream_hi, stream_lo, hooks=m_hooks(0, tail=False))
                dense(l, "gp", 1, False, stream_hi, stream_lo, hooks=m_hooks(1))
                with pe.Fori(0, 2) as i:
                    dense(l, "gm", i, False, stream_hi, stream_lo, hooks=m_hooks(i + 2))
                m_values(MH - 1)
                m_turn(MH - 1)
                wait_alone(pe, sem["m_lo"], l * MH + MH + 1)
                hm_hi = lambda s, k: hm_sp[:, k // 2, k % 2, :]
                hm_lo = lambda s, k: hm_sp[:, k // 2, 2 + k % 2, :]
                with pe.Fori(0, 2) as i:
                    dense(l, "wm", i, False, hm_hi, hm_lo)
                wait_alone(pe, sem["merged_lo_done"], l * KT + KT)
                with pe.Fori(0, 2) as i:
                    dense(l, "wo", i, False, lambda s, k: merged_hi[:, k, :], lambda s, k: merged_lo[:, k, :])
                norm(l, 1)
                with pe.Fori(0, FF // UC) as i:
                    dense(l, "gu", i, False, stream_hi, stream_lo)
                pe.wait_ge(sem["act_lo_done"], (l + 1) * FT + 1)
                for j in range(12):
                    s = j % 2
                    k0, kn = DOWN_K[j % 3]
                    pe.wait_ge(sem["split_done"], unit(l, "dn", j) + 3)
                    for t in range(2):
                        if j % 3 == 0:
                            pe.wait_ge(bank_free[t], tile(l, "dn", j // 3) + 1)
                        col = slice(t * P, (t + 1) * P)
                        for k in range(kn):
                            mm(bank[t][:, :], w_hi[s][:, k, col], act_hi[:, k0 + k, :], start=k0 + k == 0, stop=False)
                            mm(bank[t][:, :], w_hi[s][:, k, col], act_lo[:, k0 + k, :], start=False, stop=False)
                            ins = mm(bank[t][:, :], w_lo[s][:, k, col], act_hi[:, k0 + k, :], start=False, stop=k0 + k == FT - 1)
                        if t == 1:
                            ins.then_inc(sem["units_done"], 1)
                        elif j % 3 == 2:
                            ins.then_inc(sem["tile0_done"], 1)

            pe.wait_ge(sem["xt_tile"], 8 + 16 * DEPTH)
            for b in range(NB):
                for c in range(2):
                    n = 2 * b + c
                    if n >= 2:
                        pe.wait_ge(sem["fin_sb"], n - 1)
                    for k in range(4):
                        ins = tr(B[n % 2][:, k * P:(k + 1) * P], xt[:, 4 * c + k, b * P:(b + 1) * P], ident)
                    ins.then_inc(sem["fin_t"], 1)


_INS = ["x", "g_mix", "w_in", "b_if", "conv_qk", "w_m_out", "w_pool", "pool_scale", "g_qk", "lam_p", "g_diff_head",
        "w_diff_out", "w_out", "g_ffn", "w_gate_up", "w_down"]


def shape_constants():
    import math
    import numpy as np

    c = np.zeros((P, K_ALL), np.float32)
    i = np.arange(P)
    c[:, K_ID:K_ID + P] = np.eye(P)
    c[:, K_MASK:K_MASK + P] = np.where(i[None, :] > i[:, None], NEG_BIG, 0.0)
    c[:, K_BIG:K_BIG + P] = np.where(i[:, None] > i[None, :], -NEG_BIG, 0.0)
    c[:, K_ONE:K_ONE + P] = 1.0
    c[:MH, K_HOT:K_HOT + MH] = np.eye(MH)
    c[:, K_CNT:K_CNT + 16] = 1.0 / np.arange(1, 17)
    for layer in range(DEPTH):
        lam_init = 0.8 - 0.6 * math.exp(-0.3 * layer)
        c[:, K_LAM + 2 * layer] = lam_init
        c[:, K_LAM + 2 * layer + 1] = 1.0 - lam_init
    half = DK // 2
    inv = np.power(np.float32(10000.0), -np.arange(half, dtype=np.float32) / np.float32(half), dtype=np.float32)
    ang = np.arange(S, dtype=np.float32)[:, None] * inv[None, :]
    cs = np.stack([np.cos(ang), np.sin(ang)], 1).astype(np.float32)
    c[:, K_COS:] = cs.reshape(NB, P, 2 * half).transpose(1, 0, 2).reshape(P, -1)
    return c


def kernel(**inputs):
    import numpy as np
    import concourse.bacc as bacc
    from concourse.bass_utils import run_bass_kernel_spmd

    nc = bacc.Bacc("TRN2", target_bir_lowering=False, num_devices=1)
    arrays = {f"in_{name}": np.ascontiguousarray(inputs[name]) for name in _INS}
    arrays["in_consts"] = shape_constants()
    args = [nc.dram_tensor(n, a.shape, mybir.dt.from_np(a.dtype), kind="ExternalInput").ap() for n, a in arrays.items()]
    out = nc.dram_tensor("out_0", (1, S, D), F32, kind="ExternalOutput").ap()
    build_trunk(nc, *args, out)
    result = run_bass_kernel_spmd(nc, [arrays], core_ids=[0])
    return result.results[0]["out_0"]
```

```python
import concourse.bass as bass
from concourse import mybir
from concourse.alu_op_type import AluOpType as ALU

F32 = mybir.dt.float32
F32R = mybir.dt.float32r
ACT = mybir.ActivationFunctionType
AX = mybir.AxisListType

P = 128
D = 1024
S = 512
DEPTH = 2
KT = D // P
NB = S // P
FF = 2816
FT = FF // P
UC = 256
MH, MDH = 4, 256
AH, DK = 8, 64
EPS = 1e-6
NEG_BIG = -1e30

C_MQ, C_MK, C_MV, C_IF, C_PU = 0, D, 2 * D, 4 * D, 4 * D + 2 * MH
C_AQ = C_PU + D
C_GM = C_AQ + 3 * D
C_GP, C_GA = C_GM + D, C_GM + 2 * D

SECTIONS = [("aq", 4, 4), ("ak", 4, 4), ("pu", 4, 4), ("pool", 2, 4), ("av", 4, 4), ("vo", 8, 8),
            ("mq", 4, 4), ("mk", 4, 4), ("ga", 4, 4), ("wd", 4, 4), ("gp", 4, 4), ("gm", 4, 4), ("wm", 4, 4), ("wo", 4, 4),
            ("gu", 2 * FF // UC, 2 * FF // UC), ("dn", 12, 4)]
UBASE, VBASE = {}, {}
UPL = VPL = 0
for _n, _u, _v in SECTIONS:
    UBASE[_n], VBASE[_n] = UPL, VPL
    UPL, VPL = UPL + _u, VPL + _v
NATURAL = {"aq": 0, "ak": 4, "av": 8, "vo": 12}
DOWN_K = ((0, 8), (8, 8), (16, 6))

R_GMIX, R_GFFN, R_PSC, R_CONV, R_GDH = 0, KT, 2 * KT, 3 * KT, 3 * KT + 64
NROWS = R_GDH + 1

K_ID, K_MASK, K_BIG, K_ONE, K_HOT, K_CNT, K_LAM, K_COS = 0, 128, 256, 384, 512, 516, 532, 536
K_ALL = K_COS + NB * 2 * (DK // 2)


def pair_off(jc):
    return jc * (jc + 1) // 2


def row_off(sc):
    return sum(NB - c for c in range(sc)) * P


def build_trunk(nc, x, g_mix, w_in, b_if, conv_qk, w_m_out, w_pool, pool_scale, g_qk, lam_p, g_diff_head,
                w_diff_out, w_out, g_ffn, w_gate_up, w_down, consts, out):
    base = (nc.sbuf_base + 31) // 32 * 32
    KB = 1024

    def at(name, offset, shape, dt=F32):
        return nc.alloc_sbuf_tensor_at(name, shape, dt, offset=base + offset)

    h_hi = at("h_hi", 0, [P, KT, S], F32R)
    h_lo = at("h_lo", 16 * KB, [P, KT, S], F32R)
    raw = [at(f"raw{s}", (32 + 8 * s) * KB, [P, KT, UC]) for s in range(2)]
    w_hi = [at(f"w_hi{s}", (48 + 8 * s) * KB, [P, KT, UC], F32R) for s in range(2)]
    w_lo = [at(f"w_lo{s}", (64 + 8 * s) * KB, [P, KT, UC], F32R) for s in range(2)]
    Z1, Z2, Z3, Z4, ZT = 80 * KB, 112 * KB, 144 * KB, 160 * KB, 176 * KB
    qkn = at("qkn", Z1, [P, AH, 2, NB, P])
    o_sp = at("o_sp", Z1, [P, AH, 2, S], F32R)
    merged_hi = at("merged_hi", Z1, [P, KT, S], F32R)
    merged_lo = at("merged_lo", Z1 + 16 * KB, [P, KT, S], F32R)
    xnat = at("xnat", Z1, [P, NB, D])
    vo = at("vo", Z2, [P, 2 * MH, NB, UC])
    p_hi = at("p_hi", Z2, [P, KT, S], F32R)
    p_lo = at("p_lo", Z2 + 16 * KB, [P, KT, S], F32R)
    mqk = at("mqk", Z2, [P, MH, 4, S])
    hm_sp = at("hm_sp", Z2, [P, MH, 4, S], F32R)
    av = at("av", Z3, [P, NB, D])
    gate = at("gate", Z3, [P, KT, S])
    mg = at("mg", Z4, [P, KT, S])
    act_hi = at("act_hi", Z1, [P, FT, S], F32R)
    act_lo = at("act_lo", Z1 + 44 * KB, [P, FT, S], F32R)
    xt = at("xt", ZT, [P, KT, S])
    glu = at("glu", ZT + 16 * KB, [P, 2, S])
    diag = at("diag", ZT + 16 * KB, [P, NB, P])
    sqt = at("sqt", Z4 + 8 * KB, [P, 2, S])
    sqsum = at("sqsum", ZT + 20 * KB, [P, S])
    prow = at("prow", Z3, [P, DEPTH, P])
    tg = at("tg", ZT + 16 * KB, [P, 2, S])
    gate_t = at("gate_t", Z4 + 8 * KB, [P, 2, S])
    glu_up = at("glu_up", Z4 + 12 * KB, [P, 2, S])
    e0 = at("e0", ZT, [P, 2, S])
    e1 = at("e1", ZT + 4 * KB, [P, 2, S])
    qk_t = at("qk_t", ZT + 8 * KB, [P, 2, S])
    probs = at("probs", ZT + 12 * KB, [P, 10 * P])
    probs_t = at("probs_t", ZT + 17 * KB, [P, 10 * P])
    osq = at("osq", ZT + 17 * KB, [P, NB, P])
    cv = at("cv", ZT + 8 * KB, [P, 3, S])
    th = at("th", ZT + 14 * KB, [P, S])
    mvh = at("mvh", Z1, [P, 2, NB, MDH])
    moh = at("moh", Z1 + 8 * KB, [P, 2, NB, MDH])
    decay = at("decay", Z1 + 16 * KB, [P, 10 * P])
    hn = at("hn", Z1 + 21 * KB, [P, NB, MDH])
    mdiag = at("mdiag", Z1 + 25 * KB, [P, NB, P])
    qsq = at("qsq", Z3, [P, 2, S])
    pa = at("pa", Z2 + 16 * KB, [P, 2, S])
    pb = at("pb", Z2 + 20 * KB, [P, 2, S])
    ytmp = at("ytmp", ZT + 16 * KB, [P, 2, S])
    row_i = at("row_i", ZT, [P, S])
    row_b = at("row_b", ZT + 2 * KB, [P, S])
    row_t = at("row_t", ZT + 4 * KB, [P, S])
    row_u = at("row_u", ZT + 6 * KB, [P, S])
    row_a = at("row_a", ZT + 16 * KB, [P, 10 * P])
    off = ZT + 22 * KB
    table = {}
    for name, cols in (("kc", K_ALL), ("rope", 2 * 2 * NB * DK), ("pcol", DEPTH * NROWS + KT), ("rb", S),
                       ("ac", 40), ("emt", 4 * MH), ("ifn", NB * 8), ("wif", KT * 8), ("lamt", 8), ("qst", AH * 16), ("selh", MH * P),
                       ("bif", 2), ("st", 48), ("st_s", 48), ("mx2", 24), ("mp", 8)):
        table[name] = at(name, off, [P, cols])
        if name == "rope":
            rope_at = off
        off += (4 * cols + 31) // 32 * 32
    wif_hi = at("wif_hi", off, [P, KT, 8], F32R)
    wif_lo = at("wif_lo", off + 32 * KT, [P, KT, 8], F32R)
    off += 64 * KT
    assert base + off <= nc.sbuf_usable_end, (base + off, nc.sbuf_usable_end)
    kc, pcol, rb, ac, emt, ifn, lamt, bif, st, st_s, mx2, mp = (
        table[n] for n in ("kc", "pcol", "rb", "ac", "emt", "ifn", "lamt", "bif", "st", "st_s", "mx2", "mp"))
    row_m = at("row_m", rope_at, [P, S])
    rope = table["rope"][:].rearrange("p (f a b d) -> p f a b d", f=2, a=2, b=NB)
    qst = table["qst"][:].rearrange("p (h a b c) -> p h a b c", h=AH, a=2, b=NB)
    selh = table["selh"][:].rearrange("p (h j) -> p h j", h=MH)
    wif = table["wif"][:].rearrange("p (k c) -> p k c", k=KT)
    gqk = at("gqk", Z4 + 12 * KB, [P, 2, DK])
    lams = at("lams", Z4 + 13 * KB, [P, 4, DK])
    lamp = at("lamp", Z4 + 14 * KB, [P, 2, DK])
    ident = kc[:, K_ID:K_ID + P]
    causal = kc[:, K_MASK:K_MASK + P]
    big = kc[:, K_BIG:K_BIG + P]
    ones = kc[:, K_ONE:K_ONE + P]

    bank = [nc.alloc_psum_tensor(f"dense{t}", [P, S], F32) for t in range(2)]
    B = [nc.alloc_psum_tensor(f"side{t}", [P, S], F32) for t in range(6)]

    xt_dram = nc.dram_tensor("xt_spill", [P, KT * S], F32, kind="Internal").ap()
    vo_dram = nc.dram_tensor("vo_spill", [P, 2 * MH, NB * UC], F32, kind="Internal").ap()

    sem_names = """raw_ready0 raw_ready1 hi_ready split_done units_done tile0_done
        bank_free0 bank_free1 const_loaded x_loaded xt_in_t xt_tile gate_out tg_out glu_in sq_done sq_summed ms_done ms_sb rstd_done diag_done
        rb_done hhi_done hlo_done prow_loaded prow_t dve_out small_loaded rope_done lam_sum lam_exp lam_done
        if_loaded if_hi if_split if_done ifn_done spilled xt_back aev q_sq q_red q_ss q_rstd q_roped q_t q_tsb s_done s_max s_exp
        s_comb a_t a_tsb o_done o_sq o_ss o_rstd o_norm o_t o_hi o_lo row_t1 row_log row_ready row_t2 row_cols emt_cols
        v_spilled o_spilled0 o_spilled1 m_sel m_mb m_diag m_decay m_tap m_conv m_th m_c m_s m_sp m_num m_vo0 m_vo1 m_tanh m_hn m_ht m_hi m_lo
        pool_tile1 pooled p_hi p_lo pool_out tg_done gate_done merged_val merged_hi_done merged_lo_done glu_t glu_v act_hi_done act_lo_done
        waits_over fin_t fin_sb stored vo_done""".split()
    sem = {n: nc.alloc_semaphore(n) for n in sem_names}
    raw_ready = [sem["raw_ready0"], sem["raw_ready1"]]
    START_AT_1 = ("o_norm", "s_exp", "a_t", "o_lo", "m_decay", "m_num", "m_lo", "m_c", "act_lo_done")
    bank_free = [sem["bank_free0"], sem["bank_free1"]]

    def unit(l, name, j):
        return l * UPL + (UBASE[name] + j)

    def tile(l, name, j):
        return l * VPL + (VBASE[name] + j)

    def wait_alone(eng, s, value):
        eng.wait_ge(s, value)
        eng.sem_inc(sem["waits_over"], 1)

    def tile_wait(eng, l, name, j, t):
        if t == 1:
            eng.wait_ge(sem["units_done"], unit(l, name, j) + 3)
        else:
            eng.wait_ge(sem["tile0_done"], tile(l, name, j // 3 if name == "dn" else j) + 1)

    def read_out(l, name, j):
        return l * 40 + 2 * (NATURAL[name] + j)

    def dve_out(l, name, j):
        return l * (2 * (VBASE["ga"] - VBASE["mq"])) + 2 * (VBASE[name] + j - VBASE["mq"])

    def stream_tile(norm, k):
        return norm * KT + k

    with nc.Block() as block:

        @block.sync
        def _(sp):
            sp.dma_start(kc[:, :], consts).then_inc(sem["const_loaded"], 16)
            sp.dma_start(xnat[:, :, :], x[0].rearrange("(b p) d -> p b d", p=P)).then_inc(sem["x_loaded"], 16)

            def load(l, name, j, s, src, kn=KT):
                need = sp.snap(unit(l, name, j) + 1)
                sp.wait_ge(sem["split_done"], need)
                sp.dma_start(raw[s][:, 0:kn, :], src).then_inc(raw_ready[s], 16)

            def columns(w, l, col, rows=D):
                return w[bass.ds(l, 1), :, bass.ds(col, UC)].rearrange("o (k p) n -> p (o k) n", p=P)

            def section(l, name, w, col, n, first=0):
                with sp.Fori(first // 2, n // 2) as i:
                    for s in range(2):
                        load(l, name, 2 * i + s, s, columns(w, l, i * (2 * UC) + (col + s * UC)))

            def layer(l, next_l):
                load(l, "aq", 1, 1, columns(w_in, l, C_AQ + UC))
                section(l, "aq", w_in, C_AQ, 8, first=2)
                section(l, "pu", w_in, C_PU, 4)
                for s in range(2):
                    g = w_pool[bass.ds(l, 1), 2 * s:2 * s + 2].rearrange("o g (k p) n -> p (o g k) n", p=P)
                    load(l, "pool", s, s, g, 4)
                section(l, "av", w_in, C_AQ + 2 * D, 4)
                section(l, "vo", w_in, C_MV, 8)
                section(l, "mq", w_in, C_MQ, 8)
                section(l, "ga", w_in, C_GA, 4)
                section(l, "wd", w_diff_out, 0, 4)
                section(l, "gp", w_in, C_GP, 4)
                section(l, "gm", w_in, C_GM, 4)
                section(l, "wm", w_m_out, 0, 4)
                section(l, "wo", w_out, 0, 4)
                with sp.Fori(0, FF // UC) as i:
                    for s in range(2):
                        load(l, "gu", 2 * i + s, s, columns(w_gate_up, l, i * UC + s * FF))
                with sp.Fori(0, 2) as i:
                    for j in range(6):
                        k0, kn = DOWN_K[j % 3]
                        src = w_down[bass.ds(l, 1), k0 * P:(k0 + kn) * P, bass.ds(i * (2 * UC) + (j // 3) * UC, UC)]
                        load(l, "dn", 6 * i + j, j % 2, src.rearrange("o (k p) n -> p (o k) n", p=P), kn)
                load(l, "dn", 12, 0, columns(w_in, next_l, C_AQ))

            load(0, "aq", 0, 0, columns(w_in, 0, C_AQ))
            with sp.Fori(0, DEPTH - 1) as l:
                layer(l, l + 1)
            layer(DEPTH - 1, DEPTH - 1)
            for b in range(NB):
                sp.wait_ge(sem["fin_sb"], 2 * b + 2)
                sp.dma_start(out[0, b * P:(b + 1) * P, :], xnat[:, b, :]).then_inc(sem["stored"], 16)
            sp.wait_ge(sem["stored"], 16 * NB)

        @block.gpsimd
        def _(pool):
            def inv_sqrt(dst, src, n):
                return pool.tensor_tensor(dst, src, mp[:, 0:1].to_broadcast([P, n]), ALU.pow)

            pool.memset(mp[:, 0:1], -0.5)
            pool.drain()

            def attention_out(l, h):
                wait_alone(pool, sem["o_ss"], l * AH + h + 1)
                inv_sqrt(st[:, 36:40], st[:, 32:36], 4).then_inc(sem["o_rstd"], 1)

            def square_sums(norm):
                for k in range(KT):
                    wait_alone(pool, sem["sq_done"], stream_tile(norm, k) + 1)
                    if k == 0:
                        ins = pool.tensor_copy(sqsum[:, :], sqt[:, 0, :])
                    else:
                        pool.drain()
                        ins = pool.tensor_tensor(sqsum[:, :], sqsum[:, :], sqt[:, k % 2, :], ALU.add)
                    ins.then_inc(sem["sq_summed"], 1)

            def norm_rstd(norm):
                wait_alone(pool, sem["ms_sb"], norm + 1)
                inv_sqrt(st[:, 44:48], st[:, 40:44], 4).then_inc(sem["rstd_done"], 1)

            for lay in range(DEPTH):
                one = slice(lay, lay + 1)
                for row, rows, src in ((R_GMIX, KT, g_mix[one].rearrange("o (t p) -> (o t) p", p=P)),
                                       (R_GFFN, KT, g_ffn[one].rearrange("o (t p) -> (o t) p", p=P)),
                                       (R_PSC, KT, pool_scale[one].rearrange("o (t p) -> (o t) p", p=P)),
                                       (R_CONV, 64, conv_qk[one].rearrange("o w (t p) -> (o w t) p", p=P)),
                                       (R_GDH, 1, g_diff_head[one])):
                    pool.dma_start(prow[row:row + rows, lay, :], src).then_inc(sem["prow_loaded"], 16)
            square_sums(0)
            with pool.Fori(0, DEPTH) as l:
                one = bass.ds(l, 1)
                with nc.allow_non_contiguous_dma(reason="eight numbers"):
                    pool.dma_start(bif[0:MH, 0:2], b_if[one].rearrange("o (t h) -> h (o t)", t=2)).then_inc(sem["small_loaded"], 16)
                pool.dma_start(gqk[:, :, :], g_qk[one].rearrange("o a d -> o (a d)").to_broadcast([P, 2 * DK]).rearrange("p (a d) -> p a d", a=2)).then_inc(sem["small_loaded"], 16)
                pool.dma_start(lams[:, :, :], lam_p[one].rearrange("o a d -> o (a d)").to_broadcast([P, 4 * DK]).rearrange("p (a d) -> p a d", a=4)).then_inc(sem["small_loaded"], 16)
                with nc.allow_non_contiguous_dma(reason="eight columns of w_in"):
                    pool.dma_start(wif, w_in[one, :, C_IF:C_IF + 2 * MH].rearrange("o (k p) n -> p (o k) n", p=P)).then_inc(sem["if_loaded"], 16)
                norm_rstd(2 * l)
                wait_alone(pool, sem["xt_tile"], stream_tile(2 * l, KT))
                pool.dma_start(xt_dram, xt[:, :, :].rearrange("p k s -> p (k s)")).then_inc(sem["spilled"], 16)
                wait_alone(pool, sem["q_ss"], l + 1)
                inv_sqrt(table["qst"][:, :], table["qst"][:, :], AH * 16).then_inc(sem["q_rstd"], 1)
                wait_alone(pool, sem["pool_out"], (l + 1) * KT)
                for g in range(4):
                    w = 2 << g
                    y = mg[:, 2 * g:2 * g + 2, :]
                    src = y
                    for n in range(g + 1):
                        dst = (pa, pb)[n % 2]
                        v = 1 << n
                        pool.tensor_copy(dst[:, :, 0:v], src[:, :, 0:v])
                        pool.tensor_tensor(dst[:, :, v:S], src[:, :, v:S], src[:, :, 0:S - v], ALU.add)
                        pool.drain()
                        src = dst
                    pool.tensor_tensor(src[:, :, 0:w], src[:, :, 0:w], kc[:, K_CNT:K_CNT + w].unsqueeze(1).to_broadcast([P, 2, w]), ALU.mult)
                    pool.tensor_scalar(src[:, :, w:S], src[:, :, w:S], 1.0 / w, None, ALU.mult)
                    pool.drain()
                    pool.tensor_tensor(y, src[:, :, :], y, ALU.subtract).then_inc(sem["pooled"], 1)
                    pool.drain()
                attention_out(l, 0)
                for i, (units, done) in enumerate((((0, 4), "v_spilled"), ((4, 6), "o_spilled0"), ((6, 8), "o_spilled1"))):
                    attention_out(l, i + 1)
                    wait_alone(pool, sem["aev"], read_out(l, "vo", units[1]))
                    pool.dma_start(vo_dram[:, units[0]:units[1], :],
                                   vo[:, units[0]:units[1], :, :].rearrange("p u b c -> p u (b c)")).then_inc(sem[done], 16)
                with pool.Fori(4, AH) as i:
                    attention_out(l, i)
                for done in ("v_spilled", "o_spilled0", "o_spilled1"):
                    wait_alone(pool, sem[done], 16 * (l + 1))

                def vo_head(h):
                    for dst, u in ((mvh, h), (moh, h + MH)):
                        pool.dma_start(dst[:, h % 2, :, :].rearrange("p b c -> p (b c)"), vo_dram[:, u, :]).then_inc(sem[f"m_vo{h % 2}"], 16)

                wait_alone(pool, sem["units_done"], unit(l, "wd", 4) + 2)
                vo_head(0)
                vo_head(1)
                wait_alone(pool, sem["m_c"], (l + 1) * 4 * MH + 1)
                pool.dma_start(xt[:, :, :].rearrange("p k s -> p (k s)"), xt_dram).then_inc(sem["xt_back"], 16)
                for h in range(2, MH):
                    wait_alone(pool, sem["m_hn"], l * MH + h - 1)
                    vo_head(h)
                square_sums(2 * l + 1)
                norm_rstd(2 * l + 1)
                square_sums(2 * l + 2)

        @block.scalar
        def _(act):
            def copy(dst, src, scale=1.0):
                return nc.scalar.activation(dst, src, ACT.Identity, scale=scale)

            def split_hi(l, name, j, s, kn=KT):
                u = unit(l, name, j)
                act.wait_ge(sem["units_done"], u + 1)
                act.wait_ge(raw_ready[s], (u - s) * 8 + 16)
                copy(w_hi[s][:, 0:kn, :], raw[s][:, 0:kn, :]).then_inc(sem["hi_ready"], 1)

            def dense(l, name, i, evac, hooks=(None,) * 5, kn=KT, last_kn=KT, wait_tile=True):
                hooks = dict(enumerate(hooks))
                split_hi(l, name, 2 * i + 1, 1, kn)
                for s in range(2):
                    for t in range(2):
                        if hooks.get(2 * s + t):
                            hooks[2 * s + t]()
                        if (s, t) == (1, 0):
                            split_hi(l, name, 2 * i + 2, 0, last_kn)
                        if evac:
                            if wait_tile:
                                tile_wait(act, l, name, 2 * i + s, t)
                            evac(s, t)
                if hooks.get(4):
                    hooks[4]()

            def stream_hi(norm, k, kk, gcol):
                n = stream_tile(norm, k)
                wait_alone(act, sem["xt_tile"], n + 1)
                tile_k = xt[:, bass.ds(k, 1), :].rearrange("p o s -> p (o s)")
                nc.scalar.activation(h_hi[:, bass.ds(k, 1), :].rearrange("p o s -> p (o s)"), tile_k, ACT.Identity,
                                     scale=pcol[:, bass.ds(gcol + k, 1)]).then_inc(sem["hhi_done"], 1)
                wait_alone(act, sem["sq_summed"], n + 1)
                nc.scalar.activation(sqt[:, kk % 2, :], tile_k, ACT.Square).then_inc(sem["sq_done"], 1)

            def attn_qk(l, h):
                act.wait_ge(sem["q_t"], l * AH + h + 1)
                for c in range(2):
                    copy(qk_t[:, c, :], B[4 + c][:, :]).then_inc(sem["q_tsb"], 1)

            smax, ssum = st_s[:, 0:8], st_s[:, 8:16]

            def attn_exp(l, h, qbs):
                for qb in qbs:
                    n = (qb + 1) * P
                    act.wait_ge(sem["s_max"], (l * AH + h) * 4 + qb + 1)
                    e = (e0, e1)[qb % 2]
                    if qb >= 2:
                        act.wait_ge(sem["s_comb"], (l * AH + h) * 4 + qb - 1)
                    for c in range(2):
                        o = 2 * qb + c
                        ins = nc.scalar.activation(e[:, c, 0:n], B[2 * (qb % 2) + c][:, 0:n], ACT.Exp,
                                                   bias=smax[:, o:o + 1], scale=DK ** -0.5, accum_out=ssum[:, o:o + 1])
                        ins.then_inc(sem["s_exp"], 1)

            def attn_probs(l, h, qbs):
                for qb in qbs:
                    act.wait_ge(sem["a_t"], (l * AH + h) * 4 + qb + 1 + 1)
                    n = (qb + 1) * P
                    o = pair_off(qb) * P
                    copy(probs_t[:, o:o + n], B[4 + qb % 2][:, 0:n]).then_inc(sem["a_tsb"], 1)

            def attn_osq(l, h):
                act.wait_ge(sem["o_done"], l * AH + h + 1)
                nc.scalar.activation(osq[:, :, :], B[0][:, :].rearrange("p (b d) -> p b d", b=NB),
                                     ACT.Square).then_inc(sem["o_sq"], 1)

            def attn_ohi(l, h):
                act.wait_ge(sem["o_t"], l * AH + h + 1)
                nc.scalar.activation(o_sp[:, bass.ds(h, 1), 0, :].rearrange("p o s -> p (o s)"), B[5][:, :], ACT.Identity,
                                     scale=lamt[:, 4:5]).then_inc(sem["o_hi"], 1)

            def blocks(dst, t):
                for b in range(2):
                    n = 2 * t + b
                    ins = nc.scalar.activation(dst(n), bank[t][:, b * UC:(b + 1) * UC], ACT.Identity, scale=st[:, 44 + n:45 + n])
                ins.then_inc(bank_free[t], 1)
                act.drain().then_inc(sem["aev"], 1)

            def evac_qk(l, i, qk):
                def evac(s, t):
                    n = l * 16 + 8 * qk + 4 * i + 2 * s + t
                    wait_alone(act, sem["q_red"], n + 1)
                    for b in range(2):
                        ins = nc.scalar.activation(qsq[:, t, b * UC:(b + 1) * UC], bank[t][:, b * UC:(b + 1) * UC], ACT.Square,
                                                   scale=st[:, 44 + 2 * t + b:45 + 2 * t + b])
                    ins.then_inc(sem["q_sq"], 1)
                    blocks(lambda b: qkn[:, bass.ds(i * 4 + 2 * s, 2), qk, b, :], t)
                return evac

            def evac_nat(i, dst):
                def evac(s, t):
                    blocks(lambda b: dst[:, b, bass.ds(i * (2 * UC) + s * UC, UC)], t)
                return evac

            def evac_vo(i):
                def evac(s, t):
                    blocks(lambda b: vo[:, bass.ds(2 * i + s, 1), b, :].rearrange("p o c -> p (o c)"), t)
                return evac

            def evac_pu(i):
                def evac(s, t):
                    copy(p_hi[:, bass.ds(i * 4 + (2 * s + t), 1), :].rearrange("p o s -> p (o s)"), bank[t][:, :]).then_inc(sem["p_hi"], 1)
                return evac

            def attention_step(l, name, i, h, evac, tail=True):
                def before0():
                    if tail:
                        attn_probs(l, h - 1, (0, 1, 2, 3))

                def before1():
                    if tail:
                        attn_osq(l, h - 1)

                def before2():
                    attn_qk(l, h)
                    attn_exp(l, h, (0, 1))

                def before3():
                    if tail:
                        attn_ohi(l, h - 1)
                    attn_exp(l, h, (2, 3))

                dense(l, name, i, evac, (before0, before1, before2, before3, None))

            for k in range(KT):
                stream_hi(0, k, k, R_GMIX)
                if k == 1:
                    split_hi(0, "aq", 0, 0)

            def layer_head(l):
                act.wait_ge(sem["lam_sum"], l + 1)
                nc.scalar.activation(lamt[:, 2:4], lamt[:, 0:2], ACT.Exp).then_inc(sem["lam_exp"], 1)
                act.wait_ge(sem["if_loaded"], 16 * (l + 1))
                copy(wif_hi[:, :, :], wif).then_inc(sem["if_hi"], 1)

            with act.Fori(0, DEPTH) as l:
                dense(l, "aq", 0, evac_qk(l, 0, 0), (lambda: act.wait_ge(sem["rstd_done"], 2 * l + 1), None, None, None, None))
                layer_head(l)
                dense(l, "aq", 1, evac_qk(l, 1, 0))
                with act.Fori(0, 2) as i:
                    dense(l, "ak", i, evac_qk(l, i, 1))
                with act.Fori(0, 2) as i:
                    dense(l, "pu", i, evac_pu(i))
                dense(l, "pool", 0, None, kn=4)
                wait_alone(act, sem["q_red"], (l + 1) * 16 + 2)
                dense(l, "av", 0, evac_nat(0, av))
                attention_step(l, "av", 1, 0, evac_nat(1, av), tail=False)
                wait_alone(act, sem["pool_out"], (l + 1) * KT)
                with act.Fori(0, 2) as i:
                    attention_step(l, "vo", i, i + 1, evac_vo(i))
                wait_alone(act, sem["pooled"], (l + 1) * 4)
                with act.Fori(2, 4) as i:
                    attention_step(l, "vo", i, i + 1, evac_vo(i))
                with act.Fori(0, 2) as i:
                    attention_step(l, "mq", i, i + 5, None)
                attention_step(l, "mk", 0, 7, None)

                def tail0():
                    attn_probs(l, AH - 1, (0, 1, 2, 3))

                def tail1():
                    attn_osq(l, AH - 1)

                def tail3():
                    attn_ohi(l, AH - 1)

                def rows_log():
                    act.wait_ge(sem["row_t1"], l + 1)
                    nc.scalar.activation(row_i[0:MH, :], B[0][0:MH, :], ACT.Identity, bias=bif[0:MH, 0:1])
                    nc.scalar.activation(row_b[0:MH, :], B[1][0:MH, :], ACT.Identity, bias=bif[0:MH, 1:2])
                    nc.scalar.activation(row_t[0:MH, :], B[1][0:MH, :], ACT.Abs, bias=bif[0:MH, 1:2])
                    act.drain()
                    nc.scalar.activation(row_u[0:MH, :], row_t[0:MH, :], ACT.Exp, scale=-1.0)
                    act.drain()
                    nc.scalar.activation(row_t[0:MH, :], row_u[0:MH, :], ACT.Ln, bias=1.0).then_inc(sem["row_log"], 1)

                def rows_emt():
                    act.wait_ge(sem["row_t2"], l + 1)
                    nc.scalar.activation(emt[:, :], B[0][:, 0:4 * MH], ACT.Exp, scale=-1.0).then_inc(sem["emt_cols"], 1)

                dense(l, "mk", 1, None, (tail0, tail1, None, tail3, rows_log))

                def gate_tanh(which, i):
                    def tanh(s, t):
                        n = i * 4 + (2 * s + t)
                        act.wait_ge(sem["gate_out"], (2 * l + which) * KT + n + 1)
                        g = gate[:, bass.ds(n, 1), :].rearrange("p o s -> p (o s)")
                        nc.scalar.activation(g, g, ACT.Tanh, scale=0.5).then_inc(sem["gate_done"], 1)
                    return tanh

                def conv_hooks(h):
                    base = (l * MH + h) * 4

                    def tap(k):
                        act.wait_ge(sem["m_c"], base + (2 if k == 3 else 1))
                        nc.scalar.activation(cv[:, k % 3, :], mqk[:, bass.ds(h, 1), k, :].rearrange("p o s -> p (o s)"), ACT.Identity,
                                             scale=pcol[:, bass.ds(l * NROWS + h * 2 + (R_CONV + 3 * 16 + (k // 2) * 8 + k % 2), 1)]
                                             ).then_inc(sem["m_tap"], 1)

                    def tanh(k):
                        act.wait_ge(sem["m_conv"], base + k + 1)
                        act.wait_ge(sem["m_c"], base + k + 1)
                        nc.scalar.activation(th[:, :], cv[:, k % 3, :], ACT.Tanh, scale=0.5).then_inc(sem["m_th"], 1)

                    return [lambda: (tap(0), tap(1), tanh(0)), lambda: (tap(2), tanh(1)), lambda: (tap(3), tanh(2)), lambda: tanh(3)]

                wait_alone(act, sem["dve_out"], dve_out(l, "mk", 4))
                dense(l, "ga", 0, gate_tanh(0, 0), conv_hooks(0) + [None], wait_tile=False)
                dense(l, "ga", 1, gate_tanh(0, 1), (None, None, None, None, rows_emt), wait_tile=False)
                with act.Fori(0, 2) as i:
                    dense(l, "wd", i, None, conv_hooks(i + 1) + [None])

                def m_front_decay(h):
                    hd = l * MH + h + 1
                    act.wait_ge(sem["m_diag"], hd)
                    act.wait_ge(sem["m_num"], l * MH + h + 1)
                    for jc in range(NB):
                        for sc in range(jc + 1):
                            src = mdiag[:, jc, :] if sc == jc else B[3][:, jc * P:(jc + 1) * P]
                            o = row_off(sc) + (jc - sc) * P
                            ins = nc.scalar.activation(decay[:, o:o + P], src, ACT.Exp, scale=-1.0,
                                                       bias=ac[:, h + 4 * (pair_off(jc) + sc):h + 4 * (pair_off(jc) + sc) + 1])
                    ins.then_inc(sem["m_decay"], 1)

                def m_tanh(h):
                    act.wait_ge(sem[f"m_vo{h % 2}"], (l * 2 + h // 2 + 1) * 32)
                    o = moh[:, h % 2, :, :]
                    nc.scalar.activation(o, o, ACT.Tanh, scale=0.5).then_inc(sem["m_tanh"], 1)

                def m_hi(h):
                    act.wait_ge(sem["m_ht"], l * MH + h + 1)
                    for v in range(2):
                        copy(hm_sp[:, h, v, :], B[4 + v][:, :], 0.5).then_inc(sem["m_hi"], 1)

                def tg_tanh(i):
                    def tanh(s, t):
                        act.wait_ge(sem["tg_out"], l * KT + 4 * i + 2 * s + t + 1)
                        nc.scalar.activation(tg[:, t, :], tg[:, t, :], ACT.Tanh, scale=0.5).then_inc(sem["tg_done"], 1)
                    return tanh

                for h, (name, i, evac) in enumerate((("gp", 0, tg_tanh(0)), ("gp", 1, tg_tanh(1)),
                                                     ("gm", 0, gate_tanh(1, 0)), ("gm", 1, gate_tanh(1, 1)))):
                    conv = conv_hooks(MH - 1) if h == 0 else [None] * 4
                    front = lambda h=h: (m_front_decay(h), m_tanh(h))
                    hooks = (lambda: (front(), conv[0] and conv[0]()), conv[1], conv[2], conv[3], lambda: m_hi(h))
                    dense(l, name, i, evac, hooks, wait_tile=False)

                def merge_hi(n):
                    act.wait_ge(sem["merged_val"], l * KT + n + 1)
                    copy(merged_hi[:, bass.ds(n, 1), :].rearrange("p o s -> p (o s)"), mg[:, bass.ds(n, 1), :].rearrange("p o s -> p (o s)"), 0.5).then_inc(sem["merged_hi_done"], 1)

                with act.Fori(0, 2) as i:
                    dense(l, "wm", i, None, (None, lambda: merge_hi(i * 4), lambda: merge_hi(i * 4 + 1), lambda: merge_hi(i * 4 + 2), lambda: merge_hi(i * 4 + 3)))

                def stream_tiles(norm, gcol, i):
                    return lambda s, t: stream_hi(norm, i * 4 + (2 * s + t), t, gcol)

                with act.Fori(0, 2) as i:
                    dense(l, "wo", i, stream_tiles(2 * l + 1, l * NROWS + R_GFFN, i), wait_tile=False)

                def evac_gu(i):
                    def evac(s, t):
                        n = l * (2 * FF // UC) + 2 * i + t
                        if s == 0:
                            act.wait_ge(sem["glu_in"], n + 1)
                            nc.scalar.activation(gate_t[:, t, :], glu[:, t, :], ACT.Tanh, scale=0.5).then_inc(sem["glu_t"], 1)
                        else:
                            act.wait_ge(sem["glu_v"], n + 1)
                            copy(act_hi[:, bass.ds(i * 2 + t, 1), :].rearrange("p o s -> p (o s)"), glu[:, t, :]).then_inc(sem["act_hi_done"], 1)
                    return evac

                with act.Fori(0, FF // UC) as i:
                    dense(l, "gu", i, evac_gu(i), wait_tile=False)
                for i in range(6):
                    def evac_dn(s, t):
                        j = 2 * i + s
                        if j % 3 == 2:
                            stream_hi(2 * l + 2, 2 * (j // 3) + t, t, (l + 1) * NROWS + R_GMIX)
                    dense(l, "dn", i, evac_dn, kn=DOWN_K[(2 * i + 1) % 3][1], last_kn=DOWN_K[(2 * i + 2) % 3][1] if i < 5 else KT, wait_tile=False)

        @block.vector
        def _(dve):
            V = nc.vector

            def flat(a):
                return a.rearrange("p o s -> p (o s)")

            def split_lo(l, name, j, s, kn=KT):
                dve.wait_ge(sem["hi_ready"], unit(l, name, j) + 1)
                ins = V.tensor_tensor(w_lo[s][:, 0:kn, :], raw[s][:, 0:kn, :], w_hi[s][:, 0:kn, :].bitcast(F32), ALU.subtract)
                ins.then_inc(sem["split_done"], 1)

            def dense(l, name, i, evac, hooks=(None,) * 5, kn=KT, last_kn=KT):
                hooks = dict(enumerate(hooks))
                split_lo(l, name, 2 * i + 1, 1, kn)
                for s in range(2):
                    for t in range(2):
                        if hooks.get(2 * s + t):
                            hooks[2 * s + t]()
                        if (s, t) == (1, 0):
                            split_lo(l, name, 2 * i + 2, 0, last_kn)
                        if evac:
                            evac(s, t)
                if hooks.get(4):
                    hooks[4]()

            dve.wait_ge(sem["const_loaded"], 16)
            V.memset(mx2[:, 20:21], 0.0).then_inc(sem["units_done"], 2)
            V.memset(mx2[:, 21:22], 0.0).then_inc(sem["split_done"], 2)
            V.memset(mx2[:, 19:20], 0.0).then_inc(sem["sq_summed"], 2)
            V.memset(mx2[:, 18:19], 0.0).then_inc(sem["q_red"], 2)
            V.tensor_copy(selh[0:MH], kc[0:MH, K_HOT:K_HOT + MH].unsqueeze(2).to_broadcast([MH, MH, P])).then_inc(sem["m_sel"], 1)
            V.memset(mx2[:, 22:23], 0.0).then_inc(bank_free[0], 1)
            V.memset(mx2[:, 23:24], 0.0).then_inc(bank_free[1], 1)
            for n, name in enumerate(START_AT_1):
                V.memset(st[:, n:n + 1], 0.0).then_inc(sem[name], 1)
            dve.wait_ge(sem["prow_t"], 1)
            V.tensor_copy(pcol[:, 0:DEPTH * NROWS], B[2][:, 0:DEPTH * NROWS])
            V.tensor_copy(pcol[:, DEPTH * NROWS:DEPTH * NROWS + KT], B[2][:, R_GMIX:R_GMIX + KT])

            def stream_lo(norm, k, gcol):
                dve.wait_ge(sem["hhi_done"], stream_tile(norm, k) + 1)
                V.scalar_tensor_tensor(flat(h_lo[:, bass.ds(k, 1), :]), flat(xt[:, bass.ds(k, 1), :]), pcol[:, bass.ds(gcol + k, 1)],
                                       flat(h_hi[:, bass.ds(k, 1), :]).bitcast(F32), ALU.mult, ALU.subtract).then_inc(sem["hlo_done"], 1)

            for k in range(KT):
                dve.wait_ge(sem["xt_in_t"], k + 1)
                V.tensor_copy(xt[:, k, :], B[k % 2][:, :]).then_inc(sem["xt_tile"], 1)
                if k >= 1:
                    stream_lo(0, k - 1, R_GMIX)
                if k == 2:
                    split_lo(0, "aq", 0, 0)
            stream_lo(0, KT - 1, R_GMIX)

            def norm_rstd(norm):
                dve.wait_ge(sem["ms_done"], norm + 1)
                V.tensor_scalar(st[:, 40:44], B[0][:, 0:NB], 1.0 / D, EPS, ALU.mult, ALU.add).then_inc(sem["ms_sb"], 1)
                dve.wait_ge(sem["rstd_done"], norm + 1)
                V.tensor_tensor(diag[:, :, :], ident.unsqueeze(1).to_broadcast([P, NB, P]),
                                st[:, 44:48].unsqueeze(2).to_broadcast([P, NB, P]), ALU.mult).then_inc(sem["diag_done"], 1)
                dve.wait_ge(sem["rb_done"], norm + 1)
                V.tensor_copy(rb[:, :], B[1][:, :])
                dve.drain()

            def sum_squares(l, qk, i):
                def reduce(s, t):
                    dve.wait_ge(sem["q_sq"], l * 16 + 8 * qk + 4 * i + 2 * s + t + 1)
                    for b in range(2):
                        ins = V.tensor_reduce(qst[:, bass.ds(i * 4 + 2 * s, 2), qk, 2 * t + b, :],
                                              qsq[:, t, b * UC:(b + 1) * UC].rearrange("p (h c d) -> p h c d", h=2, c=2), AX.X, ALU.add)
                    ins.then_inc(sem["q_red"], 1)
                return reduce

            smax, ssum, rs, mx = st_s[:, 0:8], st_s[:, 8:16], st_s[:, 16:24], st_s[:, 24:32]

            def attn_rope(l, h):
                q = qkn[:, bass.ds(h, 1)].rearrange("p o a b d -> p (o a b d)") if not isinstance(h, int) else qkn[:, h].rearrange("p a b d -> p (a b d)")
                grp = q.rearrange("p (g d) -> p g d", d=DK)
                pos = lambda ap: ap.rearrange("p (ab c d) -> p ab c d", c=2, d=DK)
                tab = lambda f, lo, hi: rope[:, f, :, :, lo:hi].rearrange("p a b d -> p (a b) d").unsqueeze(2).to_broadcast([P, 2 * NB, 2, hi - lo])
                flat0, flat1 = e0[:, :, :].rearrange("p a s -> p (a s)"), e1[:, :, :].rearrange("p a s -> p (a s)")
                if isinstance(h, int):
                    dve.wait_ge(sem["q_rstd"], l + 1)
                    dve.wait_ge(sem["aev"], read_out(l, "av", 0))
                    dve.wait_ge(sem["spilled"], 16 * (l + 1))
                rstd = qst[:, bass.ds(h, 1)].rearrange("p o a b c -> p (o a b c)")
                V.tensor_tensor(grp, grp, rstd.unsqueeze(2).to_broadcast([P, 16, DK]), ALU.mult)
                dve.drain()
                h2 = DK // 2
                V.tensor_tensor(pos(flat1), pos(q), tab(0, 0, DK), ALU.mult)
                V.tensor_tensor(pos(flat0)[:, :, :, 0:h2], pos(q)[:, :, :, h2:DK], tab(1, 0, h2), ALU.mult)
                V.tensor_tensor(pos(flat0)[:, :, :, h2:DK], pos(q)[:, :, :, 0:h2], tab(1, h2, DK), ALU.mult)
                dve.drain()
                V.tensor_tensor(flat1, flat1, flat0, ALU.add).then_inc(sem["q_roped"], 1)

            def attn_max(l, h, qb):
                n = (qb + 1) * P
                dve.wait_ge(sem["s_done"], (l * AH + h) * 4 + qb + 1)
                for c in range(2):
                    d = B[2 * (qb % 2) + c][:, qb * P:n]
                    V.tensor_tensor(d, d, causal, ALU.add)
                dve.drain()
                for c in range(2):
                    V.tensor_reduce(mx[:, 2 * qb + c:2 * qb + c + 1], B[2 * (qb % 2) + c][:, 0:n], AX.X, ALU.max)
                dve.drain()
                V.tensor_scalar(smax[:, 2 * qb:2 * qb + 2], mx[:, 2 * qb:2 * qb + 2], -DK ** -0.5, None, ALU.mult).then_inc(sem["s_max"], 1)

            def attn_combine(l, h, qb):
                n = (qb + 1) * P
                e = (e0, e1)[qb % 2]
                o = pair_off(qb) * P
                dve.wait_ge(sem["s_exp"], (l * AH + h) * 8 + 2 * qb + 2 + 1)
                if qb == 0:
                    dve.wait_ge(sem["a_t"], (l * AH + h) * 4 + 1)
                V.reciprocal(rs[:, 2 * qb:2 * qb + 2], ssum[:, 2 * qb:2 * qb + 2])
                dve.drain()
                V.tensor_scalar(e[:, 1, 0:n], e[:, 1, 0:n], rs[:, 2 * qb + 1:2 * qb + 2], lamt[:, 5:6], ALU.mult, ALU.mult)
                dve.drain()
                V.scalar_tensor_tensor(probs[:, o:o + n], e[:, 0, 0:n], rs[:, 2 * qb:2 * qb + 1], e[:, 1, 0:n],
                                       ALU.mult, ALU.add).then_inc(sem["s_comb"], 1)

            def attn_oss(l, h):
                dve.wait_ge(sem["o_sq"], l * AH + h + 1)
                V.tensor_reduce(mx2[:, 16:20], osq[:, :, :], AX.X, ALU.add)
                dve.drain()
                V.tensor_scalar(st[:, 32:36], mx2[:, 16:20], 1.0 / P, EPS, ALU.mult, ALU.add).then_inc(sem["o_ss"], 1)

            def attn_onorm(l, h):
                dve.wait_ge(sem["o_rstd"], l * AH + h + 1)
                V.tensor_tensor(osq[:, :, :], B[0][:, :].rearrange("p (b d) -> p b d", b=NB),
                                st[:, 36:40].unsqueeze(2).to_broadcast([P, NB, P]), ALU.mult).then_inc(sem["o_norm"], 1)

            def attn_olo(l, h):
                dve.wait_ge(sem["o_hi"], l * AH + h + 1)
                V.scalar_tensor_tensor(flat(o_sp[:, bass.ds(h, 1), 1, :]), B[5][:, :], lamt[:, 4:5],
                                       flat(o_sp[:, bass.ds(h, 1), 0, :]).bitcast(F32), ALU.mult, ALU.subtract).then_inc(sem["o_lo"], 1)

            def scaled_out(l, name, i, dst, done, first=None):
                def evac(s, t):
                    tile_wait(dve, l, name, 2 * i + s, t)
                    V.tensor_tensor(dst(s, t), bank[t][:, :], rb[:, :], ALU.mult).then_inc(bank_free[t], 1)
                    dve.drain().then_inc(sem[done], 1)
                return evac

            def out_pu(l, i):
                def evac(s, t):
                    n = i * 4 + (2 * s + t)
                    dve.wait_ge(sem["p_hi"], l * KT + n + 1)
                    V.tensor_tensor(flat(p_lo[:, bass.ds(n, 1), :]), bank[t][:, :], flat(p_hi[:, bass.ds(n, 1), :]).bitcast(F32),
                                    ALU.subtract).then_inc(bank_free[t], 1)
                    dve.drain().then_inc(sem["p_lo"], 1)
                return evac

            def out_pool(l):
                def evac(s, u):
                    g = 2 * s + u
                    for t in range(2):
                        n = 2 * g + t
                        if t == 0:
                            dve.wait_ge(sem["tile0_done"], tile(l, "pool", g) + 1)
                        elif u == 0:
                            dve.wait_ge(sem["pool_tile1"], l * 2 + s + 1)
                        else:
                            dve.wait_ge(sem["units_done"], unit(l, "pool", s) + 3)
                        V.scalar_tensor_tensor(mg[:, n, :], bank[t][:, :], pcol[:, bass.ds(l * NROWS + (R_PSC + n), 1)], rb[:, :],
                                               ALU.mult, ALU.mult).then_inc(bank_free[t], 1)
                        dve.drain().then_inc(sem["pool_out"], 1)
                return evac

            def out_mqk(l, name, i, j):
                return scaled_out(l, name, i, lambda s, t: flat(mqk[:, bass.ds(i * 2 + s, 1), j + t, :]), "dve_out")

            def out_gate(l, name, i):
                return scaled_out(l, name, i, lambda s, t: flat(gate[:, bass.ds(i * 4 + (2 * s + t), 1), :]), "gate_out")

            def attention_step(l, name, i, h, evac=None, tail=True):
                def before0():
                    attn_rope(l, h)

                def before1():
                    if tail:
                        attn_oss(l, h - 1)
                        attn_onorm(l, h - 1)

                def before2():
                    for qb in (0, 1):
                        attn_max(l, h, qb)
                    for qb in (0, 1):
                        attn_combine(l, h, qb)

                def before3():
                    if tail:
                        attn_olo(l, h - 1)
                    for qb in (2, 3):
                        attn_max(l, h, qb)
                    for qb in (2, 3):
                        attn_combine(l, h, qb)

                dense(l, name, i, evac, (before0, before1, before2, before3, None))

            with dve.Fori(0, DEPTH) as l:
                dense(l, "aq", 0, sum_squares(l, 0, 0), (lambda: norm_rstd(2 * l), None, None, None, None))
                V.tensor_scalar(lamt[:, 4:5], pcol[:, bass.ds(l * NROWS + R_GDH, 1)], kc[:, bass.ds(l * 2 + (K_LAM + 1), 1)], None, ALU.mult)
                dve.wait_ge(sem["small_loaded"], 48 * (l + 1))
                V.tensor_tensor(lamp[:, :, :], lams[:, 0:4:2, :], lams[:, 1:4:2, :], ALU.mult)
                dve.drain()
                V.tensor_reduce(lamt[:, 0:2], lamp[:, :, :], AX.X, ALU.add).then_inc(sem["lam_sum"], 1)
                cs = kc[:, K_COS:K_ALL].rearrange("p (b f d) -> p b f d", b=NB, f=2)
                h2 = DK // 2
                for a in range(2):
                    g = lambda lo: gqk[:, a, lo:lo + h2].unsqueeze(1).to_broadcast([P, NB, h2])
                    V.tensor_tensor(rope[:, 0, a, :, 0:h2], cs[:, :, 0, :], g(0), ALU.mult)
                    V.tensor_tensor(rope[:, 0, a, :, h2:DK], cs[:, :, 0, :], g(h2), ALU.mult)
                    V.scalar_tensor_tensor(rope[:, 1, a, :, 0:h2], cs[:, :, 1, :], -1.0, g(h2), ALU.mult, ALU.mult)
                    V.tensor_tensor(rope[:, 1, a, :, h2:DK], cs[:, :, 1, :], g(0), ALU.mult)
                dve.wait_ge(sem["if_hi"], l + 1)
                V.tensor_tensor(wif_lo[:, :, :], wif, wif_hi[:, :, :].bitcast(F32), ALU.subtract).then_inc(sem["if_split"], 1)
                dve.wait_ge(sem["lam_exp"], l + 1)
                V.tensor_tensor(lamt[:, 6:7], lamt[:, 3:4], lamt[:, 2:3], ALU.subtract)
                dve.drain()
                V.tensor_tensor(lamt[:, 5:6], lamt[:, 6:7], kc[:, bass.ds(l * 2 + K_LAM, 1)], ALU.subtract)
                dense(l, "aq", 1, sum_squares(l, 0, 1))
                with dve.Fori(0, 2) as i:
                    dense(l, "ak", i, sum_squares(l, 1, i))
                dve.drain()
                V.tensor_scalar(table["qst"][:, :], table["qst"][:, :], 1.0 / DK, EPS, ALU.mult, ALU.add).then_inc(sem["q_ss"], 1)
                dve.wait_ge(sem["if_done"], l + 1)
                V.tensor_tensor(ifn[:, :].rearrange("p (b c) -> p b c", b=NB), B[0][:, 0:NB * 8].rearrange("p (b c) -> p b c", b=NB),
                                st[:, 44:48].unsqueeze(2).to_broadcast([P, NB, 8]), ALU.mult).then_inc(sem["ifn_done"], 1)
                with dve.Fori(0, 2) as i:
                    dense(l, "pu", i, out_pu(l, i))
                dense(l, "pool", 0, out_pool(l), kn=4)
                dense(l, "av", 0, None)
                attention_step(l, "av", 1, 0, tail=False)
                with dve.Fori(0, 4) as i:
                    attention_step(l, "vo", i, i + 1)
                for i in range(2):
                    for done in (("v_spilled",), ("o_spilled0", "o_spilled1"))[i]:
                        wait_alone(dve, sem[done], 16 * (l + 1))
                    attention_step(l, "mq", i, i + 5, out_mqk(l, "mq", i, 0))
                attention_step(l, "mk", 0, 7, out_mqk(l, "mk", 0, 2))

                def rows_scan():
                    dve.wait_ge(sem["row_log"], l + 1)
                    r = slice(0, MH)
                    V.scalar_tensor_tensor(row_u[r, :], row_b[r, :], 0.0, row_t[r, :], ALU.min, ALU.subtract)
                    dve.drain()
                    for c in range(NB):
                        k = slice(c * P, (c + 1) * P)
                        V.tensor_tensor_scan(row_b[r, k], ones[r, :], row_u[r, k], 0.0, ALU.mult, ALU.add)
                    dve.drain()
                    V.tensor_tensor(row_i[r, :], row_i[r, :], row_b[r, :], ALU.subtract)
                    V.memset(row_t[r, 0:P], 0.0)
                    dve.drain()

                def rows_maxima():
                    r = slice(0, MH)
                    for c in range(NB):
                        k = slice(c * P, (c + 1) * P)
                        first = NEG_BIG if c == 0 else mp[r, c:c + 1]
                        V.tensor_tensor_scan(row_m[r, k], row_t[r, 0:P], row_i[r, k], first, ALU.add, ALU.max)
                        V.tensor_copy(row_a[r, (pair_off(c) + c) * P:pair_off(c + 1) * P], row_i[r, k])
                        dve.drain()
                        if c < NB - 1:
                            end = (c + 1) * P - 1
                            V.tensor_tensor(mp[r, c + 1:c + 2], row_m[r, end:end + 1], row_b[r, end:end + 1], ALU.add)
                            V.tensor_scalar(row_a[r, pair_off(c + 1) * P:(pair_off(c + 1) + c + 1) * P],
                                            row_a[r, pair_off(c) * P:pair_off(c + 1) * P], row_b[r, end:end + 1], None, ALU.add)
                            dve.drain()
                    V.tensor_tensor(row_u[r, :], row_b[r, :], row_m[r, :], ALU.add).then_inc(sem["row_ready"], 1)

                def rows_cols():
                    dve.wait_ge(sem["row_t2"], l + 1)
                    V.tensor_copy(ac[:, :], B[1][:, 0:40]).then_inc(sem["row_cols"], 1)

                dense(l, "mk", 1, out_mqk(l, "mk", 1, 2), (None, lambda: (attn_oss(l, AH - 1), attn_onorm(l, AH - 1)), None, None, lambda: attn_olo(l, AH - 1)))

                def conv_hooks(h):
                    base = (l * MH + h) * 4
                    tile_k = lambda k: flat(mqk[:, bass.ds(h, 1), k, :])

                    def taps(k):
                        dve.wait_ge(sem["m_tap"], base + k + 1)
                        w = lambda tap: pcol[:, bass.ds(l * NROWS + h * 2 + (R_CONV + tap * 16 + (k // 2) * 8 + k % 2), 1)]
                        for r in range(1, 4):
                            if r > 1:
                                dve.drain()
                            ins = V.scalar_tensor_tensor(cv[:, k % 3, r:S], tile_k(k)[:, 0:S - r], w(3 - r), cv[:, k % 3, r:S], ALU.mult, ALU.add)
                        ins.then_inc(sem["m_conv"], 1)

                    def silu(k):
                        dve.wait_ge(sem["m_th"], base + k + 1)
                        V.scalar_tensor_tensor(tile_k(k), th[:, :], 1.0, cv[:, k % 3, :], ALU.add, ALU.mult).then_inc(sem["m_c"], 1)

                    return [lambda: (taps(0), taps(1)), lambda: (silu(0), taps(2)), lambda: (silu(1), taps(3)), lambda: (silu(2), silu(3))]

                dense(l, "ga", 0, out_gate(l, "ga", 0), conv_hooks(0) + [None])
                dense(l, "ga", 1, out_gate(l, "ga", 1), (rows_scan, None, rows_maxima, None, rows_cols))

                def evac_wd(i):
                    def evac(s, t):
                        tile_wait(dve, l, "wd", 2 * i + s, t)
                        g = flat(gate[:, bass.ds(i * 4 + (2 * s + t), 1), :])
                        V.scalar_tensor_tensor(g, g, 1.0, bank[t][:, :], ALU.add, ALU.mult).then_inc(bank_free[t], 1)
                    return evac

                wait_alone(dve, sem["gate_done"], (2 * l + 1) * KT)
                with dve.Fori(0, 2) as i:
                    dense(l, "wd", i, evac_wd(i), conv_hooks(i + 1) + [None])

                def evac_gp(i):
                    def evac(s, t):
                        n = 4 * i + 2 * s + t
                        if n >= 1:
                            join(n - 1)
                        tile_wait(dve, l, "gp", 2 * i + s, t)
                        V.tensor_tensor(tg[:, t, :], bank[t][:, :], rb[:, :], ALU.mult).then_inc(bank_free[t], 1)
                        dve.drain().then_inc(sem["tg_out"], 1)
                    return evac

                def join(n):
                    dve.wait_ge(sem["pooled"], l * 4 + n // 2 + 1)
                    dve.wait_ge(sem["tg_done"], l * KT + n + 1)
                    V.scalar_tensor_tensor(mg[:, n, :], tg[:, n % 2, :], 1.0, mg[:, n, :], ALU.add, ALU.mult)
                    dve.drain()
                    V.tensor_tensor(mg[:, n, :], mg[:, n, :], gate[:, n, :], ALU.add)

                def m_mask(h):
                    dve.wait_ge(sem["m_mb"], l * MH + h + 1)
                    V.tensor_tensor(mdiag[:, :, :], B[3][:, :].rearrange("p (b j) -> p b j", b=NB),
                                    big.unsqueeze(1).to_broadcast([P, NB, P]), ALU.add).then_inc(sem["m_diag"], 1)

                def m_weigh(h):
                    hd = l * MH + h + 1
                    dve.wait_ge(sem["m_s"], hd)
                    dve.wait_ge(sem["m_decay"], hd + 1)
                    where = ((0, 0), (1, 0), (2, 0), (1, 3 * P))
                    for sc in range(NB):
                        n = (NB - sc) * P
                        b, o = where[sc]
                        d = decay[:, row_off(sc):row_off(sc) + n]
                        ins = V.scalar_tensor_tensor(d, B[b][:, o:o + n], MDH ** -0.5 / 4, d, ALU.mult, ALU.mult)
                    ins.then_inc(sem["m_sp"], 1)

                def m_norm(h):
                    hd = l * MH + h + 1
                    dve.wait_ge(sem["m_num"], hd + 1)
                    dve.wait_ge(sem["m_tanh"], hd)
                    den, neg, rec = st_s[:, 32:36], st_s[:, 36:40], st_s[:, 40:44]
                    V.tensor_copy(den, B[2][:, 0:NB])
                    for b in range(2):
                        V.scalar_tensor_tensor(hn[:, 2 * b:2 * b + 2, :].rearrange("p b c -> p (b c)"),
                                               moh[:, h % 2, 2 * b:2 * b + 2, :].rearrange("p b c -> p (b c)"), 1.0,
                                               B[b][:, :], ALU.add, ALU.mult)
                    dve.drain()
                    V.scalar_tensor_tensor(neg, den, -1.0, den, ALU.mult, ALU.max)
                    dve.drain()
                    floor = emt[:, :].rearrange("p (b h) -> p b h", h=MH)[:, :, h]
                    V.tensor_tensor(den, neg, floor, ALU.max)
                    dve.drain()
                    V.reciprocal(rec, den)
                    dve.drain()
                    for b in range(NB):
                        ins = V.tensor_scalar(hn[:, b, :], hn[:, b, :], rec[:, b:b + 1], None, ALU.mult)
                    ins.then_inc(sem["m_hn"], 1)

                def m_lo(h):
                    hd = l * MH + h + 1
                    dve.wait_ge(sem["m_hi"], 2 * hd)
                    for v in range(2):
                        ins = V.scalar_tensor_tensor(hm_sp[:, h, 2 + v, :], B[4 + v][:, :], 0.5,
                                                     hm_sp[:, h, v, :].bitcast(F32), ALU.mult, ALU.subtract)
                    ins.then_inc(sem["m_lo"], 1)

                wait_alone(dve, sem["units_done"], unit(l, "wd", 4) + 2)
                for h, (name, i, evac) in enumerate((("gp", 0, evac_gp(0)), ("gp", 1, evac_gp(1)),
                                                     ("gm", 0, out_gate(l, "gm", 0)), ("gm", 1, out_gate(l, "gm", 1)))):
                    conv = conv_hooks(MH - 1) if h == 0 else [lambda: None] * 4
                    dense(l, name, i, evac, (lambda: (m_mask(h), conv[0]()), lambda: (m_weigh(h), conv[1]()),
                                             lambda: (m_norm(h), conv[2]()), conv[3], lambda: m_lo(h)))
                    if h == 1:
                        join(KT - 1)
                        dve.drain()

                def evac_wm(i):
                    def evac(s, t):
                        tile_wait(dve, l, "wm", 2 * i + s, t)
                        n = i * 4 + (2 * s + t)
                        V.scalar_tensor_tensor(ytmp[:, t, :], flat(gate[:, bass.ds(n, 1), :]), 1.0, bank[t][:, :], ALU.add, ALU.mult).then_inc(bank_free[t], 1)
                        dve.drain()
                        m = flat(mg[:, bass.ds(n, 1), :])
                        V.tensor_tensor(m, m, ytmp[:, t, :], ALU.add).then_inc(sem["merged_val"], 1)
                        dve.wait_ge(sem["merged_hi_done"], l * KT + n + 1)
                        V.scalar_tensor_tensor(flat(merged_lo[:, bass.ds(n, 1), :]), m, 0.5, flat(merged_hi[:, bass.ds(n, 1), :]).bitcast(F32),
                                               ALU.mult, ALU.subtract).then_inc(sem["merged_lo_done"], 1)
                    return evac

                wait_alone(dve, sem["gate_done"], (2 * l + 2) * KT)
                with dve.Fori(0, 2) as i:
                    dense(l, "wm", i, evac_wm(i))

                def evac_wo(i):
                    def evac(s, t):
                        tile_wait(dve, l, "wo", 2 * i + s, t)
                        k = i * 4 + (2 * s + t)
                        xk = flat(xt[:, bass.ds(k, 1), :])
                        V.tensor_tensor(xk, xk, bank[t][:, :], ALU.add).then_inc(bank_free[t], 1)
                        dve.drain().then_inc(sem["xt_tile"], 1)
                        stream_lo(2 * l + 1, k, l * NROWS + R_GFFN)
                    return evac

                wait_alone(dve, sem["xt_back"], 16 * (l + 1))
                with dve.Fori(0, 2) as i:
                    dense(l, "wo", i, evac_wo(i))

                def evac_gu(i):
                    def evac(s, t):
                        n = l * (2 * FF // UC) + 2 * i + t
                        tile_wait(dve, l, "gu", 2 * i + s, t)
                        if s == 0:
                            V.tensor_tensor(glu[:, t, :], bank[t][:, :], rb[:, :], ALU.mult).then_inc(bank_free[t], 1)
                            dve.drain().then_inc(sem["glu_in"], 1)
                        else:
                            V.scalar_tensor_tensor(glu_up[:, t, :], bank[t][:, :], 0.5, rb[:, :], ALU.mult, ALU.mult).then_inc(bank_free[t], 1)
                            dve.wait_ge(sem["glu_t"], n + 1)
                            V.scalar_tensor_tensor(glu[:, t, :], gate_t[:, t, :], 1.0, glu[:, t, :], ALU.add, ALU.mult)
                            dve.drain()
                            V.tensor_tensor(glu[:, t, :], glu[:, t, :], glu_up[:, t, :], ALU.mult)
                            dve.drain().then_inc(sem["glu_v"], 1)
                            dve.wait_ge(sem["act_hi_done"], n + 1)
                            V.tensor_tensor(flat(act_lo[:, bass.ds(i * 2 + t, 1), :]), glu[:, t, :], flat(act_hi[:, bass.ds(i * 2 + t, 1), :]).bitcast(F32),
                                            ALU.subtract).then_inc(sem["act_lo_done"], 1)
                    return evac

                dense(l, "gu", 0, evac_gu(0), (lambda: norm_rstd(2 * l + 1), None, None, None, None))
                with dve.Fori(1, FF // UC) as i:
                    dense(l, "gu", i, evac_gu(i))

                for i in range(6):
                    def evac_dn(s, t):
                        j = 2 * i + s
                        if j % 3 == 2:
                            tile_wait(dve, l, "dn", j, t)
                            n = 2 * (j // 3) + t
                            V.tensor_tensor(xt[:, n, :], xt[:, n, :], bank[t][:, :], ALU.add).then_inc(bank_free[t], 1)
                            dve.drain().then_inc(sem["xt_tile"], 1)
                            stream_lo(2 * l + 2, n, (l + 1) * NROWS + R_GMIX)
                    dense(l, "dn", i, evac_dn, kn=DOWN_K[(2 * i + 1) % 3][1], last_kn=DOWN_K[(2 * i + 2) % 3][1] if i < 5 else KT)

            for b in range(NB):
                for c in range(2):
                    n = 2 * b + c
                    dve.wait_ge(sem["fin_t"], n + 1)
                    V.tensor_copy(xnat[:, b, c * S:(c + 1) * S], B[n % 2][:, :]).then_inc(sem["fin_sb"], 1)

        @block.tensor
        def _(pe):
            mm, tr = nc.tensor.matmul, nc.tensor.transpose

            def dense(l, name, i, natural, a_hi, a_lo, kn=KT, hooks=None, first_k=None):
                hooks = hooks or {}

                def before_k(s, t, half, k):
                    if first_k and (s, t) == (0, 0) and not (natural and half):
                        first_k(k)

                for s in range(2):
                    pe.wait_ge(sem["split_done"], unit(l, name, 2 * i + s) + 3)
                    for t in range(2):
                        pe.wait_ge(bank_free[t], tile(l, name, 2 * i + s) + 1)
                        for half in range(2):
                            if 4 * s + 2 * t + half in hooks:
                                hooks[4 * s + 2 * t + half]()
                            if natural:
                                b = 2 * t + half
                                tok = slice(b * P, (b + 1) * P)
                                dst = bank[t][:, half * UC:(half + 1) * UC]
                                for k in range(kn):
                                    before_k(s, t, half, k)
                                    mm(dst, a_hi[:, k, tok], w_hi[s][:, k, :], start=k == 0, stop=False)
                                    mm(dst, a_hi[:, k, tok], w_lo[s][:, k, :], start=False, stop=False)
                                    ins = mm(dst, a_lo[:, k, tok], w_hi[s][:, k, :], start=False, stop=k == kn - 1)
                            else:
                                col = slice(t * P, (t + 1) * P)
                                for k in range(half * kn // 2, (half + 1) * kn // 2):
                                    before_k(s, t, half, k)
                                    mm(bank[t][:, :], w_hi[s][:, k, col], a_hi(s, k), start=k == 0, stop=False)
                                    mm(bank[t][:, :], w_hi[s][:, k, col], a_lo(s, k), start=False, stop=False)
                                    ins = mm(bank[t][:, :], w_lo[s][:, k, col], a_hi(s, k), start=False, stop=k == kn - 1)
                        ins.then_inc((sem["tile0_done"], sem["units_done"])[t], 1)

            stream_hi, stream_lo = (lambda s, k: h_hi[:, k, :]), (lambda s, k: h_lo[:, k, :])

            def norm_ms(norm):
                pe.wait_ge(sem["sq_summed"], stream_tile(norm, KT) + 2)
                for b in range(NB):
                    ins = mm(B[0][:, b:b + 1], sqsum[:, b * P:(b + 1) * P], ones[:, 0:1], start=True, stop=True)
                ins.then_inc(sem["ms_done"], 1)

            def norm_spread(norm):
                pe.wait_ge(sem["diag_done"], norm + 1)
                mm(B[1][:, :], ones, diag[:, :, :].rearrange("p b j -> p (b j)"), start=True, stop=True).then_inc(sem["rb_done"], 1)

            def first_pair(l, name, natural, a_hi, a_lo, norm):
                dense(l, name, 0, natural, a_hi, a_lo, hooks={2: lambda: norm_ms(norm), 3: lambda: norm_spread(norm)},
                      first_k=lambda k: pe.wait_ge(sem["hlo_done"], stream_tile(norm, k) + 1))

            def attn_tqk(l, h):
                pe.wait_ge(sem["q_roped"], l * AH + h + 1)
                src = e1[:, :, :].rearrange("p a (b d) -> p a b d", b=NB)
                for a in range(2):
                    for b in range(NB):
                        ins = tr(B[4 + a][:, b * P:(b + 1) * P], src[:, a, b, :], ident)
                ins.then_inc(sem["q_t"], 1)

            def attn_scores(l, h, qb):
                if qb == 0:
                    pe.wait_ge(sem["q_tsb"], (l * AH + h + 1) * 2)
                    pe.wait_ge(sem["s_exp"], (l * AH + h) * 8 + 1)
                    pe.wait_ge(sem["o_norm"], l * AH + h + 1)
                elif qb >= 2:
                    pe.wait_ge(sem["s_exp"], (l * AH + h) * 8 + 2 * (qb - 1) + 1)
                n = (qb + 1) * P
                for c in range(2):
                    r = slice(c * DK, (c + 1) * DK)
                    ins = mm(B[2 * (qb % 2) + c][:, 0:n], qk_t[r, 0, qb * P:n], qk_t[r, 1, 0:n], start=True, stop=True)
                ins.then_inc(sem["s_done"], 1)

            def attn_tprobs(l, h, qbs):
                for qb in qbs:
                    pe.wait_ge(sem["s_comb"], (l * AH + h) * 4 + qb + 1)
                    if qb == 1:
                        pe.wait_ge(sem["o_lo"], l * AH + h + 1)
                    if qb >= 2:
                        pe.wait_ge(sem["a_tsb"], (l * AH + h) * 4 + qb - 1)
                    for kb in range(qb + 1):
                        o = (pair_off(qb) + kb) * P
                        ins = tr(B[4 + qb % 2][:, kb * P:(kb + 1) * P], probs[:, o:o + P], ident)
                    ins.then_inc(sem["a_t"], 1)

            def attn_values(l, h):
                pe.wait_ge(sem["a_tsb"], (l * AH + h) * 4 + 4)
                pe.wait_ge(sem["aev"], read_out(l, "av", 4))
                for qb in range(NB):
                    for kb in range(qb + 1):
                        o = (pair_off(qb) + kb) * P
                        ins = mm(B[0][:, qb * P:(qb + 1) * P], probs_t[:, o:o + P],
                                 av[:, kb, bass.ds(h * P, P)], start=kb == 0, stop=kb == qb)
                ins.then_inc(sem["o_done"], 1)

            def attn_tout(l, h):
                pe.wait_ge(sem["o_norm"], l * AH + h + 1 + 1)
                for b in range(NB):
                    ins = tr(B[5][:, b * P:(b + 1) * P], osq[:, b, :], ident)
                ins.then_inc(sem["o_t"], 1)

            def attn_hooks(l, h, tail=True):
                hooks = {4: lambda: attn_tqk(l, h), 5: lambda: (attn_scores(l, h, 0), attn_scores(l, h, 1)),
                         7: lambda: (attn_scores(l, h, 2), attn_scores(l, h, 3))}
                if tail:
                    hooks[0] = lambda: attn_tprobs(l, h - 1, (0, 1))
                    hooks[2] = lambda: attn_tprobs(l, h - 1, (2, 3))
                    hooks[3] = lambda: attn_values(l, h - 1)
                    hooks[6] = lambda: (attn_tout(l, h - 1))
                return hooks

            pe.wait_ge(sem["const_loaded"], 16)
            pe.wait_ge(sem["prow_loaded"], 80 * DEPTH)
            for lay in range(DEPTH):
                ins = tr(B[2][:, lay * NROWS:(lay + 1) * NROWS], prow[0:NROWS, lay, :], ident[0:NROWS, 0:NROWS])
            ins.then_inc(sem["prow_t"], 1)
            pe.wait_ge(sem["x_loaded"], 16)
            for k in range(KT):
                if k >= 2:
                    pe.wait_ge(sem["xt_tile"], k - 1)
                for b in range(NB):
                    ins = tr(B[k % 2][:, b * P:(b + 1) * P], xnat[:, b, k * P:(k + 1) * P], ident)
                ins.then_inc(sem["xt_in_t"], 1)

            with pe.Fori(0, DEPTH) as l:
                first_pair(l, "aq", True, h_hi, h_lo, 2 * l)
                dense(l, "aq", 1, True, h_hi, h_lo)
                with pe.Fori(0, 2) as i:
                    dense(l, "ak", i, True, h_hi, h_lo)
                pe.wait_ge(sem["if_split"], l + 1)
                for b in range(NB):
                    tok = slice(b * P, (b + 1) * P)
                    dst = B[0][:, b * 8:(b + 1) * 8]
                    for k in range(KT):
                        mm(dst, h_hi[:, k, tok], wif_hi[:, k, :], start=k == 0, stop=False)
                        mm(dst, h_hi[:, k, tok], wif_lo[:, k, :], start=False, stop=False)
                        ins = mm(dst, h_lo[:, k, tok], wif_hi[:, k, :], start=False, stop=k == KT - 1)
                ins.then_inc(sem["if_done"], 1)
                with pe.Fori(0, 2) as i:
                    dense(l, "pu", i, False, stream_hi, stream_lo)
                for g in range(4):
                    s, u = g // 2, g % 2
                    if u == 0:
                        pe.wait_ge(sem["split_done"], unit(l, "pool", s) + 3)
                    pe.wait_ge(sem["p_lo"], l * KT + 2 * g + 2)
                    for t in range(2):
                        pe.wait_ge(bank_free[t], tile(l, "pool", g) + 1)
                        col = slice(t * P, (t + 1) * P)
                        for k in range(2):
                            mm(bank[t][:, :], w_hi[s][:, 2 * u + k, col], p_hi[:, 2 * g + k, :], start=k == 0, stop=False)
                            mm(bank[t][:, :], w_hi[s][:, 2 * u + k, col], p_lo[:, 2 * g + k, :], start=False, stop=False)
                            ins = mm(bank[t][:, :], w_lo[s][:, 2 * u + k, col], p_hi[:, 2 * g + k, :], start=False, stop=k == 1)
                        ins.then_inc(sem["tile0_done" if t == 0 else "units_done" if u else "pool_tile1"], 1)
                dense(l, "av", 0, True, h_hi, h_lo)
                dense(l, "av", 1, True, h_hi, h_lo, hooks=attn_hooks(l, 0, tail=False))
                with pe.Fori(0, 4) as i:
                    dense(l, "vo", i, True, h_hi, h_lo, hooks=attn_hooks(l, i + 1))
                with pe.Fori(0, 2) as i:
                    dense(l, "mq", i, False, stream_hi, stream_lo, hooks=attn_hooks(l, i + 5))
                dense(l, "mk", 0, False, stream_hi, stream_lo, hooks=attn_hooks(l, 7))

                def rows_in():
                    wait_alone(pe, sem["ifn_done"], l + 1)
                    wait_alone(pe, sem["o_norm"], l * AH + AH + 1)
                    for a in range(2):
                        for b in range(NB):
                            ins = tr(B[a][0:MH, b * P:(b + 1) * P], ifn[:, b * 8 + a * MH:b * 8 + (a + 1) * MH], ident)
                    ins.then_inc(sem["row_t1"], 1)

                def rows_out():
                    wait_alone(pe, sem["row_ready"], l + 1)
                    for b in range(NB):
                        tr(B[0][:, b * MH:(b + 1) * MH], row_u[0:MH, b * P:(b + 1) * P], ident[0:MH, 0:MH])
                    for n in range(10):
                        ins = tr(B[1][:, n * MH:(n + 1) * MH], row_a[0:MH, n * P:(n + 1) * P], ident[0:MH, 0:MH])
                    ins.then_inc(sem["row_t2"], 1)

                last = AH - 1
                dense(l, "mk", 1, False, stream_hi, stream_lo, hooks={
                    0: lambda: attn_tprobs(l, last, (0, 1)), 2: lambda: attn_tprobs(l, last, (2, 3)),
                    3: lambda: attn_values(l, last), 5: lambda: attn_tout(l, last), 6: rows_in})
                dense(l, "ga", 0, False, stream_hi, stream_lo)
                dense(l, "ga", 1, False, stream_hi, stream_lo, hooks={7: rows_out})
                wait_alone(pe, sem["o_lo"], l * AH + AH + 1)
                with pe.Fori(0, 2) as i:
                    dense(l, "wd", i, False, lambda s, k: o_sp[:, k, 0, :], lambda s, k: o_sp[:, k, 1, :])

                def m_spread(h):
                    pe.wait_ge(sem["m_sel"], 1)
                    if h == 0:
                        pe.wait_ge(sem["row_cols"], l + 1)
                    pe.wait_ge(sem["m_decay"], l * MH + h + 1)
                    mm(B[3][:, :], selh[0:MH, h, :], row_m[0:MH, :], start=True, stop=True).then_inc(sem["m_mb"], 1)

                def m_scores(h):
                    pe.wait_ge(sem["m_c"], (l * MH + h + 1) * 4 + 1)
                    for sc in range(NB):
                        b, o = ((0, 0), (1, 0), (2, 0), (1, 3 * P))[sc]
                        n = (NB - sc) * P
                        for k in range(2):
                            ins = mm(B[b][:, o:o + n], mqk[:, h, 2 + k, sc * P:(sc + 1) * P], mqk[:, h, k, sc * P:S], start=k == 0, stop=k == 1)
                    ins.then_inc(sem["m_s"], 1)

                def m_values(h):
                    hd = l * MH + h + 1
                    pe.wait_ge(sem["m_sp"], hd)
                    pe.wait_ge(sem[f"m_vo{h % 2}"], (l * 2 + h // 2 + 1) * 32)
                    for jc in range(NB):
                        for sc in range(jc + 1):
                            o = row_off(sc) + (jc - sc) * P
                            w = decay[:, o:o + P]
                            mm(B[jc // 2][:, (jc % 2) * MDH:(jc % 2 + 1) * MDH], w, mvh[:, h % 2, sc, :], start=sc == 0, stop=sc == jc)
                            ins = mm(B[2][:, jc:jc + 1], w, ones[:, 0:1], start=sc == 0, stop=sc == jc)
                    ins.then_inc(sem["m_num"], 1)

                def m_turn(h):
                    pe.wait_ge(sem["m_hn"], l * MH + h + 1)
                    pe.wait_ge(sem["m_lo"], l * MH + h + 1)
                    for v in range(2):
                        for b in range(NB):
                            ins = tr(B[4 + v][:, b * P:(b + 1) * P], hn[:, b, v * P:(v + 1) * P], ident)
                    ins.then_inc(sem["m_ht"], 1)

                for h, (name, i) in enumerate((("gp", 0), ("gp", 1), ("gm", 0), ("gm", 1))):
                    dense(l, name, i, False, stream_hi, stream_lo, hooks={
                        0: lambda: m_spread(h), 2: lambda: m_scores(h), 5: lambda: m_values(h), 7: lambda: m_turn(h)})
                hm_hi = lambda s, k: hm_sp[:, k // 2, k % 2, :]
                hm_lo = lambda s, k: hm_sp[:, k // 2, 2 + k % 2, :]
                for i in range(2):
                    dense(l, "wm", i, False, hm_hi, hm_lo, first_k=None if i else
                          lambda k: pe.wait_ge(sem["m_lo"], l * MH + k // 2 + 1 + 1))
                for i in range(2):
                    dense(l, "wo", i, False, lambda s, k: merged_hi[:, k, :], lambda s, k: merged_lo[:, k, :], first_k=None if i else
                          lambda k: pe.wait_ge(sem["merged_lo_done"], l * KT + k + 1))
                first_pair(l, "gu", False, stream_hi, stream_lo, 2 * l + 1)
                with pe.Fori(1, FF // UC) as i:
                    dense(l, "gu", i, False, stream_hi, stream_lo)
                for j in range(12):
                    s = j % 2
                    k0, kn = DOWN_K[j % 3]
                    pe.wait_ge(sem["split_done"], unit(l, "dn", j) + 3)
                    for t in range(2):
                        if j % 3 == 0:
                            pe.wait_ge(bank_free[t], tile(l, "dn", j // 3) + 1)
                        col = slice(t * P, (t + 1) * P)
                        for k in range(kn):
                            if j < 3 and t == 0:
                                pe.wait_ge(sem["act_lo_done"], l * FT + k0 + k + 1 + 1)
                            mm(bank[t][:, :], w_hi[s][:, k, col], act_hi[:, k0 + k, :], start=k0 + k == 0, stop=False)
                            mm(bank[t][:, :], w_hi[s][:, k, col], act_lo[:, k0 + k, :], start=False, stop=False)
                            ins = mm(bank[t][:, :], w_lo[s][:, k, col], act_hi[:, k0 + k, :], start=False, stop=k0 + k == FT - 1)
                        if t == 1:
                            ins.then_inc(sem["units_done"], 1)
                        elif j % 3 == 2:
                            ins.then_inc(sem["tile0_done"], 1)

            pe.wait_ge(sem["xt_tile"], 8 + 16 * DEPTH)
            for b in range(NB):
                for c in range(2):
                    n = 2 * b + c
                    if n >= 2:
                        pe.wait_ge(sem["fin_sb"], n - 1)
                    for k in range(4):
                        ins = tr(B[n % 2][:, k * P:(k + 1) * P], xt[:, 4 * c + k, b * P:(b + 1) * P], ident)
                    ins.then_inc(sem["fin_t"], 1)


_INS = ["x", "g_mix", "w_in", "b_if", "conv_qk", "w_m_out", "w_pool", "pool_scale", "g_qk", "lam_p", "g_diff_head",
        "w_diff_out", "w_out", "g_ffn", "w_gate_up", "w_down"]


def shape_constants():
    import math
    import numpy as np

    c = np.zeros((P, K_ALL), np.float32)
    i = np.arange(P)
    c[:, K_ID:K_ID + P] = np.eye(P)
    c[:, K_MASK:K_MASK + P] = np.where(i[None, :] > i[:, None], NEG_BIG, 0.0)
    c[:, K_BIG:K_BIG + P] = np.where(i[:, None] > i[None, :], -NEG_BIG, 0.0)
    c[:, K_ONE:K_ONE + P] = 1.0
    c[:MH, K_HOT:K_HOT + MH] = np.eye(MH)
    c[:, K_CNT:K_CNT + 16] = 1.0 / np.arange(1, 17)
    for layer in range(DEPTH):
        lam_init = 0.8 - 0.6 * math.exp(-0.3 * layer)
        c[:, K_LAM + 2 * layer] = lam_init
        c[:, K_LAM + 2 * layer + 1] = 1.0 - lam_init
    half = DK // 2
    inv = np.power(np.float32(10000.0), -np.arange(half, dtype=np.float32) / np.float32(half), dtype=np.float32)
    ang = np.arange(S, dtype=np.float32)[:, None] * inv[None, :]
    cs = np.stack([np.cos(ang), np.sin(ang)], 1).astype(np.float32)
    c[:, K_COS:] = cs.reshape(NB, P, 2 * half).transpose(1, 0, 2).reshape(P, -1)
    return c


def kernel(**inputs):
    import numpy as np
    import concourse.bacc as bacc
    from concourse.bass_utils import run_bass_kernel_spmd

    nc = bacc.Bacc("TRN2", target_bir_lowering=False, num_devices=1, dynamic_dma_scratch_size=8192)
    arrays = {f"in_{name}": np.ascontiguousarray(inputs[name]) for name in _INS}
    arrays["in_consts"] = shape_constants()
    args = [nc.dram_tensor(n, a.shape, mybir.dt.from_np(a.dtype), kind="ExternalInput").ap() for n, a in arrays.items()]
    out = nc.dram_tensor("out_0", (1, S, D), F32, kind="ExternalOutput").ap()
    build_trunk(nc, *args, out)
    result = run_bass_kernel_spmd(nc, [arrays], core_ids=[0])
    return result.results[0]["out_0"]
```

```python
import concourse.bass as bass
from concourse import mybir
from concourse.alu_op_type import AluOpType as ALU

F32 = mybir.dt.float32
F32R = mybir.dt.float32r
ACT = mybir.ActivationFunctionType
AX = mybir.AxisListType

P = 128
D = 1024
S = 512
DEPTH = 2
KT = D // P
NB = S // P
FF = 2816
FT = FF // P
UC = 256
MH, MDH = 4, 256
AH, DK = 8, 64
EPS = 1e-6
NEG_BIG = -1e30

C_MQ, C_MK, C_MV, C_IF, C_PU = 0, D, 2 * D, 4 * D, 4 * D + 2 * MH
C_AQ = C_PU + D
C_GM = C_AQ + 3 * D
C_GP, C_GA = C_GM + D, C_GM + 2 * D

SECTIONS = [("aq", 4, 4), ("ak", 4, 4), ("pu", 4, 4), ("pool", 2, 1), ("av", 4, 4), ("vo", 8, 8),
            ("mq", 4, 4), ("mk", 4, 4), ("ga", 4, 4), ("wd", 4, 4), ("gp", 4, 4), ("gm", 4, 4), ("wm", 4, 4), ("wo", 4, 4),
            ("gu", 2 * FF // UC, 2 * FF // UC), ("dn", 12, 4)]
UBASE, VBASE = {}, {}
UPL = VPL = 0
for _n, _u, _v in SECTIONS:
    UBASE[_n], VBASE[_n] = UPL, VPL
    UPL, VPL = UPL + _u, VPL + _v
NATURAL = {"aq": 0, "ak": 4, "av": 8, "vo": 12}
DOWN_K = ((0, 8), (8, 8), (16, 6))

R_GMIX, R_GFFN, R_PSC, R_CONV, R_GDH = 0, KT, 2 * KT, 3 * KT, 3 * KT + 64
NROWS = R_GDH + 1

K_ID, K_MASK, K_BIG, K_ONE, K_HOT, K_CNT, K_LAM, K_COS = 0, 128, 256, 384, 512, 516, 532, 536
K_ALL = K_COS + NB * 2 * (DK // 2)


def pair_off(jc):
    return jc * (jc + 1) // 2


def row_off(sc):
    return sum(NB - c for c in range(sc)) * P


def build_trunk(nc, x, g_mix, w_in, b_if, conv_qk, w_m_out, w_pool, pool_scale, g_qk, lam_p, g_diff_head,
                w_diff_out, w_out, g_ffn, w_gate_up, w_down, consts, out):
    base = (nc.sbuf_base + 31) // 32 * 32
    KB = 1024

    def at(name, offset, shape, dt=F32):
        return nc.alloc_sbuf_tensor_at(name, shape, dt, offset=base + offset)

    h_hi = at("h_hi", 0, [P, KT, S], F32R)
    h_lo = at("h_lo", 16 * KB, [P, KT, S], F32R)
    raw = [at(f"raw{s}", (32 + 8 * s) * KB, [P, KT, UC]) for s in range(2)]
    w_hi = [at(f"w_hi{s}", (48 + 8 * s) * KB, [P, KT, UC], F32R) for s in range(2)]
    w_lo = [at(f"w_lo{s}", (64 + 8 * s) * KB, [P, KT, UC], F32R) for s in range(2)]
    Z1, Z2, Z3, Z4, ZT = 80 * KB, 112 * KB, 144 * KB, 160 * KB, 176 * KB
    qkn = at("qkn", Z1, [P, AH, 2, NB, P])
    o_sp = at("o_sp", Z1, [P, AH, 2, S], F32R)
    merged_hi = at("merged_hi", Z1, [P, KT, S], F32R)
    merged_lo = at("merged_lo", Z1 + 16 * KB, [P, KT, S], F32R)
    xnat = at("xnat", Z1, [P, NB, D])
    vo = at("vo", Z2, [P, 2 * MH, NB, UC])
    p_hi = at("p_hi", Z2, [P, KT, S], F32R)
    p_lo = at("p_lo", Z2 + 16 * KB, [P, KT, S], F32R)
    mqk = at("mqk", Z2, [P, MH, 4, S])
    hm_sp = at("hm_sp", Z2, [P, MH, 4, S], F32R)
    av = at("av", Z3, [P, NB, D])
    gate = at("gate", Z3, [P, KT, S])
    mg = at("mg", Z4, [P, KT, S])
    act_hi = at("act_hi", Z1, [P, FT, S], F32R)
    act_lo = at("act_lo", Z1 + 44 * KB, [P, FT, S], F32R)
    xt = at("xt", ZT, [P, KT, S])
    glu = at("glu", ZT + 16 * KB, [P, 2, S])
    diag = at("diag", ZT + 16 * KB, [P, NB, P])
    sqt = at("sqt", Z4 + 8 * KB, [P, 2, S])
    sqsum = at("sqsum", ZT + 20 * KB, [P, S])
    prow = at("prow", Z3, [P, DEPTH, P])
    tg = at("tg", ZT + 16 * KB, [P, 2, S])
    gate_t = at("gate_t", Z4 + 8 * KB, [P, 2, S])
    glu_up = at("glu_up", Z4 + 12 * KB, [P, 2, S])
    e0 = at("e0", ZT, [P, 2, S])
    e1 = at("e1", ZT + 4 * KB, [P, 2, S])
    qk_hi = at("qk_hi", ZT + 8 * KB, [P, 2, S], F32R)
    probs = at("probs", ZT + 12 * KB, [P, 10 * P])
    probs_t = at("probs_t", ZT + 17 * KB, [P, 10 * P])
    osq = at("osq", ZT + 17 * KB, [P, NB, P])
    cv = at("cv", ZT + 8 * KB, [P, 3, S])
    th = at("th", ZT + 14 * KB, [P, S])
    mvh = at("mvh", Z1, [P, 2, NB, MDH + 1])
    moh = at("moh", Z1 + 9 * KB, [P, 2, NB, MDH])
    decay = at("decay", Z1 + 17 * KB, [P, 10 * P])
    hn = at("hn", Z1 + 22 * KB, [P, NB, MDH])
    mdiag = at("mdiag", Z1 + 26 * KB, [P, NB, P])
    qsq = at("qsq", Z3, [P, 2, S])
    pa = at("pa", Z2 + 16 * KB, [P, 2, S])
    pb = at("pb", Z2 + 20 * KB, [P, 2, S])
    ytmp = at("ytmp", ZT + 16 * KB, [P, 2, S])
    row_i = at("row_i", ZT, [P, S])
    row_b = at("row_b", ZT + 2 * KB, [P, S])
    row_t = at("row_t", ZT + 4 * KB, [P, S])
    row_u = at("row_u", ZT + 6 * KB, [P, S])
    row_a = at("row_a", ZT + 16 * KB, [P, 10 * P])
    off = ZT + 22 * KB
    table = {}
    for name, cols in (("kc", K_ALL), ("rope", 2 * 2 * NB * DK), ("pcol", DEPTH * NROWS + KT), ("rb", S),
                       ("ac", 40), ("emt", 4 * MH), ("if_rows", S), ("lamt", 8), ("qst", AH * 16),
                       ("bif", 2), ("st", 48), ("st_s", 48), ("mx2", 24), ("mp", 8)):
        table[name] = at(name, off, [P, cols])
        if name == "rope":
            rope_at = off
        off += (4 * cols + 31) // 32 * 32
    wif_hi = at("wif_hi", off, [P, KT, 8], F32R)
    wif_lo = at("wif_lo", off + 32 * KT, [P, KT, 8], F32R)
    off += 64 * KT
    qk_lo = at("qk_lo", off, [P, 2, S], F32R)
    off += 4 * KB
    assert base + off <= nc.sbuf_usable_end, (base + off, nc.sbuf_usable_end)
    kc, pcol, rb, ac, emt, if_rows, lamt, bif, st, st_s, mx2, mp = (
        table[n] for n in ("kc", "pcol", "rb", "ac", "emt", "if_rows", "lamt", "bif", "st", "st_s", "mx2", "mp"))
    row_m = at("row_m", rope_at, [P, S])
    selh = at("selh", rope_at + 2 * KB, [P, MH, P])
    rope = table["rope"][:].rearrange("p (f a b d) -> p f a b d", f=2, a=2, b=NB)
    qst = table["qst"][:].rearrange("p (h a b c) -> p h a b c", h=AH, a=2, b=NB)
    gqk = at("gqk", Z4 + 12 * KB, [P, 2, DK])
    lams = at("lams", Z4 + 13 * KB, [P, 4, DK])
    lamp = at("lamp", Z4 + 14 * KB, [P, 2, DK])
    wif = at("wif", Z4 + 15 * KB, [P, KT, 2 * MH])[:, :, :]
    ident = kc[:, K_ID:K_ID + P]
    causal = kc[:, K_MASK:K_MASK + P]
    big = kc[:, K_BIG:K_BIG + P]
    ones = kc[:, K_ONE:K_ONE + P]

    bank = [nc.alloc_psum_tensor(f"dense{t}", [P, S], F32) for t in range(2)]
    B = [nc.alloc_psum_tensor(f"side{t}", [P, S], F32) for t in range(6)]

    xt_dram = nc.dram_tensor("xt_spill", [P, KT * S], F32, kind="Internal").ap()
    vo_dram = nc.dram_tensor("vo_spill", [P, 2 * MH, NB * UC], F32, kind="Internal").ap()

    sem_names = """raw_ready0 raw_ready1 hi_ready split_done units_done tile0_done
        bank_free0 bank_free1 const_loaded x_loaded0 x_loaded1 x_half x_half_hi x_half_sq x_half_sum xt_in_t xt_tile gate_out tg_out glu_in sq_done sq_summed ms_done ms_sb rstd_done diag_done
        rb_done hhi_done hlo_half hlo_done prow_loaded prow_t dve_out small_loaded lam_sum lam_exp
        if_loaded if_hi if_split if_done if_rows_done spilled xt_back aev q_sq q_red q_ss q_normed q_roped q_t q_hi q_lo s_done s_max s_exp
        s_comb a_t a_tsb o_done o_sq o_ss o_rstd o_norm o_t o_hi o_lo row_t1 row_log row_ready row_t2 row_cols emt_cols
        v_spilled o_spilled0 o_spilled1 m_sel m_mb m_diag m_decay m_tap m_conv m_th m_c m_s m_sp m_num m_vo0 m_vo1 m_tanh m_hn m_ht m_hi m_lo
        pool_tile pooled p_hi p_lo pool_out tg_done gate_done merged_val merged_hi_done merged_lo_done glu_t glu_v act_hi_done act_lo_done
        waits_over fin_t0 fin_t1 fin_sb0 fin_sb1 stored""".split()
    sem = {n: nc.alloc_semaphore(n) for n in sem_names}
    raw_ready = [sem["raw_ready0"], sem["raw_ready1"]]
    START_AT_1 = ("o_norm", "s_exp", "a_t", "o_lo", "m_decay", "m_num", "m_lo", "m_c", "act_lo_done")
    bank_free = [sem["bank_free0"], sem["bank_free1"]]

    def unit(l, name, j):
        return l * UPL + (UBASE[name] + j)

    def tile(l, name, j):
        return l * VPL + (VBASE[name] + j)

    def wait_alone(eng, s, value):
        eng.wait_ge(s, value)
        eng.sem_inc(sem["waits_over"], 1)

    def tile_wait(eng, l, name, j, t):
        if t == 1:
            eng.wait_ge(sem["units_done"], unit(l, name, j) + 3)
        else:
            eng.wait_ge(sem["tile0_done"], tile(l, name, j // 3 if name == "dn" else j) + 1)

    def read_out(l, name, j):
        return l * 40 + 2 * (NATURAL[name] + j)

    def dve_out(l, name, j):
        return l * (2 * (VBASE["ga"] - VBASE["mq"])) + 2 * (VBASE[name] + j - VBASE["mq"])

    def stream_tile(norm, k):
        return norm * KT + k

    with nc.Block() as block:

        @block.sync
        def _(sp):
            for row, rows, src in ((R_GMIX, KT, g_mix.rearrange("l (t p) -> t l p", p=P)),
                                   (R_GFFN, KT, g_ffn.rearrange("l (t p) -> t l p", p=P)),
                                   (R_PSC, KT, pool_scale.rearrange("l (t p) -> t l p", p=P)),
                                   (R_CONV, 64, conv_qk.rearrange("l w (t p) -> (w t) l p", p=P)),
                                   (R_GDH, 1, g_diff_head.rearrange("l (t p) -> t l p", p=P))):
                sp.dma_start(prow[row:row + rows, :, :], src).then_inc(sem["prow_loaded"], 16)
            sp.dma_start(kc[:, :], consts).then_inc(sem["const_loaded"], 16)

            def load_x(half):
                rows = x[0, 2 * half * P:2 * (half + 1) * P, :].rearrange("(b p) d -> p b d", p=P)
                sp.dma_start(xnat[:, 2 * half:2 * half + 2, :], rows).then_inc(sem[f"x_loaded{half}"], 16)

            load_x(0)

            def load(l, name, j, s, src, kn=KT):
                need = sp.snap(unit(l, name, j) + 1)
                sp.wait_ge(sem["split_done"], need)
                sp.dma_start(raw[s][:, 0:kn, :], src).then_inc(raw_ready[s], 16)

            def columns(w, l, col):
                return w[bass.ds(l, 1), :, bass.ds(col, UC)].rearrange("o (k p) n -> p (o k) n", p=P)

            def section(l, name, w, col, n, first=0):
                with sp.Fori(first // 2, n // 2) as i:
                    for s in range(2):
                        load(l, name, 2 * i + s, s, columns(w, l, i * (2 * UC) + (col + s * UC)))

            def layer(l, next_l):
                load(l, "aq", 1, 1, columns(w_in, l, C_AQ + UC))
                section(l, "aq", w_in, C_AQ, 8, first=2)
                section(l, "pu", w_in, C_PU, 4)
                for s in range(2):
                    g = w_pool[bass.ds(l, 1), 2 * s:2 * s + 2].rearrange("o g (k p) n -> p (o g k) n", p=P)
                    load(l, "pool", s, s, g, 4)
                section(l, "av", w_in, C_AQ + 2 * D, 4)
                section(l, "vo", w_in, C_MV, 8)
                section(l, "mq", w_in, C_MQ, 8)
                section(l, "ga", w_in, C_GA, 4)
                section(l, "wd", w_diff_out, 0, 4)
                section(l, "gp", w_in, C_GP, 4)
                section(l, "gm", w_in, C_GM, 4)
                section(l, "wm", w_m_out, 0, 4)
                section(l, "wo", w_out, 0, 4)
                with sp.Fori(0, FF // UC) as i:
                    for s in range(2):
                        load(l, "gu", 2 * i + s, s, columns(w_gate_up, l, i * UC + s * FF))
                with sp.Fori(0, 2) as i:
                    for j in range(6):
                        k0, kn = DOWN_K[j % 3]
                        src = w_down[bass.ds(l, 1), k0 * P:(k0 + kn) * P, bass.ds(i * (2 * UC) + (j // 3) * UC, UC)]
                        load(l, "dn", 6 * i + j, j % 2, src.rearrange("o (k p) n -> p (o k) n", p=P), kn)
                load(l, "dn", 12, 0, columns(w_in, next_l, C_AQ))

            load(0, "aq", 0, 0, columns(w_in, 0, C_AQ))
            load_x(1)
            with sp.Fori(0, DEPTH - 1) as l:
                layer(l, l + 1)
            layer(DEPTH - 1, DEPTH - 1)
            for c in range(2):
                for b in range(NB):
                    sp.wait_ge(sem[f"fin_sb{c}"], b + 1)
                    sp.dma_start(out[0, b * P:(b + 1) * P, c * S:(c + 1) * S], xnat[:, b, c * S:(c + 1) * S]).then_inc(sem["stored"], 16)
            sp.wait_ge(sem["stored"], 16 * 2 * NB)

        @block.gpsimd
        def _(pool):
            def inv_sqrt(dst, src, n):
                return pool.tensor_tensor(dst, src, mp[:, 0:1].to_broadcast([P, n]), ALU.pow)

            pool.memset(mp[:, 0:1], -0.5)
            pool.drain()

            def attention_out(l, h):
                wait_alone(pool, sem["o_ss"], l * AH + h + 1)
                inv_sqrt(st[:, 36:40], st[:, 32:36], 4).then_inc(sem["o_rstd"], 1)

            def square_sums(norm):
                for k in range(KT):
                    wait_alone(pool, sem["sq_done"], stream_tile(norm, k) + 1)
                    if k == 0:
                        ins = pool.tensor_copy(sqsum[:, :], sqt[:, 0, :])
                    else:
                        pool.drain()
                        ins = pool.tensor_tensor(sqsum[:, :], sqsum[:, :], sqt[:, k % 2, :], ALU.add)
                    ins.then_inc(sem["sq_summed"], 1)

            def norm_rstd(norm):
                wait_alone(pool, sem["ms_sb"], norm + 1)
                inv_sqrt(st[:, 44:48], st[:, 40:44], 4).then_inc(sem["rstd_done"], 1)

            for half, squares, summed in ((slice(0, S // 2), "x_half_sq", "x_half_sum"), (slice(S // 2, S), "sq_done", "sq_summed")):
                for k in range(KT):
                    wait_alone(pool, sem[squares], k + 1)
                    if k == 0:
                        ins = pool.tensor_copy(sqsum[:, half], sqt[:, 0, half])
                    else:
                        pool.drain()
                        ins = pool.tensor_tensor(sqsum[:, half], sqsum[:, half], sqt[:, k % 2, half], ALU.add)
                    ins.then_inc(sem[summed], 1)
            with pool.Fori(0, DEPTH) as l:
                one = bass.ds(l, 1)
                with nc.allow_non_contiguous_dma(reason="eight numbers"):
                    pool.dma_start(bif[0:MH, 0:2], b_if[one].rearrange("o (t h) -> h (o t)", t=2)).then_inc(sem["small_loaded"], 16)
                pool.dma_start(gqk[:, :, :], g_qk[one].rearrange("o a d -> o (a d)").to_broadcast([P, 2 * DK]).rearrange("p (a d) -> p a d", a=2)).then_inc(sem["small_loaded"], 16)
                pool.dma_start(lams[:, :, :], lam_p[one].rearrange("o a d -> o (a d)").to_broadcast([P, 4 * DK]).rearrange("p (a d) -> p a d", a=4)).then_inc(sem["small_loaded"], 16)
                with nc.allow_non_contiguous_dma(reason="eight columns of w_in"):
                    pool.dma_start(wif, w_in[one, :, C_IF:C_IF + 2 * MH].rearrange("o (k p) n -> p (o k) n", p=P)).then_inc(sem["if_loaded"], 16)
                norm_rstd(2 * l)
                wait_alone(pool, sem["xt_tile"], stream_tile(2 * l, KT))
                pool.dma_start(xt_dram, xt[:, :, :].rearrange("p k s -> p (k s)")).then_inc(sem["spilled"], 16)
                wait_alone(pool, sem["q_ss"], l + 1)
                inv_sqrt(table["qst"][:, :], table["qst"][:, :], AH * 16)
                wait_alone(pool, sem["aev"], read_out(l, "av", 0))
                pool.drain()
                with pool.Fori(0, AH) as h:
                    q = qkn[:, bass.ds(h, 1)].rearrange("p o a b (c d) -> p (o a b c) d", d=DK)
                    rstd = qst[:, bass.ds(h, 1)].rearrange("p o a b c -> p (o a b c)")
                    pool.tensor_tensor(q, q, rstd.unsqueeze(2).to_broadcast([P, 16, DK]), ALU.mult).then_inc(sem["q_normed"], 1)
                wait_alone(pool, sem["pool_out"], (l + 1) * KT)
                for g in range(4):
                    w = 2 << g
                    y = mg[:, 2 * g:2 * g + 2, :]
                    src = y
                    for n in range(g + 1):
                        dst = (pa, pb)[n % 2]
                        v = 1 << n
                        pool.tensor_copy(dst[:, :, 0:v], src[:, :, 0:v])
                        pool.tensor_tensor(dst[:, :, v:S], src[:, :, v:S], src[:, :, 0:S - v], ALU.add)
                        pool.drain()
                        src = dst
                    pool.tensor_tensor(src[:, :, 0:w], src[:, :, 0:w], kc[:, K_CNT:K_CNT + w].unsqueeze(1).to_broadcast([P, 2, w]), ALU.mult)
                    pool.tensor_scalar(src[:, :, w:S], src[:, :, w:S], 1.0 / w, None, ALU.mult)
                    pool.drain()
                    pool.tensor_tensor(y, src[:, :, :], y, ALU.subtract).then_inc(sem["pooled"], 1)
                    pool.drain()
                attention_out(l, 0)
                for i, (units, done) in enumerate((((0, 4), "v_spilled"), ((4, 6), "o_spilled0"), ((6, 8), "o_spilled1"))):
                    attention_out(l, i + 1)
                    wait_alone(pool, sem["aev"], read_out(l, "vo", units[1]))
                    pool.dma_start(vo_dram[:, units[0]:units[1], :],
                                   vo[:, units[0]:units[1], :, :].rearrange("p u b c -> p u (b c)")).then_inc(sem[done], 16)
                with pool.Fori(4, AH) as i:
                    attention_out(l, i)
                for done in ("v_spilled", "o_spilled0", "o_spilled1"):
                    wait_alone(pool, sem[done], 16 * (l + 1))

                def vo_head(h):
                    for dst, u in ((mvh, h), (moh, h + MH)):
                        pool.dma_start(dst[:, h % 2, :, 0:MDH], vo_dram[:, u, :].rearrange("p (b c) -> p b c", b=NB)).then_inc(sem[f"m_vo{h % 2}"], 16)

                wait_alone(pool, sem["units_done"], unit(l, "wd", 4) + 2)
                vo_head(0)
                vo_head(1)
                wait_alone(pool, sem["m_c"], (l + 1) * 4 * MH + 1)
                pool.dma_start(xt[:, :, :].rearrange("p k s -> p (k s)"), xt_dram).then_inc(sem["xt_back"], 16)
                for h in range(2, MH):
                    wait_alone(pool, sem["m_hn"], l * MH + h - 1)
                    vo_head(h)
                square_sums(2 * l + 1)
                norm_rstd(2 * l + 1)
                square_sums(2 * l + 2)

        @block.scalar
        def _(act):
            def copy(dst, src, scale=1.0):
                return nc.scalar.activation(dst, src, ACT.Identity, scale=scale)

            def split_hi(l, name, j, s, kn=KT):
                u = unit(l, name, j)
                act.wait_ge(sem["units_done"], u + 1)
                act.wait_ge(raw_ready[s], (u - s) * 8 + 16)
                copy(w_hi[s][:, 0:kn, :], raw[s][:, 0:kn, :]).then_inc(sem["hi_ready"], 1)

            def dense(l, name, i, evac, hooks=(None,) * 5, kn=KT, last_kn=KT, wait_tile=True, first=None):
                hooks = dict(enumerate(hooks))
                if first:
                    first()
                split_hi(l, name, 2 * i + 1, 1, kn)
                for s in range(2):
                    for t in range(2):
                        if hooks.get(2 * s + t):
                            hooks[2 * s + t]()
                        if (s, t) == (1, 0):
                            split_hi(l, name, 2 * i + 2, 0, last_kn)
                        if evac:
                            if wait_tile:
                                tile_wait(act, l, name, 2 * i + s, t)
                            evac(s, t)
                if hooks.get(4):
                    hooks[4]()

            def stream_hi(norm, k, kk, gcol):
                n = stream_tile(norm, k)
                wait_alone(act, sem["xt_tile"], n + 1)
                tile_k = xt[:, bass.ds(k, 1), :].rearrange("p o s -> p (o s)")
                nc.scalar.activation(h_hi[:, bass.ds(k, 1), :].rearrange("p o s -> p (o s)"), tile_k, ACT.Identity,
                                     scale=pcol[:, bass.ds(gcol + k, 1)]).then_inc(sem["hhi_done"], 1)
                wait_alone(act, sem["sq_summed"], n + 1)
                nc.scalar.activation(sqt[:, kk % 2, :], tile_k, ACT.Square).then_inc(sem["sq_done"], 1)

            def attn_qk(l, h):
                act.wait_ge(sem["q_t"], l * AH + h + 1)
                for c in range(2):
                    copy(qk_hi[:, c, :], B[4 + c][:, :]).then_inc(sem["q_hi"], 1)

            smax, ssum = st_s[:, 0:8], st_s[:, 8:16]

            def attn_exp(l, h, qbs):
                for qb in qbs:
                    n = (qb + 1) * P
                    act.wait_ge(sem["s_max"], (l * AH + h) * 4 + qb + 1)
                    e = (e0, e1)[qb % 2]
                    if qb >= 2:
                        act.wait_ge(sem["s_comb"], (l * AH + h) * 4 + qb - 1)
                    for c in range(2):
                        o = 2 * qb + c
                        ins = nc.scalar.activation(e[:, c, 0:n], B[2 * (qb % 2) + c][:, 0:n], ACT.Exp,
                                                   bias=smax[:, o:o + 1], scale=DK ** -0.5, accum_out=ssum[:, o:o + 1])
                        ins.then_inc(sem["s_exp"], 1)

            def attn_probs(l, h, qbs):
                for qb in qbs:
                    act.wait_ge(sem["a_t"], (l * AH + h) * 4 + qb + 1 + 1)
                    n = (qb + 1) * P
                    o = pair_off(qb) * P
                    copy(probs_t[:, o:o + n], B[4 + qb % 2][:, 0:n]).then_inc(sem["a_tsb"], 1)

            def attn_osq(l, h):
                act.wait_ge(sem["o_done"], l * AH + h + 1)
                nc.scalar.activation(osq[:, :, :], B[0][:, :].rearrange("p (b d) -> p b d", b=NB),
                                     ACT.Square).then_inc(sem["o_sq"], 1)

            def attn_ohi(l, h):
                act.wait_ge(sem["o_t"], l * AH + h + 1)
                nc.scalar.activation(o_sp[:, bass.ds(h, 1), 0, :].rearrange("p o s -> p (o s)"), B[5][:, :], ACT.Identity,
                                     scale=lamt[:, 4:5]).then_inc(sem["o_hi"], 1)

            def blocks(dst, t):
                for b in range(2):
                    n = 2 * t + b
                    ins = nc.scalar.activation(dst(n), bank[t][:, b * UC:(b + 1) * UC], ACT.Identity, scale=st[:, 44 + n:45 + n])
                ins.then_inc(bank_free[t], 1)
                act.drain().then_inc(sem["aev"], 1)

            def evac_qk(l, i, qk):
                def evac(s, t):
                    n = l * 16 + 8 * qk + 4 * i + 2 * s + t
                    wait_alone(act, sem["q_red"], n + 1)
                    for b in range(2):
                        ins = nc.scalar.activation(qsq[:, t, b * UC:(b + 1) * UC], bank[t][:, b * UC:(b + 1) * UC], ACT.Square,
                                                   scale=st[:, 44 + 2 * t + b:45 + 2 * t + b])
                    ins.then_inc(sem["q_sq"], 1)
                    blocks(lambda b: qkn[:, bass.ds(i * 4 + 2 * s, 2), qk, b, :], t)
                return evac

            def evac_nat(i, dst):
                def evac(s, t):
                    blocks(lambda b: dst[:, b, bass.ds(i * (2 * UC) + s * UC, UC)], t)
                return evac

            def evac_vo(i):
                def evac(s, t):
                    blocks(lambda b: vo[:, bass.ds(2 * i + s, 1), b, :].rearrange("p o c -> p (o c)"), t)
                return evac

            def evac_pu(i):
                def evac(s, t):
                    copy(p_hi[:, bass.ds(i * 4 + (2 * s + t), 1), :].rearrange("p o s -> p (o s)"), bank[t][:, :]).then_inc(sem["p_hi"], 1)
                return evac

            def attention_step(l, name, i, h, evac, tail=True):
                def first():
                    if tail:
                        attn_probs(l, h - 1, (0, 1))

                def before0():
                    if tail:
                        attn_probs(l, h - 1, (2, 3))

                def before1():
                    if tail:
                        attn_osq(l, h - 1)

                def before2():
                    attn_qk(l, h)
                    attn_exp(l, h, (0, 1))

                def before3():
                    if tail:
                        attn_ohi(l, h - 1)
                    attn_exp(l, h, (2, 3))

                dense(l, name, i, evac, (before0, before1, before2, before3, None), first=first)

            half = slice(0, S // 2)
            for k in range(KT):
                if k == 3:
                    split_hi(0, "aq", 0, 0)
                act.wait_ge(sem["x_half"], k // 2 + 1)
                nc.scalar.activation(h_hi[:, k, half], xt[:, k, half], ACT.Identity, scale=pcol[:, R_GMIX + k:R_GMIX + k + 1]).then_inc(sem["x_half_hi"], 1)
            for k in range(KT):
                if k >= 2:
                    act.wait_ge(sem["x_half_sum"], k - 1)
                nc.scalar.activation(sqt[:, k % 2, half], xt[:, k, half], ACT.Square).then_inc(sem["x_half_sq"], 1)
            half = slice(S // 2, S)
            for k in range(KT):
                act.wait_ge(sem["xt_tile"], k + 1)
                nc.scalar.activation(h_hi[:, k, half], xt[:, k, half], ACT.Identity, scale=pcol[:, R_GMIX + k:R_GMIX + k + 1]).then_inc(sem["hhi_done"], 1)
                act.wait_ge(sem["sq_summed"], k + 1)
                nc.scalar.activation(sqt[:, k % 2, half], xt[:, k, half], ACT.Square).then_inc(sem["sq_done"], 1)

            def layer_head(l):
                act.wait_ge(sem["lam_sum"], l + 1)
                nc.scalar.activation(lamt[:, 2:4], lamt[:, 0:2], ACT.Exp).then_inc(sem["lam_exp"], 1)
                act.wait_ge(sem["if_loaded"], 16 * (l + 1))
                copy(wif_hi[:, :, :], wif).then_inc(sem["if_hi"], 1)

            with act.Fori(0, DEPTH) as l:
                dense(l, "aq", 0, evac_qk(l, 0, 0), (lambda: act.wait_ge(sem["rstd_done"], 2 * l + 1), None, None, None, None))
                layer_head(l)
                dense(l, "aq", 1, evac_qk(l, 1, 0))
                with act.Fori(0, 2) as i:
                    dense(l, "ak", i, evac_qk(l, i, 1))
                with act.Fori(0, 2) as i:
                    dense(l, "pu", i, evac_pu(i))
                dense(l, "pool", 0, None, kn=4)
                wait_alone(act, sem["q_red"], (l + 1) * 16 + 2)
                dense(l, "av", 0, evac_nat(0, av))
                attention_step(l, "av", 1, 0, evac_nat(1, av), tail=False)
                wait_alone(act, sem["pool_out"], (l + 1) * KT)
                with act.Fori(0, 2) as i:
                    attention_step(l, "vo", i, i + 1, evac_vo(i))
                wait_alone(act, sem["pooled"], (l + 1) * 4)
                with act.Fori(2, 4) as i:
                    attention_step(l, "vo", i, i + 1, evac_vo(i))
                with act.Fori(0, 2) as i:
                    attention_step(l, "mq", i, i + 5, None)
                attention_step(l, "mk", 0, 7, None)

                def tail0():
                    attn_probs(l, AH - 1, (0, 1, 2, 3))

                def tail1():
                    attn_osq(l, AH - 1)

                def tail3():
                    attn_ohi(l, AH - 1)

                def rows_log():
                    act.wait_ge(sem["row_t1"], l + 1)
                    nc.scalar.activation(row_i[0:MH, :], B[0][0:MH, :], ACT.Identity, bias=bif[0:MH, 0:1])
                    nc.scalar.activation(row_b[0:MH, :], B[1][0:MH, :], ACT.Identity, bias=bif[0:MH, 1:2])
                    nc.scalar.activation(row_t[0:MH, :], B[1][0:MH, :], ACT.Abs, bias=bif[0:MH, 1:2])
                    act.drain()
                    nc.scalar.activation(row_u[0:MH, :], row_t[0:MH, :], ACT.Exp, scale=-1.0)
                    act.drain()
                    nc.scalar.activation(row_t[0:MH, :], row_u[0:MH, :], ACT.Ln, bias=1.0).then_inc(sem["row_log"], 1)

                def rows_emt():
                    act.wait_ge(sem["row_t2"], l + 1)
                    nc.scalar.activation(emt[:, :], B[0][:, 0:4 * MH], ACT.Exp, scale=-1.0).then_inc(sem["emt_cols"], 1)

                dense(l, "mk", 1, None, (tail0, tail1, None, tail3, rows_log))

                def gate_tanh(which, i):
                    def tanh(s, t):
                        n = i * 4 + (2 * s + t)
                        act.wait_ge(sem["gate_out"], (2 * l + which) * KT + n + 1)
                        g = gate[:, bass.ds(n, 1), :].rearrange("p o s -> p (o s)")
                        nc.scalar.activation(g, g, ACT.Tanh, scale=0.5).then_inc(sem["gate_done"], 1)
                    return tanh

                def conv_hooks(h, part=None):
                    base = (l * MH + h) * 4

                    def tap(k):
                        act.wait_ge(sem["m_c"], base + (2 if k == 3 else 1))
                        nc.scalar.activation(cv[:, k % 3, :], mqk[:, bass.ds(h, 1), k, :].rearrange("p o s -> p (o s)"), ACT.Identity,
                                             scale=pcol[:, bass.ds(l * NROWS + h * 2 + (R_CONV + 3 * 16 + (k // 2) * 8 + k % 2), 1)]
                                             ).then_inc(sem["m_tap"], 1)

                    def tanh(k):
                        act.wait_ge(sem["m_conv"], base + k + 1)
                        act.wait_ge(sem["m_c"], base + k + 1)
                        nc.scalar.activation(th[:, :], cv[:, k % 3, :], ACT.Tanh, scale=0.5).then_inc(sem["m_th"], 1)

                    if part is not None:
                        k = 2 * part
                        return [lambda: (tap(k), tap(k + 1)), lambda: tanh(k), lambda: tanh(k + 1)]
                    return [lambda: (tap(0), tap(1), tanh(0)), lambda: (tanh(1), tap(2), tap(3)), None, lambda: (tanh(2), tanh(3))]

                wait_alone(act, sem["dve_out"], dve_out(l, "mk", 4))
                dense(l, "ga", 0, gate_tanh(0, 0), conv_hooks(0) + [None], wait_tile=False)
                dense(l, "ga", 1, gate_tanh(0, 1), (None, None, None, None, rows_emt), wait_tile=False)
                with act.Fori(0, 2) as i:
                    dense(l, "wd", i, None, conv_hooks(i + 1) + [None])

                def m_front_decay(h):
                    hd = l * MH + h + 1
                    act.wait_ge(sem["m_diag"], hd)
                    act.wait_ge(sem["m_num"], l * MH + h + 1)
                    for jc in range(NB):
                        for sc in range(jc + 1):
                            src = mdiag[:, jc, :] if sc == jc else B[3][:, jc * P:(jc + 1) * P]
                            o = row_off(sc) + (jc - sc) * P
                            ins = nc.scalar.activation(decay[:, o:o + P], src, ACT.Exp, scale=-1.0,
                                                       bias=ac[:, h + 4 * (pair_off(jc) + sc):h + 4 * (pair_off(jc) + sc) + 1])
                    ins.then_inc(sem["m_decay"], 1)

                def m_tanh(h):
                    act.wait_ge(sem[f"m_vo{h % 2}"], (l * 2 + h // 2 + 1) * 32)
                    o = moh[:, h % 2, :, :]
                    nc.scalar.activation(o, o, ACT.Tanh, scale=0.5).then_inc(sem["m_tanh"], 1)

                def m_hi(h):
                    act.wait_ge(sem["m_ht"], l * MH + h + 1)
                    for v in range(2):
                        copy(hm_sp[:, h, v, :], B[4 + v][:, :], 0.5).then_inc(sem["m_hi"], 1)

                def tg_tanh(i):
                    def tanh(s, t):
                        act.wait_ge(sem["tg_out"], l * KT + 4 * i + 2 * s + t + 1)
                        nc.scalar.activation(tg[:, t, :], tg[:, t, :], ACT.Tanh, scale=0.5).then_inc(sem["tg_done"], 1)
                    return tanh

                for h, (name, i, evac) in enumerate((("gp", 0, tg_tanh(0)), ("gp", 1, tg_tanh(1)),
                                                     ("gm", 0, gate_tanh(1, 0)), ("gm", 1, gate_tanh(1, 1)))):
                    conv = conv_hooks(MH - 1, h) if h < 2 else [lambda: None] * 3
                    front = lambda h=h: (m_front_decay(h), m_tanh(h))
                    hooks = (lambda: (conv[0](), front(), conv[1]()), conv[2], None, None, lambda: m_hi(h))
                    dense(l, name, i, evac, hooks, wait_tile=False)

                def merge_hi(n):
                    act.wait_ge(sem["merged_val"], l * KT + n + 1)
                    copy(merged_hi[:, bass.ds(n, 1), :].rearrange("p o s -> p (o s)"), mg[:, bass.ds(n, 1), :].rearrange("p o s -> p (o s)"), 0.5).then_inc(sem["merged_hi_done"], 1)

                with act.Fori(0, 2) as i:
                    dense(l, "wm", i, None, (None, lambda: merge_hi(i * 4), lambda: merge_hi(i * 4 + 1), lambda: merge_hi(i * 4 + 2), lambda: merge_hi(i * 4 + 3)))

                def stream_tiles(norm, gcol, i):
                    return lambda s, t: stream_hi(norm, i * 4 + (2 * s + t), t, gcol)

                with act.Fori(0, 2) as i:
                    dense(l, "wo", i, stream_tiles(2 * l + 1, l * NROWS + R_GFFN, i), wait_tile=False)

                def evac_gu(i):
                    def evac(s, t):
                        n = l * (2 * FF // UC) + 2 * i + t
                        if s == 0:
                            act.wait_ge(sem["glu_in"], n + 1)
                            nc.scalar.activation(gate_t[:, t, :], glu[:, t, :], ACT.Tanh, scale=0.5).then_inc(sem["glu_t"], 1)
                        else:
                            act.wait_ge(sem["glu_v"], n + 1)
                            copy(act_hi[:, bass.ds(i * 2 + t, 1), :].rearrange("p o s -> p (o s)"), glu[:, t, :]).then_inc(sem["act_hi_done"], 1)
                    return evac

                with act.Fori(0, FF // UC) as i:
                    dense(l, "gu", i, evac_gu(i), wait_tile=False)
                for i in range(6):
                    def evac_dn(s, t):
                        j = 2 * i + s
                        if j % 3 == 2:
                            stream_hi(2 * l + 2, 2 * (j // 3) + t, t, (l + 1) * NROWS + R_GMIX)
                    dense(l, "dn", i, evac_dn, kn=DOWN_K[(2 * i + 1) % 3][1], last_kn=DOWN_K[(2 * i + 2) % 3][1] if i < 5 else KT, wait_tile=False)

            for b in range(NB):
                act.wait_ge(sem["fin_t0"], b + 1)
                copy(xnat[:, b, 0:S], B[b][:, :]).then_inc(sem["fin_sb0"], 1)

        @block.vector
        def _(dve):
            V = nc.vector

            def flat(a):
                return a.rearrange("p o s -> p (o s)")

            def split_lo(l, name, j, s, kn=KT):
                dve.wait_ge(sem["hi_ready"], unit(l, name, j) + 1)
                ins = V.tensor_tensor(w_lo[s][:, 0:kn, :], raw[s][:, 0:kn, :], w_hi[s][:, 0:kn, :].bitcast(F32), ALU.subtract)
                ins.then_inc(sem["split_done"], 1)

            def dense(l, name, i, evac, hooks=(None,) * 5, kn=KT, last_kn=KT):
                hooks = dict(enumerate(hooks))
                split_lo(l, name, 2 * i + 1, 1, kn)
                for s in range(2):
                    for t in range(2):
                        if hooks.get(2 * s + t):
                            hooks[2 * s + t]()
                        if (s, t) == (1, 0):
                            split_lo(l, name, 2 * i + 2, 0, last_kn)
                        if evac:
                            evac(s, t)
                if hooks.get(4):
                    hooks[4]()

            dve.wait_ge(sem["const_loaded"], 16)
            V.memset(mx2[:, 20:21], 0.0).then_inc(sem["units_done"], 2)
            V.memset(mx2[:, 21:22], 0.0).then_inc(sem["split_done"], 2)
            V.memset(mx2[:, 19:20], 0.0).then_inc(sem["sq_summed"], 2)
            V.memset(mx2[:, 18:19], 0.0).then_inc(sem["q_red"], 2)
            for n, name in enumerate(START_AT_1):
                V.memset(st[:, n:n + 1], 0.0).then_inc(sem[name], 1)
            dve.wait_ge(sem["prow_t"], 1)
            V.tensor_copy(pcol[:, 0:DEPTH * NROWS], B[5][:, 0:DEPTH * NROWS])
            V.tensor_copy(pcol[:, DEPTH * NROWS:DEPTH * NROWS + KT], B[5][:, R_GMIX:R_GMIX + KT])

            def stream_lo(norm, k, gcol):
                dve.wait_ge(sem["hhi_done"], stream_tile(norm, k) + 1)
                V.scalar_tensor_tensor(flat(h_lo[:, bass.ds(k, 1), :]), flat(xt[:, bass.ds(k, 1), :]), pcol[:, bass.ds(gcol + k, 1)],
                                       flat(h_hi[:, bass.ds(k, 1), :]).bitcast(F32), ALU.mult, ALU.subtract).then_inc(sem["hlo_half"], 1)
                dve.drain().then_inc(sem["hlo_done"], 1)

            def x_lo(k, half):
                V.scalar_tensor_tensor(h_lo[:, k, half], xt[:, k, half], pcol[:, R_GMIX + k:R_GMIX + k + 1],
                                       h_hi[:, k, half].bitcast(F32), ALU.mult, ALU.subtract).then_inc(sem["hlo_done" if half.start else "hlo_half"], 1)

            def x_copy(j, half):
                src = (bank + B)[j + (4 if half.start else 0)]
                dve.wait_ge(sem["xt_in_t"], j + (4 if half.start else 0) + 1)
                return V.tensor_copy(xt[:, 2 * j:2 * j + 2, half], src[:, :].rearrange("p (k s) -> p k s", k=2))

            half = slice(0, S // 2)
            for j in range(KT // 2):
                x_copy(j, half).then_inc(sem["x_half"], 1)
            V.memset(mx2[:, 22:23], 0.0).then_inc(bank_free[0], 1)
            V.memset(mx2[:, 23:24], 0.0).then_inc(bank_free[1], 1)
            for k in range(KT):
                if k == 3:
                    split_lo(0, "aq", 0, 0)
                dve.wait_ge(sem["x_half_hi"], k + 1)
                x_lo(k, half)
            half = slice(S // 2, S)
            for j in range(KT // 2):
                x_copy(j, half).then_inc(sem["xt_tile"], 2)
            for k in range(KT):
                dve.wait_ge(sem["hhi_done"], k + 1)
                x_lo(k, half)

            def norm_rstd(norm):
                dve.wait_ge(sem["ms_done"], norm + 1)
                V.tensor_scalar(st[:, 40:44], B[0][:, 0:NB], 1.0 / D, EPS, ALU.mult, ALU.add).then_inc(sem["ms_sb"], 1)
                dve.wait_ge(sem["rstd_done"], norm + 1)
                V.tensor_tensor(diag[:, :, :], ident.unsqueeze(1).to_broadcast([P, NB, P]),
                                st[:, 44:48].unsqueeze(2).to_broadcast([P, NB, P]), ALU.mult).then_inc(sem["diag_done"], 1)
                dve.wait_ge(sem["rb_done"], norm + 1)
                V.tensor_copy(rb[:, :], B[1][:, :])
                dve.drain()

            def sum_squares(l, qk, i):
                def reduce(s, t):
                    dve.wait_ge(sem["q_sq"], l * 16 + 8 * qk + 4 * i + 2 * s + t + 1)
                    for b in range(2):
                        ins = V.tensor_reduce(qst[:, bass.ds(i * 4 + 2 * s, 2), qk, 2 * t + b, :],
                                              qsq[:, t, b * UC:(b + 1) * UC].rearrange("p (h c d) -> p h c d", h=2, c=2), AX.X, ALU.add)
                    ins.then_inc(sem["q_red"], 1)
                return reduce

            smax, ssum, rs, mx = st_s[:, 0:8], st_s[:, 8:16], st_s[:, 16:24], st_s[:, 24:32]

            def attn_rope(l, h):
                dve.drain()
                q = qkn[:, bass.ds(h, 1)].rearrange("p o a b d -> p (o a b d)") if not isinstance(h, int) else qkn[:, h].rearrange("p a b d -> p (a b d)")
                pos = lambda ap: ap.rearrange("p (ab c d) -> p ab c d", c=2, d=DK)
                tab = lambda f, lo, hi: rope[:, f, :, :, lo:hi].rearrange("p a b d -> p (a b) d").unsqueeze(2).to_broadcast([P, 2 * NB, 2, hi - lo])
                flat0, flat1 = e0[:, :, :].rearrange("p a s -> p (a s)"), e1[:, :, :].rearrange("p a s -> p (a s)")
                if isinstance(h, int):
                    dve.wait_ge(sem["q_normed"], (l + 1) * AH)
                    dve.wait_ge(sem["spilled"], 16 * (l + 1))
                h2 = DK // 2
                V.tensor_tensor(pos(flat1), pos(q), tab(0, 0, DK), ALU.mult)
                V.tensor_tensor(pos(flat0)[:, :, :, 0:h2], pos(q)[:, :, :, h2:DK], tab(1, 0, h2), ALU.mult)
                V.tensor_tensor(pos(flat0)[:, :, :, h2:DK], pos(q)[:, :, :, 0:h2], tab(1, h2, DK), ALU.mult)
                dve.drain()
                V.tensor_tensor(flat1, flat1, flat0, ALU.add).then_inc(sem["q_roped"], 1)

            def attn_qk_lo(l, h):
                for c in range(2):
                    dve.wait_ge(sem["q_hi"], (l * AH + h) * 2 + c + 1)
                    V.tensor_tensor(qk_lo[:, c, :], B[4 + c][:, :], qk_hi[:, c, :].bitcast(F32), ALU.subtract).then_inc(sem["q_lo"], 1)

            def attn_max(l, h, qb):
                n = (qb + 1) * P
                dve.wait_ge(sem["s_done"], (l * AH + h) * 4 + qb + 1)
                for c in range(2):
                    d = B[2 * (qb % 2) + c][:, qb * P:n]
                    V.tensor_tensor(d, d, causal, ALU.add)
                dve.drain()
                for c in range(2):
                    V.tensor_reduce(mx[:, 2 * qb + c:2 * qb + c + 1], B[2 * (qb % 2) + c][:, 0:n], AX.X, ALU.max)
                dve.drain()
                V.tensor_scalar(smax[:, 2 * qb:2 * qb + 2], mx[:, 2 * qb:2 * qb + 2], -DK ** -0.5, None, ALU.mult).then_inc(sem["s_max"], 1)

            def attn_combine(l, h, qb):
                n = (qb + 1) * P
                e = (e0, e1)[qb % 2]
                o = pair_off(qb) * P
                dve.wait_ge(sem["s_exp"], (l * AH + h) * 8 + 2 * qb + 2 + 1)
                if qb == 0:
                    dve.wait_ge(sem["a_t"], (l * AH + h) * 4 + 1)
                V.reciprocal(rs[:, 2 * qb:2 * qb + 2], ssum[:, 2 * qb:2 * qb + 2])
                dve.drain()
                V.tensor_scalar(e[:, 1, 0:n], e[:, 1, 0:n], rs[:, 2 * qb + 1:2 * qb + 2], lamt[:, 5:6], ALU.mult, ALU.mult)
                dve.drain()
                V.scalar_tensor_tensor(probs[:, o:o + n], e[:, 0, 0:n], rs[:, 2 * qb:2 * qb + 1], e[:, 1, 0:n],
                                       ALU.mult, ALU.add).then_inc(sem["s_comb"], 1)

            def attn_oss(l, h):
                dve.wait_ge(sem["o_sq"], l * AH + h + 1)
                V.tensor_reduce(mx2[:, 16:20], osq[:, :, :], AX.X, ALU.add)
                dve.drain()
                V.tensor_scalar(st[:, 32:36], mx2[:, 16:20], 1.0 / P, EPS, ALU.mult, ALU.add).then_inc(sem["o_ss"], 1)

            def attn_onorm(l, h):
                dve.wait_ge(sem["o_rstd"], l * AH + h + 1)
                V.tensor_tensor(osq[:, :, :], B[0][:, :].rearrange("p (b d) -> p b d", b=NB),
                                st[:, 36:40].unsqueeze(2).to_broadcast([P, NB, P]), ALU.mult).then_inc(sem["o_norm"], 1)

            def attn_olo(l, h):
                dve.wait_ge(sem["o_hi"], l * AH + h + 1)
                V.scalar_tensor_tensor(flat(o_sp[:, bass.ds(h, 1), 1, :]), B[5][:, :], lamt[:, 4:5],
                                       flat(o_sp[:, bass.ds(h, 1), 0, :]).bitcast(F32), ALU.mult, ALU.subtract).then_inc(sem["o_lo"], 1)

            def scaled_out(l, name, i, dst, done):
                def evac(s, t):
                    tile_wait(dve, l, name, 2 * i + s, t)
                    V.tensor_tensor(dst(s, t), bank[t][:, :], rb[:, :], ALU.mult).then_inc(bank_free[t], 1)
                    dve.drain().then_inc(sem[done], 1)
                return evac

            def out_pu(l, i):
                def evac(s, t):
                    n = i * 4 + (2 * s + t)
                    dve.wait_ge(sem["p_hi"], l * KT + n + 1)
                    V.tensor_tensor(flat(p_lo[:, bass.ds(n, 1), :]), bank[t][:, :], flat(p_hi[:, bass.ds(n, 1), :]).bitcast(F32),
                                    ALU.subtract).then_inc(bank_free[t], 1)
                    dve.drain().then_inc(sem["p_lo"], 1)
                return evac

            def out_pool(l):
                def evac(s, u):
                    g = 2 * s + u
                    for t in range(2):
                        n = 2 * g + t
                        if t == 1 and u == 1:
                            dve.wait_ge(sem["units_done"], unit(l, "pool", s) + 3)
                        elif n == 0:
                            dve.wait_ge(sem["tile0_done"], tile(l, "pool", 0) + 1)
                        else:
                            dve.wait_ge(sem["pool_tile"], l * 5 + (n if n < 3 else n - 1))
                        src = B[n - 2] if n >= 2 else bank[t]
                        ins = V.scalar_tensor_tensor(mg[:, n, :], src[:, :], pcol[:, bass.ds(l * NROWS + (R_PSC + n), 1)], rb[:, :],
                                                     ALU.mult, ALU.mult)
                        if n < 2:
                            ins.then_inc(bank_free[t], 1)
                        dve.drain().then_inc(sem["pool_out"], 1)
                return evac

            def out_mqk(l, name, i, j):
                return scaled_out(l, name, i, lambda s, t: flat(mqk[:, bass.ds(i * 2 + s, 1), j + t, :]), "dve_out")

            def out_gate(l, name, i):
                return scaled_out(l, name, i, lambda s, t: flat(gate[:, bass.ds(i * 4 + (2 * s + t), 1), :]), "gate_out")

            def attention_step(l, name, i, h, evac=None, tail=True):
                def before0():
                    attn_rope(l, h)

                def before1():
                    if tail:
                        attn_oss(l, h - 1)
                        attn_onorm(l, h - 1)

                def before2():
                    attn_qk_lo(l, h)
                    for qb in (0, 1):
                        attn_max(l, h, qb)
                    for qb in (0, 1):
                        attn_combine(l, h, qb)

                def before3():
                    if tail:
                        attn_olo(l, h - 1)
                    for qb in (2, 3):
                        attn_max(l, h, qb)
                    for qb in (2, 3):
                        attn_combine(l, h, qb)

                dense(l, name, i, evac, (before0, before1, before2, before3, None))

            with dve.Fori(0, DEPTH) as l:
                dense(l, "aq", 0, sum_squares(l, 0, 0), (lambda: norm_rstd(2 * l), None, None, None, None))
                V.tensor_scalar(lamt[:, 4:5], pcol[:, bass.ds(l * NROWS + R_GDH, 1)], kc[:, bass.ds(l * 2 + (K_LAM + 1), 1)], None, ALU.mult)
                dve.wait_ge(sem["small_loaded"], 48 * (l + 1))
                V.tensor_tensor(lamp[:, :, :], lams[:, 0:4:2, :], lams[:, 1:4:2, :], ALU.mult)
                dve.drain()
                V.tensor_reduce(lamt[:, 0:2], lamp[:, :, :], AX.X, ALU.add).then_inc(sem["lam_sum"], 1)
                cs = kc[:, K_COS:K_ALL].rearrange("p (b f d) -> p b f d", b=NB, f=2)
                h2 = DK // 2
                for a in range(2):
                    g = lambda lo: gqk[:, a, lo:lo + h2].unsqueeze(1).to_broadcast([P, NB, h2])
                    V.tensor_tensor(rope[:, 0, a, :, 0:h2], cs[:, :, 0, :], g(0), ALU.mult)
                    V.tensor_tensor(rope[:, 0, a, :, h2:DK], cs[:, :, 0, :], g(h2), ALU.mult)
                    V.scalar_tensor_tensor(rope[:, 1, a, :, 0:h2], cs[:, :, 1, :], -1.0, g(h2), ALU.mult, ALU.mult)
                    V.tensor_tensor(rope[:, 1, a, :, h2:DK], cs[:, :, 1, :], g(0), ALU.mult)
                dve.wait_ge(sem["if_hi"], l + 1)
                V.tensor_tensor(wif_lo[:, :, :], wif, wif_hi[:, :, :].bitcast(F32), ALU.subtract).then_inc(sem["if_split"], 1)
                dve.wait_ge(sem["lam_exp"], l + 1)
                V.tensor_tensor(lamt[:, 6:7], lamt[:, 3:4], lamt[:, 2:3], ALU.subtract)
                dve.drain()
                V.tensor_tensor(lamt[:, 5:6], lamt[:, 6:7], kc[:, bass.ds(l * 2 + K_LAM, 1)], ALU.subtract)
                dense(l, "aq", 1, sum_squares(l, 0, 1))
                with dve.Fori(0, 2) as i:
                    dense(l, "ak", i, sum_squares(l, 1, i))
                dve.drain()
                V.tensor_scalar(table["qst"][:, :], table["qst"][:, :], 1.0 / DK, EPS, ALU.mult, ALU.add).then_inc(sem["q_ss"], 1)
                dve.wait_ge(sem["if_done"], l + 1)
                V.tensor_tensor(if_rows[0:2 * MH, :], B[0][0:2 * MH, :], rb[0:2 * MH, :], ALU.mult).then_inc(sem["if_rows_done"], 1)
                with dve.Fori(0, 2) as i:
                    dense(l, "pu", i, out_pu(l, i))
                dense(l, "pool", 0, out_pool(l), kn=4)
                dense(l, "av", 0, None)
                attention_step(l, "av", 1, 0, tail=False)
                with dve.Fori(0, 4) as i:
                    attention_step(l, "vo", i, i + 1)
                for i in range(2):
                    for done in (("v_spilled",), ("o_spilled0", "o_spilled1"))[i]:
                        wait_alone(dve, sem[done], 16 * (l + 1))
                    attention_step(l, "mq", i, i + 5, out_mqk(l, "mq", i, 0))
                attention_step(l, "mk", 0, 7, out_mqk(l, "mk", 0, 2))

                def rows_scan():
                    dve.wait_ge(sem["row_log"], l + 1)
                    r = slice(0, MH)
                    V.tensor_copy(selh[r], kc[r, K_HOT:K_HOT + MH].unsqueeze(2).to_broadcast([MH, MH, P])).then_inc(sem["m_sel"], 1)
                    V.scalar_tensor_tensor(row_u[r, :], row_b[r, :], 0.0, row_t[r, :], ALU.min, ALU.subtract)
                    dve.drain()
                    for c in range(NB):
                        k = slice(c * P, (c + 1) * P)
                        V.tensor_tensor_scan(row_b[r, k], ones[r, :], row_u[r, k], 0.0, ALU.mult, ALU.add)
                    dve.drain()
                    V.tensor_tensor(row_i[r, :], row_i[r, :], row_b[r, :], ALU.subtract)
                    V.memset(row_t[r, 0:P], 0.0)
                    dve.drain()

                def rows_maxima():
                    r = slice(0, MH)
                    for c in range(NB):
                        k = slice(c * P, (c + 1) * P)
                        first = NEG_BIG if c == 0 else mp[r, c:c + 1]
                        V.tensor_tensor_scan(row_m[r, k], row_t[r, 0:P], row_i[r, k], first, ALU.add, ALU.max)
                        V.tensor_copy(row_a[r, (pair_off(c) + c) * P:pair_off(c + 1) * P], row_i[r, k])
                        dve.drain()
                        if c < NB - 1:
                            end = (c + 1) * P - 1
                            V.tensor_tensor(mp[r, c + 1:c + 2], row_m[r, end:end + 1], row_b[r, end:end + 1], ALU.add)
                            V.tensor_scalar(row_a[r, pair_off(c + 1) * P:(pair_off(c + 1) + c + 1) * P],
                                            row_a[r, pair_off(c) * P:pair_off(c + 1) * P], row_b[r, end:end + 1], None, ALU.add)
                            dve.drain()
                    V.tensor_tensor(row_u[r, :], row_b[r, :], row_m[r, :], ALU.add).then_inc(sem["row_ready"], 1)

                def rows_cols():
                    dve.wait_ge(sem["row_t2"], l + 1)
                    V.tensor_copy(ac[:, :], B[1][:, 0:40]).then_inc(sem["row_cols"], 1)

                dense(l, "mk", 1, out_mqk(l, "mk", 1, 2), (None, lambda: (attn_oss(l, AH - 1), attn_onorm(l, AH - 1)), None, None, lambda: attn_olo(l, AH - 1)))

                def conv_hooks(h, part=None):
                    base = (l * MH + h) * 4
                    tile_k = lambda k: flat(mqk[:, bass.ds(h, 1), k, :])

                    def taps(k0):
                        for r in range(1, 4):
                            if r > 1:
                                dve.drain()
                            for k in (k0, k0 + 1):
                                if r == 1:
                                    dve.wait_ge(sem["m_tap"], base + k + 1)
                                w = pcol[:, bass.ds(l * NROWS + h * 2 + (R_CONV + (3 - r) * 16 + (k // 2) * 8 + k % 2), 1)]
                                ins = V.scalar_tensor_tensor(cv[:, k % 3, r:S], tile_k(k)[:, 0:S - r], w, cv[:, k % 3, r:S], ALU.mult, ALU.add)
                                if r == 3:
                                    ins.then_inc(sem["m_conv"], 1)

                    def silu(k):
                        dve.wait_ge(sem["m_th"], base + k + 1)
                        V.scalar_tensor_tensor(tile_k(k), th[:, :], 1.0, cv[:, k % 3, :], ALU.add, ALU.mult).then_inc(sem["m_c"], 1)

                    if part is not None:
                        k = 2 * part
                        return [lambda: taps(k), lambda: silu(k), lambda: silu(k + 1), lambda: None]
                    return [lambda: taps(0), lambda: silu(0), lambda: (silu(1), taps(2)), lambda: (silu(2), silu(3))]

                dense(l, "ga", 0, out_gate(l, "ga", 0), conv_hooks(0) + [None])
                dense(l, "ga", 1, out_gate(l, "ga", 1), (None, rows_scan, rows_maxima, None, rows_cols))

                def evac_wd(i):
                    def evac(s, t):
                        tile_wait(dve, l, "wd", 2 * i + s, t)
                        g = flat(gate[:, bass.ds(i * 4 + (2 * s + t), 1), :])
                        V.scalar_tensor_tensor(g, g, 1.0, bank[t][:, :], ALU.add, ALU.mult).then_inc(bank_free[t], 1)
                    return evac

                wait_alone(dve, sem["gate_done"], (2 * l + 1) * KT)
                with dve.Fori(0, 2) as i:
                    dense(l, "wd", i, evac_wd(i), conv_hooks(i + 1) + [None])

                def evac_gp(i):
                    def evac(s, t):
                        n = 4 * i + 2 * s + t
                        if n >= 1:
                            join(n - 1)
                        tile_wait(dve, l, "gp", 2 * i + s, t)
                        V.tensor_tensor(tg[:, t, :], bank[t][:, :], rb[:, :], ALU.mult).then_inc(bank_free[t], 1)
                        dve.drain().then_inc(sem["tg_out"], 1)
                    return evac

                def join(n):
                    dve.wait_ge(sem["pooled"], l * 4 + n // 2 + 1)
                    dve.wait_ge(sem["tg_done"], l * KT + n + 1)
                    V.scalar_tensor_tensor(mg[:, n, :], tg[:, n % 2, :], 1.0, mg[:, n, :], ALU.add, ALU.mult)
                    dve.drain()
                    V.tensor_tensor(mg[:, n, :], mg[:, n, :], gate[:, n, :], ALU.add)

                def m_mask(h):
                    dve.wait_ge(sem["m_mb"], l * MH + h + 1)
                    V.tensor_tensor(mdiag[:, :, :], B[3][:, :].rearrange("p (b j) -> p b j", b=NB),
                                    big.unsqueeze(1).to_broadcast([P, NB, P]), ALU.add).then_inc(sem["m_diag"], 1)

                def m_weigh(h):
                    hd = l * MH + h + 1
                    dve.wait_ge(sem["m_s"], hd)
                    dve.wait_ge(sem["m_decay"], hd + 1)
                    where = ((0, 0), (1, 0), (2, 0), (1, 3 * P))
                    for sc in range(NB):
                        n = (NB - sc) * P
                        b, o = where[sc]
                        d = decay[:, row_off(sc):row_off(sc) + n]
                        ins = V.scalar_tensor_tensor(d, B[b][:, o:o + n], MDH ** -0.5 / 4, d, ALU.mult, ALU.mult)
                    ins.then_inc(sem["m_sp"], 1)

                def m_norm(h):
                    hd = l * MH + h + 1
                    dve.wait_ge(sem["m_num"], hd + 1)
                    dve.wait_ge(sem["m_tanh"], hd)
                    dve.wait_ge(sem["emt_cols"], l + 1)
                    den, neg, rec = st_s[:, 32:36], st_s[:, 36:40], st_s[:, 40:44]
                    for b in range(NB):
                        V.tensor_copy(den[:, b:b + 1], B[b][:, MDH:MDH + 1])
                        V.scalar_tensor_tensor(hn[:, b, :], moh[:, h % 2, b, :], 1.0, B[b][:, 0:MDH], ALU.add, ALU.mult)
                    dve.drain()
                    V.scalar_tensor_tensor(neg, den, -1.0, den, ALU.mult, ALU.max)
                    dve.drain()
                    floor = emt[:, :].rearrange("p (b h) -> p b h", h=MH)[:, :, h]
                    V.tensor_tensor(den, neg, floor, ALU.max)
                    dve.drain()
                    V.reciprocal(rec, den)
                    dve.drain()
                    for b in range(NB):
                        ins = V.tensor_scalar(hn[:, b, :], hn[:, b, :], rec[:, b:b + 1], None, ALU.mult)
                    ins.then_inc(sem["m_hn"], 1)

                def m_lo(h):
                    hd = l * MH + h + 1
                    dve.wait_ge(sem["m_hi"], 2 * hd)
                    for v in range(2):
                        ins = V.scalar_tensor_tensor(hm_sp[:, h, 2 + v, :], B[4 + v][:, :], 0.5,
                                                     hm_sp[:, h, v, :].bitcast(F32), ALU.mult, ALU.subtract)
                    ins.then_inc(sem["m_lo"], 1)

                wait_alone(dve, sem["units_done"], unit(l, "wd", 4) + 2)
                V.memset(mvh[:, :, :, MDH:MDH + 1], 1.0)
                for h, (name, i, evac) in enumerate((("gp", 0, evac_gp(0)), ("gp", 1, evac_gp(1)),
                                                     ("gm", 0, out_gate(l, "gm", 0)), ("gm", 1, out_gate(l, "gm", 1)))):
                    conv = conv_hooks(MH - 1, h) if h < 2 else [lambda: None] * 4
                    dense(l, name, i, evac, (lambda: (m_mask(h), conv[0]()), lambda: (m_weigh(h), conv[1]()),
                                             lambda: (m_norm(h), conv[2]()), conv[3], lambda: m_lo(h)))
                    if h == 1:
                        join(KT - 1)
                        dve.drain()

                def evac_wm(i):
                    def evac(s, t):
                        tile_wait(dve, l, "wm", 2 * i + s, t)
                        n = i * 4 + (2 * s + t)
                        V.scalar_tensor_tensor(ytmp[:, t, :], flat(gate[:, bass.ds(n, 1), :]), 1.0, bank[t][:, :], ALU.add, ALU.mult).then_inc(bank_free[t], 1)
                        dve.drain()
                        m = flat(mg[:, bass.ds(n, 1), :])
                        V.tensor_tensor(m, m, ytmp[:, t, :], ALU.add).then_inc(sem["merged_val"], 1)
                        dve.wait_ge(sem["merged_hi_done"], l * KT + n + 1)
                        V.scalar_tensor_tensor(flat(merged_lo[:, bass.ds(n, 1), :]), m, 0.5, flat(merged_hi[:, bass.ds(n, 1), :]).bitcast(F32),
                                               ALU.mult, ALU.subtract).then_inc(sem["merged_lo_done"], 1)
                    return evac

                wait_alone(dve, sem["gate_done"], (2 * l + 2) * KT)
                with dve.Fori(0, 2) as i:
                    dense(l, "wm", i, evac_wm(i))

                def evac_wo(i):
                    def evac(s, t):
                        tile_wait(dve, l, "wo", 2 * i + s, t)
                        k = i * 4 + (2 * s + t)
                        xk = flat(xt[:, bass.ds(k, 1), :])
                        V.tensor_tensor(xk, xk, bank[t][:, :], ALU.add).then_inc(bank_free[t], 1)
                        dve.drain().then_inc(sem["xt_tile"], 1)
                        stream_lo(2 * l + 1, k, l * NROWS + R_GFFN)
                    return evac

                wait_alone(dve, sem["xt_back"], 16 * (l + 1))
                with dve.Fori(0, 2) as i:
                    dense(l, "wo", i, evac_wo(i))

                def evac_gu(i):
                    def evac(s, t):
                        n = l * (2 * FF // UC) + 2 * i + t
                        tile_wait(dve, l, "gu", 2 * i + s, t)
                        if s == 0:
                            V.tensor_tensor(glu[:, t, :], bank[t][:, :], rb[:, :], ALU.mult).then_inc(bank_free[t], 1)
                            dve.drain().then_inc(sem["glu_in"], 1)
                        else:
                            V.scalar_tensor_tensor(glu_up[:, t, :], bank[t][:, :], 0.5, rb[:, :], ALU.mult, ALU.mult).then_inc(bank_free[t], 1)
                            dve.wait_ge(sem["glu_t"], n + 1)
                            V.scalar_tensor_tensor(glu[:, t, :], gate_t[:, t, :], 1.0, glu[:, t, :], ALU.add, ALU.mult)
                            dve.drain()
                            V.tensor_tensor(glu[:, t, :], glu[:, t, :], glu_up[:, t, :], ALU.mult)
                            dve.drain().then_inc(sem["glu_v"], 1)
                            dve.wait_ge(sem["act_hi_done"], n + 1)
                            V.tensor_tensor(flat(act_lo[:, bass.ds(i * 2 + t, 1), :]), glu[:, t, :], flat(act_hi[:, bass.ds(i * 2 + t, 1), :]).bitcast(F32),
                                            ALU.subtract).then_inc(sem["act_lo_done"], 1)
                    return evac

                dense(l, "gu", 0, evac_gu(0), (lambda: norm_rstd(2 * l + 1), None, None, None, None))
                with dve.Fori(1, FF // UC) as i:
                    dense(l, "gu", i, evac_gu(i))

                for i in range(6):
                    def evac_dn(s, t):
                        j = 2 * i + s
                        if j % 3 == 2:
                            tile_wait(dve, l, "dn", j, t)
                            n = 2 * (j // 3) + t
                            V.tensor_tensor(xt[:, n, :], xt[:, n, :], bank[t][:, :], ALU.add).then_inc(bank_free[t], 1)
                            dve.drain().then_inc(sem["xt_tile"], 1)
                            stream_lo(2 * l + 2, n, (l + 1) * NROWS + R_GMIX)
                    dense(l, "dn", i, evac_dn, kn=DOWN_K[(2 * i + 1) % 3][1], last_kn=DOWN_K[(2 * i + 2) % 3][1] if i < 5 else KT)

            for b in range(NB):
                dve.wait_ge(sem["fin_t1"], b + 1)
                V.tensor_copy(xnat[:, b, S:2 * S], (B[4:] + bank)[b][:, :]).then_inc(sem["fin_sb1"], 1)

        @block.tensor
        def _(pe):
            mm, tr = nc.tensor.matmul, nc.tensor.transpose

            def dense(l, name, i, natural, a_hi, a_lo, kn=KT, hooks=None, first_k=None):
                hooks = hooks or {}

                def before_k(s, t, half, k):
                    if first_k and s == 0 and (half == 0 if natural else t == 0):
                        first_k(t, k)

                for s in range(2):
                    pe.wait_ge(sem["split_done"], unit(l, name, 2 * i + s) + 3)
                    for t in range(2):
                        pe.wait_ge(bank_free[t], tile(l, name, 2 * i + s) + 1)
                        for half in range(2):
                            if 4 * s + 2 * t + half in hooks:
                                hooks[4 * s + 2 * t + half]()
                            if natural:
                                b = 2 * t + half
                                tok = slice(b * P, (b + 1) * P)
                                dst = bank[t][:, half * UC:(half + 1) * UC]
                                for k in range(kn):
                                    before_k(s, t, half, k)
                                    mm(dst, a_hi[:, k, tok], w_hi[s][:, k, :], start=k == 0, stop=False)
                                    mm(dst, a_hi[:, k, tok], w_lo[s][:, k, :], start=False, stop=False)
                                    ins = mm(dst, a_lo[:, k, tok], w_hi[s][:, k, :], start=False, stop=k == kn - 1)
                            else:
                                col = slice(t * P, (t + 1) * P)
                                for k in range(half * kn // 2, (half + 1) * kn // 2):
                                    before_k(s, t, half, k)
                                    mm(bank[t][:, :], w_hi[s][:, k, col], a_hi(s, k), start=k == 0, stop=False)
                                    mm(bank[t][:, :], w_hi[s][:, k, col], a_lo(s, k), start=False, stop=False)
                                    ins = mm(bank[t][:, :], w_lo[s][:, k, col], a_hi(s, k), start=False, stop=k == kn - 1)
                        ins.then_inc((sem["tile0_done"], sem["units_done"])[t], 1)

            stream_hi, stream_lo = (lambda s, k: h_hi[:, k, :]), (lambda s, k: h_lo[:, k, :])

            def norm_ms(norm):
                pe.wait_ge(sem["sq_summed"], stream_tile(norm, KT) + 2)
                for b in range(NB):
                    ins = mm(B[0][:, b:b + 1], sqsum[:, b * P:(b + 1) * P], ones[:, 0:1], start=True, stop=True)
                ins.then_inc(sem["ms_done"], 1)

            def norm_spread(norm):
                pe.wait_ge(sem["diag_done"], norm + 1)
                mm(B[1][:, :], ones, diag[:, :, :].rearrange("p b j -> p (b j)"), start=True, stop=True).then_inc(sem["rb_done"], 1)

            def first_pair(l, name, natural, a_hi, a_lo, norm):
                dense(l, name, 0, natural, a_hi, a_lo, hooks={2 + natural: lambda: norm_ms(norm), 3 + 2 * natural: lambda: norm_spread(norm)},
                      first_k=lambda t, k: pe.wait_ge(sem["hlo_half" if natural and t == 0 else "hlo_done"], stream_tile(norm, k) + 1))

            def attn_tqk(l, h):
                pe.wait_ge(sem["q_roped"], l * AH + h + 1)
                src = e1[:, :, :].rearrange("p a (b d) -> p a b d", b=NB)
                for a in range(2):
                    for b in range(NB):
                        ins = tr(B[4 + a][:, b * P:(b + 1) * P], src[:, a, b, :], ident)
                ins.then_inc(sem["q_t"], 1)

            def attn_scores(l, h, qb):
                if qb == 0:
                    pe.wait_ge(sem["q_lo"], (l * AH + h + 1) * 2)
                    pe.wait_ge(sem["s_exp"], (l * AH + h) * 8 + 1)
                    pe.wait_ge(sem["o_norm"], l * AH + h + 1)
                elif qb >= 2:
                    pe.wait_ge(sem["s_exp"], (l * AH + h) * 8 + 2 * (qb - 1) + 1)
                n = (qb + 1) * P
                for c in range(2):
                    r = slice(c * DK, (c + 1) * DK)
                    dst, q = B[2 * (qb % 2) + c][:, 0:n], slice(qb * P, n)
                    mm(dst, qk_hi[r, 0, q], qk_hi[r, 1, 0:n], start=True, stop=False)
                    mm(dst, qk_hi[r, 0, q], qk_lo[r, 1, 0:n], start=False, stop=False)
                    ins = mm(dst, qk_lo[r, 0, q], qk_hi[r, 1, 0:n], start=False, stop=True)
                ins.then_inc(sem["s_done"], 1)

            def attn_tprobs(l, h, qbs):
                for qb in qbs:
                    pe.wait_ge(sem["s_comb"], (l * AH + h) * 4 + qb + 1)
                    if qb == 1:
                        pe.wait_ge(sem["o_lo"], l * AH + h + 1)
                    if qb >= 2:
                        pe.wait_ge(sem["a_tsb"], (l * AH + h) * 4 + qb - 1)
                    for kb in range(qb + 1):
                        o = (pair_off(qb) + kb) * P
                        ins = tr(B[4 + qb % 2][:, kb * P:(kb + 1) * P], probs[:, o:o + P], ident)
                    ins.then_inc(sem["a_t"], 1)

            def attn_values(l, h):
                pe.wait_ge(sem["a_tsb"], (l * AH + h) * 4 + 4)
                pe.wait_ge(sem["aev"], read_out(l, "av", 4))
                for qb in range(NB):
                    for kb in range(qb + 1):
                        o = (pair_off(qb) + kb) * P
                        ins = mm(B[0][:, qb * P:(qb + 1) * P], probs_t[:, o:o + P],
                                 av[:, kb, bass.ds(h * P, P)], start=kb == 0, stop=kb == qb)
                ins.then_inc(sem["o_done"], 1)

            def attn_tout(l, h):
                pe.wait_ge(sem["o_norm"], l * AH + h + 1 + 1)
                for b in range(NB):
                    ins = tr(B[5][:, b * P:(b + 1) * P], osq[:, b, :], ident)
                ins.then_inc(sem["o_t"], 1)

            def attn_hooks(l, h, tail=True):
                hooks = {4: lambda: attn_tqk(l, h), 5: lambda: (attn_scores(l, h, 0), attn_scores(l, h, 1)),
                         7: lambda: (attn_scores(l, h, 2), attn_scores(l, h, 3))}
                if tail:
                    hooks[0] = lambda: attn_tprobs(l, h - 1, (0, 1))
                    hooks[2] = lambda: attn_tprobs(l, h - 1, (2, 3))
                    hooks[3] = lambda: attn_values(l, h - 1)
                    hooks[6] = lambda: (attn_tout(l, h - 1))
                return hooks

            pe.wait_ge(sem["const_loaded"], 16)
            pe.wait_ge(sem["prow_loaded"], 80)
            for lay in range(DEPTH):
                ins = tr(B[5][:, lay * NROWS:(lay + 1) * NROWS], prow[0:NROWS, lay, :], ident[0:NROWS, 0:NROWS])
            ins.then_inc(sem["prow_t"], 1)
            for half in range(2):
                pe.wait_ge(sem[f"x_loaded{half}"], 16)
                if half:
                    pe.wait_ge(sem["x_half"], 1)
                for j in range(KT // 2):
                    dst = (bank + B)[4 * half + j]
                    for k in range(2):
                        for b in range(2):
                            ins = tr(dst[:, (2 * k + b) * P:(2 * k + b + 1) * P], xnat[:, 2 * half + b, (2 * j + k) * P:(2 * j + k + 1) * P], ident)
                    ins.then_inc(sem["xt_in_t"], 1)

            with pe.Fori(0, DEPTH) as l:
                first_pair(l, "aq", True, h_hi, h_lo, 2 * l)
                dense(l, "aq", 1, True, h_hi, h_lo)
                with pe.Fori(0, 2) as i:
                    dense(l, "ak", i, True, h_hi, h_lo)
                pe.wait_ge(sem["if_split"], l + 1)
                for k in range(KT):
                    mm(B[0][0:2 * MH, :], wif_hi[:, k, :], h_hi[:, k, :], start=k == 0, stop=False)
                    mm(B[0][0:2 * MH, :], wif_hi[:, k, :], h_lo[:, k, :], start=False, stop=False)
                    ins = mm(B[0][0:2 * MH, :], wif_lo[:, k, :], h_hi[:, k, :], start=False, stop=k == KT - 1)
                ins.then_inc(sem["if_done"], 1)
                with pe.Fori(0, 2) as i:
                    dense(l, "pu", i, False, stream_hi, stream_lo)
                wait_alone(pe, sem["if_rows_done"], l + 1)
                for g in range(4):
                    s, u = g // 2, g % 2
                    if u == 0:
                        pe.wait_ge(sem["split_done"], unit(l, "pool", s) + 3)
                    pe.wait_ge(sem["p_lo"], l * KT + 2 * g + 2)
                    for t in range(2):
                        dst = B[2 * g + t - 2] if g else bank[t]
                        if g == 0:
                            pe.wait_ge(bank_free[t], tile(l, "pool", 0) + 1)
                        col = slice(t * P, (t + 1) * P)
                        for k in range(2):
                            mm(dst[:, :], w_hi[s][:, 2 * u + k, col], p_hi[:, 2 * g + k, :], start=k == 0, stop=False)
                            mm(dst[:, :], w_hi[s][:, 2 * u + k, col], p_lo[:, 2 * g + k, :], start=False, stop=False)
                            ins = mm(dst[:, :], w_lo[s][:, 2 * u + k, col], p_hi[:, 2 * g + k, :], start=False, stop=k == 1)
                        ins.then_inc(sem["units_done" if t and u else "tile0_done" if g == t == 0 else "pool_tile"], 1)
                dense(l, "av", 0, True, h_hi, h_lo)
                wait_alone(pe, sem["pool_out"], (l + 1) * KT)
                dense(l, "av", 1, True, h_hi, h_lo, hooks=attn_hooks(l, 0, tail=False))
                with pe.Fori(0, 4) as i:
                    dense(l, "vo", i, True, h_hi, h_lo, hooks=attn_hooks(l, i + 1))
                with pe.Fori(0, 2) as i:
                    dense(l, "mq", i, False, stream_hi, stream_lo, hooks=attn_hooks(l, i + 5))
                dense(l, "mk", 0, False, stream_hi, stream_lo, hooks=attn_hooks(l, 7))

                def rows_in():
                    wait_alone(pe, sem["if_rows_done"], l + 1)
                    wait_alone(pe, sem["o_norm"], l * AH + AH + 1)
                    for a in range(2):
                        ins = mm(B[a][0:MH, :], ident[0:2 * MH, a * MH:(a + 1) * MH], if_rows[0:2 * MH, :], start=True, stop=True)
                    ins.then_inc(sem["row_t1"], 1)

                def rows_out():
                    wait_alone(pe, sem["row_ready"], l + 1)
                    for b in range(NB):
                        tr(B[0][:, b * MH:(b + 1) * MH], row_u[0:MH, b * P:(b + 1) * P], ident[0:MH, 0:MH])
                    for n in range(10):
                        ins = tr(B[1][:, n * MH:(n + 1) * MH], row_a[0:MH, n * P:(n + 1) * P], ident[0:MH, 0:MH])
                    ins.then_inc(sem["row_t2"], 1)

                last = AH - 1
                dense(l, "mk", 1, False, stream_hi, stream_lo, hooks={
                    0: lambda: attn_tprobs(l, last, (0, 1)), 2: lambda: attn_tprobs(l, last, (2, 3)),
                    3: lambda: attn_values(l, last), 5: lambda: attn_tout(l, last), 6: rows_in})
                dense(l, "ga", 0, False, stream_hi, stream_lo)
                dense(l, "ga", 1, False, stream_hi, stream_lo, hooks={7: rows_out})
                wait_alone(pe, sem["o_lo"], l * AH + AH + 1)
                with pe.Fori(0, 2) as i:
                    dense(l, "wd", i, False, lambda s, k: o_sp[:, k, 0, :], lambda s, k: o_sp[:, k, 1, :])

                def m_spread(h):
                    pe.wait_ge(sem["m_sel"], l + 1)
                    if h == 0:
                        pe.wait_ge(sem["row_cols"], l + 1)
                    pe.wait_ge(sem["m_decay"], l * MH + h + 1)
                    mm(B[3][:, :], selh[0:MH, h, :], row_m[0:MH, :], start=True, stop=True).then_inc(sem["m_mb"], 1)

                def m_scores(h):
                    pe.wait_ge(sem["m_c"], (l * MH + h + 1) * 4 + 1)
                    for sc in range(NB):
                        b, o = ((0, 0), (1, 0), (2, 0), (1, 3 * P))[sc]
                        n = (NB - sc) * P
                        for k in range(2):
                            ins = mm(B[b][:, o:o + n], mqk[:, h, 2 + k, sc * P:(sc + 1) * P], mqk[:, h, k, sc * P:S], start=k == 0, stop=k == 1)
                    ins.then_inc(sem["m_s"], 1)

                def m_values(h):
                    hd = l * MH + h + 1
                    pe.wait_ge(sem["m_sp"], hd)
                    pe.wait_ge(sem[f"m_vo{h % 2}"], (l * 2 + h // 2 + 1) * 32)
                    for jc in range(NB):
                        for sc in range(jc + 1):
                            o = row_off(sc) + (jc - sc) * P
                            w = decay[:, o:o + P]
                            ins = mm(B[jc][:, 0:MDH + 1], w, mvh[:, h % 2, sc, :], start=sc == 0, stop=sc == jc)
                    ins.then_inc(sem["m_num"], 1)

                def m_turn(h):
                    pe.wait_ge(sem["m_hn"], l * MH + h + 1)
                    pe.wait_ge(sem["m_lo"], l * MH + h + 1)
                    for v in range(2):
                        for b in range(NB):
                            ins = tr(B[4 + v][:, b * P:(b + 1) * P], hn[:, b, v * P:(v + 1) * P], ident)
                    ins.then_inc(sem["m_ht"], 1)

                for h, (name, i) in enumerate((("gp", 0), ("gp", 1), ("gm", 0), ("gm", 1))):
                    dense(l, name, i, False, stream_hi, stream_lo, hooks={
                        0: lambda: m_spread(h), 2: lambda: m_scores(h), 5: lambda: m_values(h), 7: lambda: m_turn(h)})
                hm_hi = lambda s, k: hm_sp[:, k // 2, k % 2, :]
                hm_lo = lambda s, k: hm_sp[:, k // 2, 2 + k % 2, :]
                for i in range(2):
                    dense(l, "wm", i, False, hm_hi, hm_lo, first_k=None if i else
                          lambda t, k: pe.wait_ge(sem["m_lo"], l * MH + k // 2 + 1 + 1))
                for i in range(2):
                    dense(l, "wo", i, False, lambda s, k: merged_hi[:, k, :], lambda s, k: merged_lo[:, k, :], first_k=None if i else
                          lambda t, k: pe.wait_ge(sem["merged_lo_done"], l * KT + k + 1))
                first_pair(l, "gu", False, stream_hi, stream_lo, 2 * l + 1)
                with pe.Fori(1, FF // UC) as i:
                    dense(l, "gu", i, False, stream_hi, stream_lo)
                for j in range(12):
                    s = j % 2
                    k0, kn = DOWN_K[j % 3]
                    pe.wait_ge(sem["split_done"], unit(l, "dn", j) + 3)
                    for t in range(2):
                        if j % 3 == 0:
                            pe.wait_ge(bank_free[t], tile(l, "dn", j // 3) + 1)
                        col = slice(t * P, (t + 1) * P)
                        for k in range(kn):
                            if j < 3 and t == 0:
                                pe.wait_ge(sem["act_lo_done"], l * FT + k0 + k + 1 + 1)
                            mm(bank[t][:, :], w_hi[s][:, k, col], act_hi[:, k0 + k, :], start=k0 + k == 0, stop=False)
                            mm(bank[t][:, :], w_hi[s][:, k, col], act_lo[:, k0 + k, :], start=False, stop=False)
                            ins = mm(bank[t][:, :], w_lo[s][:, k, col], act_hi[:, k0 + k, :], start=False, stop=k0 + k == FT - 1)
                        if t == 1:
                            ins.then_inc(sem["units_done"], 1)
                        elif j % 3 == 2:
                            ins.then_inc(sem["tile0_done"], 1)

            for c in range(2):
                pe.wait_ge(sem["xt_tile"], stream_tile(2 * DEPTH, 4 * (c + 1)))
                for b in range(NB):
                    dst = (B + bank)[4 * c + b]
                    for k in range(4):
                        ins = tr(dst[:, k * P:(k + 1) * P], xt[:, 4 * c + k, b * P:(b + 1) * P], ident)
                    ins.then_inc(sem[f"fin_t{c}"], 1)


_INS = ["x", "g_mix", "w_in", "b_if", "conv_qk", "w_m_out", "w_pool", "pool_scale", "g_qk", "lam_p", "g_diff_head",
        "w_diff_out", "w_out", "g_ffn", "w_gate_up", "w_down"]


def shape_constants():
    import math
    import numpy as np

    c = np.zeros((P, K_ALL), np.float32)
    i = np.arange(P)
    c[:, K_ID:K_ID + P] = np.eye(P)
    c[:, K_MASK:K_MASK + P] = np.where(i[None, :] > i[:, None], NEG_BIG, 0.0)
    c[:, K_BIG:K_BIG + P] = np.where(i[:, None] > i[None, :], -NEG_BIG, 0.0)
    c[:, K_ONE:K_ONE + P] = 1.0
    c[:MH, K_HOT:K_HOT + MH] = np.eye(MH)
    c[:, K_CNT:K_CNT + 16] = 1.0 / np.arange(1, 17)
    for layer in range(DEPTH):
        lam_init = 0.8 - 0.6 * math.exp(-0.3 * layer)
        c[:, K_LAM + 2 * layer] = lam_init
        c[:, K_LAM + 2 * layer + 1] = 1.0 - lam_init
    half = DK // 2
    inv = np.power(np.float32(10000.0), -np.arange(half, dtype=np.float32) / np.float32(half), dtype=np.float32)
    ang = np.arange(S, dtype=np.float32)[:, None] * inv[None, :]
    cs = np.stack([np.cos(ang), np.sin(ang)], 1).astype(np.float32)
    c[:, K_COS:] = cs.reshape(NB, P, 2 * half).transpose(1, 0, 2).reshape(P, -1)
    return c


def kernel(**inputs):
    import numpy as np
    import concourse.bacc as bacc
    from concourse.bass_utils import run_bass_kernel_spmd

    nc = bacc.Bacc("TRN2", target_bir_lowering=False, num_devices=1, dynamic_dma_scratch_size=8192)
    arrays = {f"in_{name}": np.ascontiguousarray(inputs[name]) for name in _INS}
    arrays["in_consts"] = shape_constants()
    args = [nc.dram_tensor(n, a.shape, mybir.dt.from_np(a.dtype), kind="ExternalInput").ap() for n, a in arrays.items()]
    out = nc.dram_tensor("out_0", (1, S, D), F32, kind="ExternalOutput").ap()
    build_trunk(nc, *args, out)
    result = run_bass_kernel_spmd(nc, [arrays], core_ids=[0])
    return result.results[0]["out_0"]
```
